# Optimizing a Trainium2 kernel written in Bass

```python
import jax, jax.numpy as jnp
from jax import lax
import numpy as np

D_MODEL = 1024
BATCH = 1
SEQ = 1024
DEPTH = 1

D_MIX = D_MODEL
D_POOL = D_MIX // 2
D_CONV = D_MIX - D_POOL
POOL_WINDOWS = (2, 4, 8, 16)
N_POOL_GROUPS = len(POOL_WINDOWS)
POOL_GROUP = D_POOL // N_POOL_GROUPS
CONV_WIDTH = 31
N_CONV_HEADS = 4
CONV_HEAD = D_CONV // N_CONV_HEADS
D_IN = D_POOL + 2 * D_CONV
N_GROUPS = 4
EXPERTS_PER_GROUP = 8
N_EXPERTS = N_GROUPS * EXPERTS_PER_GROUP
TOP_K_FINE = 2
D_EXPERT = D_MODEL // 2
MOE_BLOCK = 128
D_PLE = 256
LN_EPS = 1e-5
DN_ALPHA = (2 * DEPTH) ** 0.25
DN_BETA = (8 * DEPTH) ** -0.25

kernel_name = "hybrid_pool_conv_hmoe_deepnorm"

def layer_norm(x, g, b):
    xf = x.astype(jnp.float32)
    mu = xf.mean(-1, keepdims=True)
    var = jnp.square(xf - mu).mean(-1, keepdims=True)
    return ((xf - mu) * lax.rsqrt(var + LN_EPS) * g + b).astype(x.dtype)

def causal_multiscale_pool(u):
    B, S, _ = u.shape
    ug = u.astype(jnp.float32).reshape(B, S, N_POOL_GROUPS, POOL_GROUP)
    csp = jnp.pad(jnp.cumsum(ug, axis=1), ((0, 0), (1, 0), (0, 0), (0, 0)))
    t = jnp.arange(S)
    outs = []
    for gi, w in enumerate(POOL_WINDOWS):
        start = jnp.maximum(t + 1 - w, 0)
        window_sum = csp[:, 1:, gi] - csp[:, start, gi]
        count = jnp.minimum(t + 1, w).astype(jnp.float32)
        outs.append(window_sum / count[None, :, None] - ug[:, :, gi])
    return jnp.stack(outs, axis=2)

def conformer_conv(a, b, w_dw, b_dw, g, beta):
    u = a * jax.nn.sigmoid(b)
    B, S, C = u.shape
    y = lax.conv_general_dilated(
        u, w_dw.astype(u.dtype)[:, None, :], window_strides=(1,),
        padding=[(CONV_WIDTH - 1, 0)], dimension_numbers=("NWC", "WIO", "NWC"),
        feature_group_count=C) + b_dw
    yh = layer_norm(y.reshape(B, S, N_CONV_HEADS, CONV_HEAD),
                    g.reshape(N_CONV_HEADS, CONV_HEAD), beta.reshape(N_CONV_HEADS, CONV_HEAD))
    return jax.nn.silu(yh.reshape(B, S, C))

def grouped_expert_ffn(hf, expert, weights, w_gate, w_up, w_down):
    T, D = hf.shape
    A = expert.size
    e_flat = expert.reshape(A)
    tok = jnp.repeat(jnp.arange(T, dtype=jnp.int32), TOP_K_FINE)
    w_flat = weights.reshape(A)
    order = jnp.argsort(e_flat)
    e_s, tok_s, w_s = e_flat[order], tok[order], w_flat[order]
    counts = jnp.bincount(e_flat, length=N_EXPERTS)
    padded = (counts + MOE_BLOCK - 1) // MOE_BLOCK * MOE_BLOCK
    start = jnp.cumsum(counts) - counts
    pend = jnp.cumsum(padded)
    pstart = pend - padded
    dest = pstart[e_s] + jnp.arange(A) - start[e_s]
    n_blocks = -(-A // MOE_BLOCK) + N_EXPERTS
    P = n_blocks * MOE_BLOCK
    buf_tok = jnp.full((P,), T, jnp.int32).at[dest].set(tok_s)
    buf_w = jnp.zeros((P,), jnp.float32).at[dest].set(w_s)
    block_expert = jnp.minimum(
        jnp.searchsorted(pend, jnp.arange(n_blocks) * MOE_BLOCK, side="right"), N_EXPERTS - 1)
    h_pad = jnp.concatenate([hf, jnp.zeros((1, D), hf.dtype)], axis=0)
    xb = h_pad[buf_tok].reshape(n_blocks, MOE_BLOCK, D)

    def block_ffn(args):
        xblk, e = args
        return (jax.nn.silu(xblk @ w_gate[e]) * (xblk @ w_up[e])) @ w_down[e]

    yb = lax.map(block_ffn, (xb, block_expert)).reshape(P, D)
    y = jax.ops.segment_sum(yb * buf_w[:, None].astype(yb.dtype), buf_tok, num_segments=T + 1)
    return y[:T]

def hierarchical_moe(h, w_coarse, b_coarse, w_fine, b_fine, w_gate, w_up, w_down):
    B, S, D = h.shape
    T = B * S
    hf = h.reshape(T, D)
    coarse = jax.nn.softmax((hf @ w_coarse).astype(jnp.float32) + b_coarse, axis=-1)
    p_group, g_idx = lax.top_k(coarse, 1)
    fine_logits = ((hf @ w_fine).astype(jnp.float32) + b_fine).reshape(T, N_GROUPS, EXPERTS_PER_GROUP)
    sel = jnp.take_along_axis(fine_logits, g_idx[:, :, None], axis=1)[:, 0]
    p_fine, e_local = lax.top_k(jax.nn.softmax(sel, axis=-1), TOP_K_FINE)
    p_fine = p_fine / p_fine.sum(-1, keepdims=True)
    weights = p_group * p_fine
    expert = g_idx * EXPERTS_PER_GROUP + e_local
    y = grouped_expert_ffn(hf, expert, weights, w_gate, w_up, w_down)
    return y.reshape(B, S, D)

def setup_inputs(seed: int = 0) -> dict:
    key = jax.random.key(seed)
    k = jax.random.split(key, 26)
    f32 = jnp.float32
    nrm = lambda kk, shape, s: jax.random.normal(kk, shape, f32) * s
    L = DEPTH
    return {
        "x": nrm(k[0], (BATCH, SEQ, D_MODEL), 1.0),
        "p": nrm(k[1], (DEPTH, BATCH, SEQ, D_PLE), 1.0),
        "w_in": nrm(k[2], (L, D_MODEL, D_IN), D_MODEL ** -0.5),
        "w_pool_mix": nrm(k[3], (L, N_POOL_GROUPS, POOL_GROUP, POOL_GROUP), POOL_GROUP ** -0.5),
        "pool_scale": 1.0 + nrm(k[4], (L, D_POOL), 0.1),
        "w_dw": nrm(k[5], (L, CONV_WIDTH, D_CONV), CONV_WIDTH ** -0.5),
        "b_dw": nrm(k[6], (L, D_CONV), 0.01),
        "conv_ln_g": 1.0 + nrm(k[7], (L, D_CONV), 0.05),
        "conv_ln_b": nrm(k[8], (L, D_CONV), 0.01),
        "w_out": nrm(k[9], (L, D_MIX, D_MODEL), D_MIX ** -0.5 * DN_BETA),
        "ln1_g": 1.0 + nrm(k[10], (L, D_MODEL), 0.05),
        "ln1_b": nrm(k[11], (L, D_MODEL), 0.01),
        "w_coarse": nrm(k[12], (L, D_MODEL, N_GROUPS), D_MODEL ** -0.5),
        "b_coarse": nrm(k[13], (L, N_GROUPS), 0.01),
        "w_fine": nrm(k[14], (L, D_MODEL, N_EXPERTS), D_MODEL ** -0.5),
        "b_fine": nrm(k[15], (L, N_EXPERTS), 0.01),
        "w_gate": nrm(k[16], (L, N_EXPERTS, D_MODEL, D_EXPERT), D_MODEL ** -0.5),
        "w_up": nrm(k[17], (L, N_EXPERTS, D_MODEL, D_EXPERT), D_MODEL ** -0.5),
        "w_down": nrm(k[18], (L, N_EXPERTS, D_EXPERT, D_MODEL), D_EXPERT ** -0.5 * DN_BETA),
        "ln2_g": 1.0 + nrm(k[19], (L, D_MODEL), 0.05),
        "ln2_b": nrm(k[20], (L, D_MODEL), 0.01),
        "w_ple_proj": nrm(k[21], (L, D_PLE, D_MODEL), D_PLE ** -0.5 * DN_BETA),
        "w_ple_gate": nrm(k[22], (L, D_MODEL, D_MODEL), D_MODEL ** -0.5),
        "ln3_g": 1.0 + nrm(k[23], (L, D_MODEL), 0.05),
        "ln3_b": nrm(k[24], (L, D_MODEL), 0.01),
    }

def reference(x, p, w_in, w_pool_mix, pool_scale, w_dw, b_dw, conv_ln_g, conv_ln_b, w_out,
              ln1_g, ln1_b, w_coarse, b_coarse, w_fine, b_fine, w_gate, w_up, w_down,
              ln2_g, ln2_b, w_ple_proj, w_ple_gate, ln3_g, ln3_b):
    B, S, _ = x.shape
    for i in range(DEPTH):
        z = x @ w_in[i]
        u_pool = z[..., :D_POOL]
        u_a = z[..., D_POOL:D_POOL + D_CONV]
        u_b = z[..., D_POOL + D_CONV:]
        pooled = causal_multiscale_pool(u_pool)
        pool_out = (jnp.einsum("bsgc,gcd->bsgd", pooled, w_pool_mix[i]).reshape(B, S, D_POOL)
                    * pool_scale[i]).astype(x.dtype)
        conv_out = conformer_conv(u_a, u_b, w_dw[i], b_dw[i], conv_ln_g[i], conv_ln_b[i])
        mix = jnp.concatenate([pool_out, conv_out], axis=-1) @ w_out[i]
        h = layer_norm(DN_ALPHA * x + mix, ln1_g[i], ln1_b[i])
        moe = hierarchical_moe(h, w_coarse[i], b_coarse[i], w_fine[i], b_fine[i],
                               w_gate[i], w_up[i], w_down[i])
        y = layer_norm(DN_ALPHA * h + moe, ln2_g[i], ln2_b[i])
        ple = (p[i] @ w_ple_proj[i]) * jax.nn.sigmoid(y @ w_ple_gate[i])
        x = layer_norm(DN_ALPHA * y + ple, ln3_g[i], ln3_b[i])
    return x


_drawn_inputs = setup_inputs


def setup_inputs(seed=0):
    import zlib

    import numpy as np

    out = dict(_drawn_inputs(seed))
    spreads = {}
    factors = {'b_dw': 8.0,
     'conv_ln_g': 3.51,
     'conv_ln_b': 23.682,
     'ln1_b': 4.179,
     'b_coarse': 25.034,
     'b_fine': 25.139,
     'ln2_b': 6.087,
     'ln3_b': 5.698}
    for name, (base, spread) in spreads.items():
        noise = np.random.default_rng([zlib.crc32(name.encode()), seed]).standard_normal(out[name].shape)
        drawn = base * np.exp(spread * noise) if base else spread * noise
        out[name] = __import__('jax').numpy.asarray(drawn.astype(out[name].dtype))
    for name, factor in factors.items():
        out[name] = (out[name] * factor).astype(out[name].dtype)
    return out
```

```python
import concourse.bass as bass
from concourse import mybir
from contextlib import ExitStack

P = 128


def build_block(nc, x, p, w_in, w_pool_mix, pool_scale, w_dw, b_dw, conv_ln_g, conv_ln_b, w_out,
                ln1_g, ln1_b, w_coarse, b_coarse, w_fine, b_fine, w_gate, w_up, w_down,
                ln2_g, ln2_b, w_ple_proj, w_ple_gate, ln3_g, ln3_b, out, *debug):
    f32, f32r, i32 = mybir.dt.float32, mybir.dt.float32r, mybir.dt.int32
    ALU, ACT, AX = mybir.AluOpType, mybir.ActivationFunctionType, mybir.AxisListType
    ADD, SUB, MUL = ALU.add, ALU.subtract, ALU.mult

    _, S, D = x.shape
    TT = S // P
    KC = D // P
    HALF = S // 2
    DEPTH = p.shape[0]
    DP = p.shape[3]
    KP = DP // P
    NPG = w_pool_mix.shape[1]
    DPOOL = NPG * P
    DCONV = w_dw.shape[2]
    HEADS = DCONV // P
    TAPS = w_dw.shape[1]
    WINDOWS = [2 << g for g in range(NPG)]
    NG = w_coarse.shape[2]
    NE = w_fine.shape[2]
    EG = NE // NG
    NR = NG + NE
    FE = w_gate.shape[3]
    KF = FE // P
    BT = 64
    MAXB = 64
    SLOTS = 3
    ALPHA = float((2 * DEPTH) ** 0.25)
    EPS = 1e-5
    BIG = 8192.0
    NPRM = TAPS + 4
    PAD = TAPS - 1
    WPAD = 16

    ctx = ExitStack()
    with ctx:
        RING = 16512
        GU = KC * 2 * FE * 4
        WD = KF * D * 4
        SLOT = GU + WD
        FIX = RING + SLOTS * SLOT

        def at(name, shape, dt, offset):
            return nc.alloc_sbuf_tensor_at(name, shape, dt, offset=offset)

        gu_w = [at(f"gu_w{s}", [P, KC, 2, FE], f32, RING + s * SLOT) for s in range(SLOTS)]
        wd_w = [at(f"wd_w{s}", [P, KF, D], f32, RING + s * SLOT + GU) for s in range(SLOTS)]

        top = [FIX]

        def fix(name, shape, dt=f32):
            size = 4
            for n in shape[1:]:
                size *= n
            a = at(name, shape, dt, top[0])
            top[0] += (size + 31) // 32 * 32
            return a

        xh = fix("xh", [P, TT, D])
        ident = fix("ident", [P, P])
        meanw = fix("meanw", [P, P])
        ones = fix("ones", [P, P])
        before = fix("before", [P, P])
        prm = fix("prm", [P, HEADS, NPRM])
        wr = fix("wr", [P, KC, NR])
        rbias = fix("rbias", [P, NR])
        io64 = fix("io64", [P, MAXB])
        iolo = fix("iolo", [P, P])
        tokA = fix("tokA", [P, 2, TT])
        tokB = fix("tokB", [P, 2, TT])
        halfv = fix("halfv", [P, 1])
        thr = fix("thr", [P, S // BT])
        rev4 = fix("rev4", [P, NG])
        rev8 = fix("rev8", [P, EG])
        rcnt = fix("rcnt", [P, WPAD])
        epsv = fix("epsv", [P, 1])
        onev = fix("onev", [P, NE])
        lg = fix("lg", [P, TT, NR])
        wts = fix("wts", [P, 2, TT])
        gtab = fix("gtab", [P, MAXB], i32)
        stab = fix("stab", [P, MAXB], i32)
        bnd = fix("bnd", [P, NE + 1], i32)
        gidx = fix("gidx", [P, 1], i32)
        sidx = fix("sidx", [P, 1], i32)
        SCR = top[0]
        SCR_END = 229368

        xTh = at("xTh", [P, KC, S], f32r, RING)
        xTl = at("xTl", [P, KC, S], f32r, RING + SLOT)
        mixT = at("mixT", [P, KC, S], f32, RING + 2 * SLOT)
        P0, P1, P2 = (RING + s * SLOT + GU for s in range(SLOTS))
        wch = [at(f"wch{j}", [P, KC, P], f32r, P0 + j * 4096) for j in range(3)]
        wcl = [at(f"wcl{j}", [P, KC, P], f32r, (P0 + 3 * 4096, P1, P1 + 4096)[j]) for j in range(3)]
        win2 = at("win2", [P, S], f32, P1 + 8192)
        win3 = at("win3", [P, S], f32, P1 + 12288)
        wcs = [at(f"wcs{j}", [P, KC, P], f32, P2 + j * 4096) for j in range(3)]
        wmix = at("wmix", [P, NPG, P], f32, P2 + 12288)
        rows = at("rows", [NPRM, DCONV], f32, P2 + 12288 + 2048)
        scr = [SCR]

        def scratch(name, shape, dt=f32):
            size = 4
            for n in shape[1:]:
                size *= n
            a = at(name, shape, dt, scr[0])
            scr[0] += (size + 31) // 32 * 32
            if scr[0] > SCR_END:
                raise ValueError(name)
            return a

        uT = scratch("uT", [P, PAD + S])
        acc0 = scratch("acc0", [P, S])
        acc1 = scratch("acc1", [P, S])
        sig1 = scratch("sig1", [P, S])
        sqr = scratch("sqr", [P, S])
        upT = scratch("upT", [P, WPAD + S])
        cur = scratch("cur", [P, NPRM])

        woh = at("woh", [P, KC, D], f32r, RING)
        wol = at("wol", [P, KC, D], f32r, RING + SLOT)
        mh = [at(f"mh{b}", [P, KC, P], f32r, P0 + b * 4096) for b in range(2)]
        ml = [at(f"ml{b}", [P, KC, P], f32r, P0 + 8192 + b * 4096) for b in range(2)]
        wos = [at(f"wos{b}", [P, D], f32, P1 + b * 4096) for b in range(2)]
        hb = [at(f"hb{b}", [P, D], f32, P1 + 8192 + b * 4096) for b in range(2)]
        scr[0] = SCR
        g1 = scratch("g1", [P, D])
        b1 = scratch("b1", [P, D])
        hTt = [scratch(f"hTt{b}", [P, KC, P]) for b in range(2)]
        vt1 = scratch("vt1", [P, D])
        turn1 = scratch("turn1", [P, 1])
        st1 = scratch("st1", [P, 2, 6])
        mv1 = scratch("mv1", [P, 2])
        sd1 = scratch("sd1", [P, 2])

        scr[0] = SCR
        hblk = scratch("hblk", [P, D // 2])
        hTb = scratch("hTb", [P, KC // 2, 2, BT])
        sg = scratch("sg", [P, FE // 2])
        gact = scratch("gact", [P, FE // 2])
        aT = scratch("aT", [P, KF // 2, 2, BT])
        yb = scratch("yb", [P, D // 2])
        RSCR = scr[0]
        onehot = scratch("onehot", [P, 2, TT, NG, EG])
        gsel = scratch("gsel", [P, TT, NG, EG])
        base = scratch("base", [P, TT, NE])
        ohhi = scratch("ohhi", [P, 2 * TT, MAXB])
        ohlo = at("ohlo", [P, 2 * TT, P], f32, P2)
        ohab = at("ohab", [P, 2 * TT, 2, MAXB], f32, P2 + 8192)
        small = [RSCR + 2048 + 1024 + 1024 + 4096]

        def tiny(name, shape, dt=f32):
            size = 4
            for n in shape[1:]:
                size *= n
            a = at(name, shape, dt, small[0])
            small[0] += (size + 31) // 32 * 32
            return a

        cm = tiny("cm", [P, TT])
        cd = tiny("cd", [P, TT, NG])
        ce = tiny("ce", [P, TT, NG])
        cs = tiny("cs", [P, TT])
        ohg = tiny("ohg", [P, TT, NG])
        sel = tiny("sel", [P, TT, EG])
        sel2 = tiny("sel2", [P, TT, EG])
        oh12 = tiny("oh12", [P, 2, TT, EG])
        m2 = tiny("m2", [P, TT])
        ex = tiny("ex", [P, TT])
        tpre = tiny("tpre", [P, TT + 1, NE])
        nbf = tiny("nbf", [P, NE])
        incl = tiny("incl", [P, NE])
        cmp16 = tiny("cmp16", [P, NE, S // BT])
        posf = tiny("posf", [P, 2 * TT])
        posi = tiny("posi", [P, 2 * TT], i32)
        hif = tiny("hif", [P, 2 * TT])

        wgh = at("wgh", [P, KC, D], f32r, RING)
        wgl = at("wgl", [P, KC, D], f32r, RING + 32768)
        wph = at("wph", [P, KP, D], f32r, RING + 65536)
        wpl = at("wpl", [P, KP, D], f32r, RING + 73728)
        wgs = [at(f"wgs{b}", [P, D], f32, RING + 81920 + b * 4096) for b in range(2)]
        yp = [at(f"yp{b}", [P, 2, D], f32, RING + 90112 + b * 8192) for b in range(2)]
        yt = [at(f"yt{b}", [P, D], f32, RING + 106496 + b * 4096) for b in range(2)]
        yTh = [at(f"yTh{b}", [P, KC, P], f32r, RING + 114688 + b * 4096) for b in range(2)]
        yTl = [at(f"yTl{b}", [P, KC, P], f32r, RING + 122880 + b * 4096) for b in range(2)]
        sg3 = at("sg3", [P, D], f32, RING + 131072)
        z3 = at("z3", [P, D], f32, RING + 135168)
        ob = [at(f"ob{b}", [P, D], f32, RING + 139264 + b * 4096) for b in range(2)]
        scr[0] = SCR
        g2 = scratch("g2", [P, D])
        b2 = scratch("b2", [P, D])
        g3 = scratch("g3", [P, D])
        b3 = scratch("b3", [P, D])
        pt = [scratch(f"pt{b}", [P, DP]) for b in range(2)]
        pTh = [scratch(f"pTh{b}", [P, KP, P], f32r) for b in range(2)]
        pTl = [scratch(f"pTl{b}", [P, KP, P], f32r) for b in range(2)]
        turn3 = scratch("turn3", [P, 1])
        st3 = scratch("st3", [P, 2, 6])
        mv3 = scratch("mv3", [P, 2])
        sd3 = scratch("sd3", [P, 2])

        ps = ctx.enter_context(nc.psum_tensor("ps", [P, 8, 512], f32))

        def bank(b, n=1):
            return ps[:, b, :] if n == 1 else ps[:, b:b + n, :].rearrange("q b n -> q (b n)")

        h_dram = nc.dram_tensor("h_dram", [2 * S, D // 2], f32, kind="Internal").ap()
        y_dram = nc.dram_tensor("y_dram", [4 * S, D // 2], f32, kind="Internal").ap()

        def sem(name):
            return ctx.enter_context(nc.semaphore(name))

        x_in = [sem(f"x_in{t}") for t in range(TT)]
        rows_in = sem("rows_in")
        small_in = sem("small_in")
        wc_in = [sem(f"wc_in{j}") for j in range(3)]
        wch_ready = [sem(f"wch_ready{j}") for j in range(3)]
        wcl_ready = [sem(f"wcl_ready{j}") for j in range(3)]
        z_done = [sem(f"z_done{j}") for j in range(3)]
        consts = sem("consts")
        ident_ready = sem("ident_ready")
        pool_own = sem("pool_own")
        dve_own = sem("dve_own")
        act_own = sem("act_own")
        xt_done = sem("xt_done")
        xh_ready = sem("xh_ready")
        xl_ready = sem("xl_ready")
        rcnt_ready = sem("rcnt_ready")
        prm_done = sem("prm_done")
        prm_ready = sem("prm_ready")
        sig_ready = sem("sig_ready")
        u_ready = sem("u_ready")
        up_ready = sem("up_ready")
        pooled_ready = sem("pooled_ready")
        mix_done = sem("mix_done")
        mix_ready = sem("mix_ready")
        conv_step = sem("conv_step")
        conv_ready = sem("conv_ready")
        mean_done = sem("mean_done")
        dev_ready = sem("dev_ready")
        sq_ready = sem("sq_ready")
        var_done = sem("var_done")
        csd_ready = sem("csd_ready")
        yn_ready = sem("yn_ready")
        conv_out = sem("conv_out")
        wos_in = [sem(f"wos_in{b}") for b in range(2)]
        woh_ready = sem("woh_ready")
        wol_ready = sem("wol_ready")
        ln1_in = sem("ln1_in")
        mh_ready = sem("mh_ready")
        ml_ready = sem("ml_ready")
        op_done = sem("op_done")
        v1_ready = sem("v1_ready")
        var1_ready = sem("var1_ready")
        sd1_ready = sem("sd1_ready")
        h_ready = sem("h_ready")
        h_stored = [sem(f"h_stored{b}") for b in range(2)]
        h_kept = sem("h_kept")
        ht_done = sem("ht_done")
        ht_ready = sem("ht_ready")
        rt_done = sem("rt_done")
        lg_ready = sem("lg_ready")
        conv_rec = sem("conv_rec")
        ln1_own = sem("ln1_own")
        ln2_own = sem("ln2_own")
        ln3_own = sem("ln3_own")
        y2_own = sem("y2_own")
        cd_ready = sem("cd_ready")
        ce_ready = sem("ce_ready")
        m2_ready = sem("m2_ready")
        ex_ready = sem("ex_ready")
        oneh_ready = sem("oneh_ready")
        rank_done = sem("rank_done")
        oh_ready = sem("oh_ready")
        tab_done = sem("tab_done")
        tab_ready = sem("tab_ready")
        gu_in = [sem(f"gu_in{s}") for s in range(SLOTS)]
        wd_in = [sem(f"wd_in{s}") for s in range(SLOTS)]
        gath = sem("gath")
        gidx_ready = sem("gidx_ready")
        sidx_ready = sem("sidx_ready")
        hbt_done = sem("hbt_done")
        hbt_ready = sem("hbt_ready")
        gu_done = sem("gu_done")
        silu_ready = sem("silu_ready")
        gact_ready = sem("gact_ready")
        at_done = sem("at_done")
        at_ready = sem("at_ready")
        down_done = sem("down_done")
        y_ready = sem("y_ready")
        scat = sem("scat")
        wgs_in = [sem(f"wgs_in{b}") for b in range(2)]
        wgh_ready = sem("wgh_ready")
        wgl_ready = sem("wgl_ready")
        ln23_in = sem("ln23_in")
        yp_in = [sem(f"yp_in{b}") for b in range(2)]
        pt_in = [sem(f"pt_in{b}") for b in range(2)]
        v2_ready = sem("v2_ready")
        var2_ready = sem("var2_ready")
        sd2_ready = sem("sd2_ready")
        y2_ready = sem("y2_ready")
        yt_done = sem("yt_done")
        yth_ready = sem("yth_ready")
        ytl_ready = sem("ytl_ready")
        ple_done = sem("ple_done")
        sig3_ready = sem("sig3_ready")
        z3_ready = sem("z3_ready")
        var3_ready = sem("var3_ready")
        sd3_ready = sem("sd3_ready")
        o_ready = sem("o_ready")
        o_stored = [sem(f"o_stored{b}") for b in range(2)]

        block = ctx.enter_context(nc.Block())

        def passes(dst, ah, al, bh, bl, first, last):
            nc.tensor.matmul(dst, ah, bh, start=first, stop=False)
            nc.tensor.matmul(dst, ah, bl, start=False, stop=False)
            return nc.tensor.matmul(dst, al, bh, start=False, stop=last)

        def pairs(eng, body):
            body(0, 0, 0)
            body(1, 1, 1)
            with eng.Fori(1, TT // 2 - 1) as i:
                body(2 * i, 0, 2)
                body(2 * i + 1, 1, 3)
            body(TT - 2, 0, TT - 2)
            body(TT - 1, 1, TT - 1)

        def tile_cols(t):
            return bass.ds(t * P, P)

        def chunk_col(j, i):
            return (DPOOL, DPOOL + DCONV, 0)[j] + i * P

        def bc_row(v):
            return v.rearrange("a n -> (a n)").rearrange("(o n) -> o n", o=1).broadcast_to([P, v.shape[1]])

        @block.sync
        def _(sp):
            w_in_v = w_in[0].rearrange("(k q) n -> q k n", q=P)

            def chunk(j, i):
                sp.dma_start(wcs[j][:, :, :], w_in_v[:, :, bass.ds(chunk_col(j, i), P)]).then_inc(wc_in[j], 16)

            for t in range(TT):
                sp.dma_start(xh[:, t, :], x[0, t * P:(t + 1) * P, :]).then_inc(x_in[t], 16)
                if t == 1:
                    chunk(0, 0)
                    chunk(1, 0)
            chunk(2, 0)
            for i in range(1, HEADS):
                for j in range(3):
                    sp.wait_ge(wcl_ready[j], i)
                    chunk(j, i)
            sp.wait_ge(pooled_ready, HEADS)
            for k in range(KC):
                if k >= 2:
                    sp.wait_ge(wol_ready, k - 1)
                sp.dma_start(wos[k % 2][:, :], w_out[0, k * P:(k + 1) * P, :]).then_inc(wos_in[k % 2], 16)
            sp.wait_ge(conv_out, HEADS)
            sp.dma_start(g1[:, :], bc_row(ln1_g)).then_inc(ln1_in, 16)
            sp.dma_start(b1[:, :], bc_row(ln1_b)).then_inc(ln1_in, 16)
            h_rows = h_dram.rearrange("(t q c) n -> t q (c n)", q=P, c=2)

            def store_h(t, b, _):
                sp.wait_ge(h_ready, t + 1)
                sp.dma_start(h_rows[bass.ds(t, 1), :, :].rearrange("a q n -> (a q) n"), hb[b][:, :]).then_inc(h_stored[b], 16)

            pairs(sp, store_h)
            sp.wait_ge(h_stored[0], 16 * TT // 2)
            sp.wait_ge(h_stored[1], 16 * TT // 2)

            wg_v = w_gate[0].rearrange("e (k q) f -> e q k f", q=P)
            wu_v = w_up[0].rearrange("e (k q) f -> e q k f", q=P)
            wd_v = w_down[0].rearrange("e (k q) d -> e q k d", q=P)

            def load_gu(e, s):
                one = bass.ds(e, 1)
                sp.dma_start(gu_w[s][:, :, 0, :], wg_v[one, :, :, :].rearrange("a q k f -> (a q) k f")).then_inc(gu_in[s], 16)
                sp.dma_start(gu_w[s][:, :, 1, :], wu_v[one, :, :, :].rearrange("a q k f -> (a q) k f")).then_inc(gu_in[s], 16)

            def load_wd(e, s):
                one = bass.ds(e, 1)
                sp.dma_start(wd_w[s][:, :, :], wd_v[one, :, :, :].rearrange("a q k d -> (a q) k d")).then_inc(wd_in[s], 16)

            sp.wait_ge(op_done, TT)
            sp.wait_ge(h_kept, TT)
            sp.wait_ge(ht_done, TT)
            for s in range(2):
                load_gu(s, s)
                load_wd(s, s)
            load_gu(2, 2)
            sp.wait_ge(tab_done, 1)
            load_wd(2, 2)
            sp.wait_ge(tab_ready, 1)

            def next_expert(e, s):
                sp_end = sp.value_load(bnd[0:1, bass.ds(e - (SLOTS - 1), 1)], min_val=1, max_val=MAXB)
                sp.wait_ge(gu_done, sp_end)
                load_gu(e, s)
                sp.wait_ge(down_done, sp_end)
                load_wd(e, s)

            with sp.Fori(1, NE // SLOTS) as r:
                for s in range(SLOTS):
                    next_expert(SLOTS * r + s, s)
            for e in range(NE // SLOTS * SLOTS, NE):
                next_expert(e, e % SLOTS)

            sp_all = sp.value_load(bnd[0:1, NE:NE + 1], min_val=NE, max_val=MAXB - 1)
            sp.wait_ge(down_done, sp_all)
            for k in range(KC + KP):
                if k >= 2:
                    sp.wait_ge(wgl_ready, k - 1)
                src = w_ple_gate[0, k * P:(k + 1) * P, :] if k < KC else w_ple_proj[0, (k - KC) * P:(k - KC + 1) * P, :]
                sp.dma_start(wgs[k % 2][:, :], src).then_inc(wgs_in[k % 2], 16)
            sp.wait_ge(scat, sp_all * 16)
            for v, dst in ((ln2_g, g2), (ln2_b, b2), (ln3_g, g3), (ln3_b, b3)):
                sp.dma_start(dst[:, :], bc_row(v)).then_inc(ln23_in, 16)
            y_rows = y_dram.rearrange("(t q c) n -> t q (c n)", q=P, c=4)
            p_rows = p[0].rearrange("a (t q) n -> (a t) q n", q=P)
            out_rows = out.rearrange("a (t q) n -> (a t) q n", q=P)

            def load_tile(t, b):
                sp.dma_start(yp[b][:, :, :].rearrange("q c n -> q (c n)"),
                             y_rows[bass.ds(t, 1), :, :].rearrange("a q n -> (a q) n")).then_inc(yp_in[b], 16)
                sp.dma_start(pt[b][:, :], p_rows[bass.ds(t, 1), :, :].rearrange("a q n -> (a q) n")).then_inc(pt_in[b], 16)

            load_tile(0, 0)
            load_tile(1, 1)

            def last(t, b, at_least):
                if at_least < TT - 2:
                    sp.wait_ge(v2_ready, t + 1)
                    sp.wait_ge(yt_done, t + 1)
                    load_tile(t + 2, b)
                sp.wait_ge(o_ready, t + 1)
                sp.dma_start(out_rows[bass.ds(t, 1), :, :].rearrange("a q n -> (a q) n"), ob[b][:, :]).then_inc(o_stored[b], 16)

            pairs(sp, last)
            sp.wait_ge(o_stored[0], 16 * TT // 2)
            sp.wait_ge(o_stored[1], 16 * TT // 2)

        @block.gpsimd
        def _(pool):
            n_own = [0]

            def own(ins):
                n_own[0] += 1
                ins.then_inc(pool_own, 1)
                pool.wait_ge(pool_own, n_own[0])

            own(nc.gpsimd.memset(ident[:, :], 0.0))
            nc.gpsimd.affine_select(out=ident[:, :], in_=ident[:, :], compare_op=ALU.not_equal, fill=1.0,
                                    base=0, pattern=[[-1, P]], channel_multiplier=1).then_inc(ident_ready, 1)
            own(nc.gpsimd.memset(ones[:, :], 1.0))
            own(nc.gpsimd.memset(meanw[:, :], 1.0 / P))
            own(nc.gpsimd.affine_select(out=before[:, :], in_=ones[:, :], compare_op=ALU.is_gt, fill=0.0,
                                        base=0, pattern=[[1, P]], channel_multiplier=-1))
            own(nc.gpsimd.memset(epsv[:, :], EPS))
            own(nc.gpsimd.memset(onev[:, :], 1.0))
            own(nc.gpsimd.memset(upT[:, 0:WPAD], 0.0))
            own(nc.gpsimd.memset(uT[:, 0:PAD], 0.0))

            def ramp(dst, pattern, base_, mult):
                nc.gpsimd.iota(dst, pattern, base=base_, channel_multiplier=mult,
                               allow_small_or_imprecise_dtypes=True)

            ramp(io64[:, :], [[1, MAXB]], 0, 0)
            ramp(iolo[:, :], [[0, 2], [1, BT]], 0, 0)
            ramp(tokA[:, :, :], [[0, 2], [2 * P, TT]], -int(BIG), 2)
            ramp(tokB[:, :, :], [[2, 2], [4 * P, TT]], -int(BIG), 4)
            ramp(thr[:, :], [[BT, S // BT]], 0, 0)
            ramp(rev4[:, :], [[-1, NG]], NG, 0)
            ramp(rev8[:, :], [[-1, EG]], EG, 0)
            ramp(rcnt[:, :], [[1, WPAD]], 1, 0)
            own(nc.gpsimd.memset(halfv[0:BT, :], BIG))
            own(nc.gpsimd.memset(halfv[BT:P, :], BIG + 1.0))
            own(nc.gpsimd.memset(thr[:, 0:1], -1.0))
            nc.gpsimd.memset(cur[:, 0:1], 0.0).then_inc(consts, 1)

            def low(j, i):
                pool.wait_ge(wch_ready[j], i + 1)
                nc.gpsimd.tensor_tensor(wcl[j][:, :, :], wcs[j][:, :, :], wch[j][:, :, :].bitcast(f32), SUB)\
                    .then_inc(wcl_ready[j], 1)

            def windows(g):
                pool.wait_ge(up_ready, 2 * (g + 1))
                src, pad = upT, WPAD
                w = 1
                dsts = [win2, win3]
                if g:
                    pool.wait_ge(mix_done, 2 * g)
                cur_sum, cur_pad = upT, WPAD
                n = 0
                while w < WINDOWS[g]:
                    dst = dsts[n % 2]
                    a = cur_sum[:, cur_pad + w:cur_pad + S]
                    b = cur_sum[:, cur_pad:cur_pad + S - w]
                    own(nc.gpsimd.tensor_tensor(dst[:, w:S], a, b, ADD))
                    own(nc.gpsimd.tensor_copy(dst[:, 0:w], cur_sum[:, cur_pad:cur_pad + w]))
                    cur_sum, cur_pad = dst, 0
                    w *= 2
                    n += 1
                pool.wait_ge(rcnt_ready, 1)
                W = WINDOWS[g]
                own(nc.gpsimd.tensor_tensor(cur_sum[:, 0:W], cur_sum[:, 0:W], rcnt[:, 0:W], MUL))
                own(nc.gpsimd.tensor_scalar(cur_sum[:, W:S], cur_sum[:, W:S], 1.0 / W, None, MUL))
                pooled = dsts[n % 2]
                nc.gpsimd.tensor_tensor(pooled[:, :], cur_sum[:, 0:S], upT[:, WPAD:WPAD + S], SUB).then_inc(pooled_ready, 1)

            pool.wait_ge(small_in, 80)
            for j in range(3):
                low(j, 0)
            for g in range(NPG):
                if g + 1 < HEADS:
                    for j in range(3):
                        low(j, g + 1)
                windows(g)

            for k in range(KC):
                pool.wait_ge(woh_ready, k + 1)
                nc.gpsimd.tensor_tensor(wol[:, k, :], wos[k % 2][:, :], woh[:, k, :].bitcast(f32), SUB).then_inc(wol_ready, 1)

            pool.wait_ge(tab_ready, 1)
            nc.gpsimd.memset(hblk[:, :], 0.0).then_inc(pool_own, 1)
            n_own[0] += 1
            pool.wait_ge(pool_own, n_own[0])

            bound = pool.alloc_register("bound")
            nil = pool.alloc_register("nil")
            pool.reg_mov(nil, 0)

            def gather(n):
                nc.gpsimd.tensor_copy(gidx[:, :], gtab[:, bass.ds(n, 1)]).then_inc(gidx_ready, 1)
                pool.wait_ge(gidx_ready, n + 1)
                pool.reg_alu(bound, nil, 2 * S - 1, ADD)
                nc.gpsimd.indirect_dma_start(
                    out=hblk[:, :], out_offset=None, in_=h_dram,
                    in_offset=bass.IndirectOffsetOnAxis(ap=gidx[:, 0:1], axis=0),
                    bounds_check=bound, oob_is_err=False).then_inc(gath, 16)

            def scatter(n, first=False):
                if not first:
                    pool.wait_ge(scat, n * 16)
                nc.gpsimd.tensor_copy(sidx[:, :], stab[:, bass.ds(n, 1)]).then_inc(sidx_ready, 1)
                pool.wait_ge(sidx_ready, n + 1)
                pool.wait_ge(y_ready, n + 1)
                pool.reg_alu(bound, nil, 4 * S - 1, ADD)
                nc.gpsimd.indirect_dma_start(
                    out=y_dram, out_offset=bass.IndirectOffsetOnAxis(ap=sidx[:, 0:1], axis=0),
                    in_=yb[:, :], in_offset=None,
                    bounds_check=bound, oob_is_err=False).then_inc(scat, 16)

            pool.wait_ge(h_stored[0], 16 * TT // 2)
            pool.wait_ge(h_stored[1], 16 * TT // 2)
            gather(0)
            n_blocks = pool.value_load(bnd[0:1, NE:NE + 1], min_val=NE, max_val=MAXB - 1)
            pool.wait_ge(hbt_done, 1)
            gather(1)
            scatter(0, first=True)
            with pool.Fori(1, n_blocks) as n:
                pool.wait_ge(hbt_done, n + 1)
                gather(n + 1)
                scatter(n)
            pool.wait_ge(scat, n_blocks * 16)

        @block.scalar
        def _(act):
            CP = ACT.Copy
            for r, v in ((slice(0, TAPS), w_dw[0]), (slice(TAPS, TAPS + 1), b_dw), (slice(TAPS + 1, TAPS + 2), conv_ln_g),
                         (slice(TAPS + 2, TAPS + 3), conv_ln_b), (slice(TAPS + 3, TAPS + 4), pool_scale)):
                act.dma_start(rows[r, :], v).then_inc(rows_in, 16)
            act.dma_start(wmix[:, :, :], w_pool_mix[0].rearrange("g c d -> c g d")).then_inc(small_in, 16)
            act.dma_start(wr[:, :, 0:NG], w_coarse[0].rearrange("(k q) n -> q k n", q=P)).then_inc(small_in, 16)
            act.dma_start(wr[:, :, NG:NR], w_fine[0].rearrange("(k q) n -> q k n", q=P)).then_inc(small_in, 16)
            act.dma_start(rbias[:, 0:NG], bc_row(b_coarse)).then_inc(small_in, 16)
            act.dma_start(rbias[:, NG:NR], bc_row(b_fine)).then_inc(small_in, 16)

            def high(j, i):
                act.wait_ge(wc_in[j], 16 * (i + 1))
                nc.scalar.activation(wch[j][:, :, :], wcs[j][:, :, :], CP).then_inc(wch_ready[j], 1)

            for t in range(TT):
                act.wait_ge(xt_done, t + 1)
                nc.scalar.activation(xTh[:, :, t * P:(t + 1) * P],
                                     bank(2 * (t % 2), 2).rearrange("q (k m) -> q k m", k=KC), CP).then_inc(xh_ready, 1)
                if t == 1:
                    high(0, 0)
                    high(1, 0)
            high(2, 0)

            def head_in(i, later, first=False):
                for th in range(2):
                    act.wait_ge(z_done[1], 2 * i + th + 1)
                    if not first:
                        act.wait_ge(u_ready, 2 * i)
                    nc.scalar.activation(sig1[:, th * HALF:(th + 1) * HALF], bank(2 + th), ACT.Sigmoid).then_inc(sig_ready, 1)
                if later:
                    high(0, i + 1)
                    high(1, i + 1)
                for th in range(2):
                    act.wait_ge(z_done[2], 2 * i + th + 1)
                    if not first:
                        act.wait_ge(pooled_ready, i)
                    nc.scalar.activation(upT[:, WPAD + th * HALF:WPAD + (th + 1) * HALF], bank(4 + th), CP).then_inc(up_ready, 1)
                if later:
                    high(2, i + 1)

            def head_out(i):
                for th in range(2):
                    act.wait_ge(mix_done, 2 * i + th + 1)
                    nc.scalar.activation(mixT[:, bass.ds(i, 1), th * HALF:(th + 1) * HALF].rearrange("q a n -> q (a n)"),
                                         bank(6 + th), CP, scale=prm[:, i, NPRM - 1:NPRM]).then_inc(mix_ready, 1)
                for th in range(2):
                    cols = slice(th * HALF, (th + 1) * HALF)
                    act.wait_ge(dev_ready, 2 * i + th + 1)
                    nc.scalar.activation(sqr[:, cols], acc0[:, cols], ACT.Square).then_inc(sq_ready, 1)
                for th in range(2):
                    act.wait_ge(var_done, 2 * i + th + 1)
                    nc.scalar.activation(sqr[:, th * HALF:(th + 1) * HALF], bank(6 + th), ACT.Sqrt, bias=epsv[:, :]).then_inc(csd_ready, 1)
                act.wait_ge(yn_ready, i + 1)
                nc.scalar.activation(mixT[:, bass.ds(i + NPG, 1), :].rearrange("q a n -> q (a n)"), acc1[:, :], ACT.Silu,
                                     scale=cur[:, TAPS + 1:TAPS + 2], bias=cur[:, TAPS + 2:TAPS + 3]).then_inc(conv_out, 1)

            act.wait_ge(consts, 1)
            head_in(0, True, first=True)
            for i in range(1, HEADS - 1):
                head_in(i, True)
                head_out(i - 1)
            head_in(HEADS - 1, False)
            head_out(HEADS - 2)
            def w_out_high(k):
                act.wait_ge(wos_in[k % 2], 16 * (k // 2 + 1))
                nc.scalar.activation(woh[:, k, :], wos[k % 2][:, :], CP).then_inc(woh_ready, 1)

            act.wait_ge(z_done[2], 2 * HEADS)
            for k in range(KC):
                w_out_high(k)
            head_out(HEADS - 1)

            def split_mix(t, b):
                nc.scalar.activation(mh[b][:, :, :], mixT[:, :, tile_cols(t)], CP).then_inc(mh_ready, 1)

            def evac_ht(t, b):
                act.wait_ge(ht_done, t + 1)
                nc.scalar.activation(hTt[b][:, :, :], bank(4, 2).rearrange("q (k m) -> q k m", k=KC), CP).then_inc(ht_ready, 1)

            act.wait_ge(conv_out, HEADS)
            act.wait_ge(mix_ready, 2 * NPG)
            split_mix(0, 0)

            def proj_tile(t, b, at_least):
                if at_least < TT - 1:
                    if at_least >= 1:
                        act.wait_ge(op_done, t)
                    split_mix(t + 1, 1 - b)
                act.wait_ge(var1_ready, t + 1)
                nc.scalar.activation(sd1[:, 0:1], mv1[:, 1:2], ACT.Sqrt, bias=epsv[:, :]).then_inc(sd1_ready, 1)
                act.wait_ge(h_ready, t + 1)
                nc.scalar.activation(xh[:, bass.ds(t, 1), :].rearrange("q a n -> q (a n)"), hb[b][:, :], CP, scale=ALPHA).then_inc(h_kept, 1)
                if at_least >= 1:
                    evac_ht(t - 1, 1 - b)

            pairs(act, proj_tile)
            evac_ht(TT - 1, 1)

            act.wait_ge(cd_ready, 1)
            nc.scalar.activation(ce[:, :, :], cd[:, :, :], ACT.Exp).then_inc(ce_ready, 1)
            act.wait_ge(m2_ready, 1)
            nc.scalar.activation(ex[:, :], m2[:, :], ACT.Exp).then_inc(ex_ready, 1)

            act.wait_ge(tab_ready, 1)
            act_blocks = act.value_load(bnd[0:1, NE:NE + 1], min_val=NE, max_val=MAXB - 1)

            def act_block(n, first=False):
                act.wait_ge(gu_done, n + 1)
                nc.scalar.activation(sg[:, :], bank(0)[:, 0:FE // 2], ACT.Silu).then_inc(silu_ready, 1)
                act.wait_ge(at_done, n + 1)
                nc.scalar.activation(aT[:, :, :, :].rearrange("q c h m -> q (c h m)"), bank(2)[:, 0:FE // 2], CP).then_inc(at_ready, 1)
                act.wait_ge(down_done, n + 1)
                if not first:
                    act.wait_ge(scat, n * 16)
                nc.scalar.activation(yb[:, :], bank(3), CP).then_inc(y_ready, 1)

            act_block(0, first=True)
            with act.Fori(1, act_blocks) as n:
                act_block(n)

            for k in range(KC + KP):
                act.wait_ge(wgs_in[k % 2], 16 * (k // 2 + 1))
                dst = wgh[:, k, :] if k < KC else wph[:, k - KC, :]
                nc.scalar.activation(dst, wgs[k % 2][:, :], CP).then_inc(wgh_ready, 1)

            def finish_tile(t):
                act.wait_ge(ple_done, t + 1)
                nc.scalar.activation(sg3[:, :], bank(3, 2), ACT.Sigmoid).then_inc(sig3_ready, 1)
                act.wait_ge(var3_ready, t + 1)
                nc.scalar.activation(sd3[:, 0:1], mv3[:, 1:2], ACT.Sqrt, bias=epsv[:, :]).then_inc(sd3_ready, 1)

            def last_tile(t, b, at_least):
                act.wait_ge(var2_ready, t + 1)
                nc.scalar.activation(sd3[:, 1:2], mv3[:, 1:2], ACT.Sqrt, bias=epsv[:, :]).then_inc(sd2_ready, 1)
                act.wait_ge(yt_done, t + 1)
                nc.scalar.activation(pTh[b][:, :, :], bank(2)[:, 0:DP].rearrange("q (k m) -> q k m", k=KP), CP)
                nc.scalar.activation(yTh[b][:, :, :], bank(0, 2).rearrange("q (k m) -> q k m", k=KC), CP).then_inc(yth_ready, 1)
                if at_least >= 1:
                    finish_tile(t - 1)

            pairs(act, last_tile)
            finish_tile(TT - 1)

        @block.vector
        def _(dve):
            V = nc.vector
            n_own = [0]

            def own(ins):
                n_own[0] += 1
                ins.then_inc(dve_own, 1)
                dve.wait_ge(dve_own, n_own[0])

            for t in range(TT):
                dve.wait_ge(xh_ready, t + 1)
                cols = slice(t * P, (t + 1) * P)
                V.tensor_tensor(xTl[:, :, cols], bank(2 * (t % 2), 2).rearrange("q (k m) -> q k m", k=KC),
                                xTh[:, :, cols].bitcast(f32), SUB).then_inc(xl_ready, 1)
            dve.wait_ge(prm_done, 1)
            V.tensor_copy(prm[:, :, :].rearrange("q h n -> q (h n)"), bank(7)[:, 0:HEADS * NPRM]).then_inc(prm_ready, 1)
            dve.wait_ge(prm_ready, 1)
            dve.wait_ge(consts, 1)
            V.reciprocal(rcnt[:, :], rcnt[:, :]).then_inc(rcnt_ready, 1)
            NSTEP = TAPS + 1

            def conv_head(i, first=False):
                if not first:
                    dve.wait_ge(conv_out, i)
                V.tensor_copy(cur[:, :], prm[:, bass.ds(i, 1), :].rearrange("q a n -> q (a n)")).then_inc(conv_step, 1)
                for th in range(2):
                    dve.wait_ge(sig_ready, 2 * i + th + 1)
                    dve.wait_ge(z_done[0], 2 * i + th + 1)
                    cols = slice(th * HALF, (th + 1) * HALF)
                    V.tensor_tensor(uT[:, PAD + th * HALF:PAD + (th + 1) * HALF], bank(th), sig1[:, cols], MUL).then_inc(u_ready, 1)
                dve.wait_ge(u_ready, 2 * (i + 1))
                dve.wait_ge(conv_step, i * NSTEP + 1)
                V.tensor_scalar(acc0[:, :], uT[:, 0:S], cur[:, 0:1], cur[:, TAPS:TAPS + 1], MUL, ADD).then_inc(conv_step, 1)
                V.tensor_scalar(acc1[:, :], uT[:, 1:1 + S], cur[:, 1:2], None, MUL).then_inc(conv_step, 1)
                for j in range(2, TAPS):
                    acc = (acc0, acc1)[j % 2]
                    dve.wait_ge(conv_step, i * NSTEP + j)
                    V.scalar_tensor_tensor(acc[:, :], uT[:, j:j + S], cur[:, j:j + 1], acc[:, :], MUL, ADD).then_inc(conv_step, 1)
                dve.wait_ge(conv_step, (i + 1) * NSTEP)
                for th in range(2):
                    cols = slice(th * HALF, (th + 1) * HALF)
                    V.tensor_tensor(acc0[:, cols], acc0[:, cols], acc1[:, cols], ADD).then_inc(conv_ready, 1)
                for th in range(2):
                    cols = slice(th * HALF, (th + 1) * HALF)
                    dve.wait_ge(mean_done, 2 * i + th + 1)
                    V.tensor_tensor(acc0[:, cols], acc0[:, cols], bank(6 + th), SUB).then_inc(dev_ready, 1)
                dve.wait_ge(csd_ready, 2 * (i + 1))
                V.reciprocal(sqr[:, :], sqr[:, :]).then_inc(conv_rec, 1)
                dve.wait_ge(conv_rec, i + 1)
                V.tensor_tensor(acc1[:, :], acc0[:, :], sqr[:, :], MUL).then_inc(yn_ready, 1)

            conv_head(0, first=True)
            with dve.Fori(1, HEADS) as i:
                conv_head(i)

            def split_mix(t, b):
                dve.wait_ge(mh_ready, t + 1)
                V.tensor_tensor(ml[b][:, :, :], mixT[:, :, tile_cols(t)], mh[b][:, :, :].bitcast(f32), SUB).then_inc(ml_ready, 1)

            def logits(t):
                dve.wait_ge(rt_done, t + 1)
                V.tensor_tensor(lg[:, bass.ds(t, 1), :].rearrange("q a n -> q (a n)"), bank(6)[:, 0:NR], rbias[:, :], ADD).then_inc(lg_ready, 1)

            dve.wait_ge(ln1_in, 32)
            dve.wait_ge(small_in, 80)
            split_mix(0, 0)
            LN1 = 5

            def proj_tile(t, b, at_least):
                xt = xh[:, bass.ds(t, 1), :].rearrange("q a n -> q (a n)")
                if at_least >= 1:
                    dve.wait_ge(h_ready, t)
                dve.wait_ge(op_done, t + 1)
                V.scalar_tensor_tensor(vt1[:, :], xt, ALPHA, bank(2 * b, 2), MUL, ADD).then_inc(v1_ready, 1)
                if at_least < TT - 1:
                    split_mix(t + 1, 1 - b)
                dve.wait_ge(v1_ready, t + 1)
                n = t * LN1
                for c in range(2):
                    V.bn_stats(st1[:, c, :], vt1[:, c * 512:(c + 1) * 512]).then_inc(ln1_own, 1)
                dve.wait_ge(ln1_own, n + 2)
                V.memset(turn1[:, :], 0.0)
                V.bn_aggr(mv1[:, :], st1[:, :, :].rearrange("q c s -> q (c s)")).then_inc(var1_ready, 1)
                dve.wait_ge(sd1_ready, t + 1)
                V.reciprocal(sd1[:, 1:2], sd1[:, 0:1]).then_inc(ln1_own, 1)
                dve.wait_ge(ln1_own, n + 3)
                dve.wait_ge(var1_ready, t + 1)
                V.tensor_scalar(vt1[:, :], vt1[:, :], mv1[:, 0:1], sd1[:, 1:2], SUB, MUL).then_inc(ln1_own, 1)
                dve.wait_ge(ln1_own, n + 4)
                V.tensor_tensor(vt1[:, :], vt1[:, :], g1[:, :], MUL).then_inc(ln1_own, 1)
                dve.wait_ge(ln1_own, n + 5)
                if at_least >= 2:
                    dve.wait_ge(h_stored[b], (t - b) * 8)
                    dve.wait_ge(h_kept, t - 1)
                    dve.wait_ge(ht_done, t - 1)
                V.tensor_tensor(hb[b][:, :], vt1[:, :], b1[:, :], ADD).then_inc(h_ready, 1)
                if at_least >= 1:
                    logits(t - 1)

            pairs(dve, proj_tile)
            logits(TT - 1)

            dve.wait_ge(lg_ready, TT)
            coarse = lg[:, :, 0:NG]
            fine = lg[:, :, NG:NR].rearrange("q t (g e) -> q t g e", g=NG)

            def over(a, *shape):
                return a.broadcast_to([P, *shape])

            own(V.tensor_reduce(cm[:, :], coarse, op=ALU.max, axis=AX.X))
            V.tensor_tensor(cd[:, :, :], coarse, over(cm[:, :].unsqueeze(2), TT, NG), SUB).then_inc(cd_ready, 1)
            dve.wait_ge(cd_ready, 1)
            own(V.tensor_scalar(ohg[:, :, :], cd[:, :, :], 0.0, None, ALU.is_ge))
            own(V.tensor_tensor(ohg[:, :, :], ohg[:, :, :], over(rev4[:, :].unsqueeze(1), TT, NG), MUL))
            own(V.tensor_reduce(cm[:, :], ohg[:, :, :], op=ALU.max, axis=AX.X))
            own(V.tensor_tensor(ohg[:, :, :], over(rev4[:, :].unsqueeze(1), TT, NG), over(cm[:, :].unsqueeze(2), TT, NG), ALU.is_equal))
            own(V.tensor_tensor(gsel[:, :, :, :], fine, over(ohg[:, :, :].unsqueeze(3), TT, NG, EG), MUL))
            own(V.tensor_reduce(sel[:, :, :], gsel[:, :, :, :].rearrange("q t g e -> q t e g"), op=ADD, axis=AX.X))
            own(V.tensor_reduce(cm[:, :], sel[:, :, :], op=ALU.max, axis=AX.X))
            own(V.tensor_tensor(sel[:, :, :], sel[:, :, :], over(cm[:, :].unsqueeze(2), TT, EG), SUB))

            def first_max(src, limit, dst):
                own(V.tensor_tensor(dst, src, limit, ALU.is_ge))
                own(V.tensor_tensor(dst, dst, over(rev8[:, :].unsqueeze(1), TT, EG), MUL))
                own(V.tensor_reduce(cm[:, :], dst, op=ALU.max, axis=AX.X))
                own(V.tensor_tensor(dst, over(rev8[:, :].unsqueeze(1), TT, EG), over(cm[:, :].unsqueeze(2), TT, EG), ALU.is_equal))

            own(V.memset(m2[:, :], 0.0))
            first_max(sel[:, :, :], over(m2[:, :].unsqueeze(2), TT, EG), oh12[:, 0, :, :])
            own(V.scalar_tensor_tensor(sel2[:, :, :], oh12[:, 0, :, :], -1e30, sel[:, :, :], MUL, ADD))
            V.tensor_reduce(m2[:, :], sel2[:, :, :], op=ALU.max, axis=AX.X).then_inc(m2_ready, 1)
            dve.wait_ge(m2_ready, 1)
            first_max(sel2[:, :, :], over(m2[:, :].unsqueeze(2), TT, EG), oh12[:, 1, :, :])
            for k in range(2):
                ins = V.tensor_tensor(onehot[:, k, :, :, :], over(ohg[:, :, :].unsqueeze(3), TT, NG, EG),
                                      over(oh12[:, k, :, :].unsqueeze(2), TT, NG, EG), MUL)
                own(ins)
            V.tensor_tensor(gsel[:, :, :, :], onehot[:, 0, :, :, :], onehot[:, 1, :, :, :], ADD).then_inc(oneh_ready, 1)
            dve.wait_ge(ce_ready, 1)
            own(V.tensor_reduce(cs[:, :], ce[:, :, :], op=ADD, axis=AX.X))
            dve.wait_ge(ex_ready, 1)
            own(V.scalar_tensor_tensor(cs[:, :], ex[:, :], 1.0, cs[:, :], ADD, MUL))
            own(V.reciprocal(wts[:, 0, :], cs[:, :]))
            own(V.tensor_tensor(wts[:, 1, :], wts[:, 0, :], ex[:, :], MUL))
            dve.wait_ge(rank_done, 1)
            tot = bank(1)[:, 0:TT * NE].rearrange("q (t e) -> q t e", t=TT)
            rank = bank(0)[:, 0:TT * NE].rearrange("q (t e) -> q t e", t=TT)
            own(V.memset(tpre[:, 0, :], 0.0))
            for t in range(TT):
                own(V.tensor_tensor(tpre[:, t + 1, :], tpre[:, t, :], tot[:, t, :], ADD))
            own(V.tensor_tensor(cmp16[:, :, :], over(tpre[:, TT, :].unsqueeze(2), NE, S // BT),
                                over(thr[:, :].unsqueeze(1), NE, S // BT), ALU.is_gt))
            own(V.tensor_reduce(nbf[:, :], cmp16[:, :, :], op=ADD, axis=AX.X))
            own(V.tensor_tensor_scan(incl[:, :], onev[:, :], nbf[:, :], 0.0, MUL, ADD))
            own(V.memset(bnd[:, 0:1], 0))
            own(V.tensor_copy(bnd[:, 1:NE + 1], incl[:, :]))
            own(V.tensor_tensor(nbf[:, :], incl[:, :], nbf[:, :], SUB))
            own(V.scalar_tensor_tensor(base[:, :, :], over(nbf[:, :].unsqueeze(1), TT, NE), float(BT), tpre[:, 0:TT, :], MUL, ADD))
            own(V.tensor_tensor(base[:, :, :], base[:, :, :], rank, ADD))
            for k in range(2):
                own(V.tensor_tensor(onehot[:, k, :, :, :].rearrange("q t g e -> q t (g e)"),
                                    onehot[:, k, :, :, :].rearrange("q t g e -> q t (g e)"), base[:, :, :], MUL))
                own(V.tensor_reduce(posf[:, k * TT:(k + 1) * TT], onehot[:, k, :, :, :].rearrange("q t g e -> q t (g e)"),
                                    op=ADD, axis=AX.X))
            own(V.tensor_copy(posi[:, :], posf[:, :]))
            own(V.tensor_scalar(posi[:, :], posi[:, :], 6, None, ALU.arith_shift_right))
            own(V.tensor_copy(hif[:, :], posi[:, :]))
            own(V.scalar_tensor_tensor(posf[:, :], hif[:, :], -float(BT), posf[:, :], MUL, ADD))
            own(V.tensor_tensor(ohlo[:, :, :], over(iolo[:, :].unsqueeze(1), 2 * TT, P), over(posf[:, :].unsqueeze(2), 2 * TT, P), ALU.is_equal))
            own(V.tensor_tensor(ohhi[:, :, :], over(io64[:, :].unsqueeze(1), 2 * TT, MAXB), over(hif[:, :].unsqueeze(2), 2 * TT, MAXB), ALU.is_equal))
            for c, tok in ((0, tokA), (1, tokB)):
                V.tensor_tensor(ohab[:, :, c, :], ohhi[:, :, :],
                                over(tok[:, :, :].rearrange("q k t -> q (k t)").unsqueeze(2), 2 * TT, MAXB), MUL).then_inc(oh_ready, 1)
            dve.wait_ge(tab_done, 1)
            own(V.tensor_scalar(gtab[:, :], bank(0)[:, 0:MAXB], halfv[:, :], None, ADD))
            V.tensor_scalar(stab[:, :], bank(0)[:, MAXB:2 * MAXB], halfv[:, :], None, ADD).then_inc(tab_ready, 1)
            dve.wait_ge(tab_ready, 1)

            dve_blocks = dve.value_load(bnd[0:1, NE:NE + 1], min_val=NE, max_val=MAXB - 1)

            def h_block(n):
                dve.wait_ge(hbt_done, n)
                V.tensor_copy(hTb[:, :, :, :].rearrange("q c h m -> q (c h m)"), bank(1)).then_inc(hbt_ready, 1)

            h_block(1)
            with dve.Fori(0, dve_blocks) as n:
                dve.wait_ge(silu_ready, n + 1)
                V.tensor_tensor(gact[:, :], sg[:, :], bank(0)[:, FE // 2:FE], MUL).then_inc(gact_ready, 1)
                h_block(n + 2)

            for k in range(KC + KP):
                dve.wait_ge(wgh_ready, k + 1)
                hi, lo = (wgh[:, k, :], wgl[:, k, :]) if k < KC else (wph[:, k - KC, :], wpl[:, k - KC, :])
                V.tensor_tensor(lo, wgs[k % 2][:, :], hi.bitcast(f32), SUB).then_inc(wgl_ready, 1)
            dve.wait_ge(ln23_in, 64)

            def finish_tile(t, b, at_least):
                n = t * 6
                if at_least >= 1:
                    dve.wait_ge(o_ready, t)
                dve.wait_ge(sig3_ready, t + 1)
                V.tensor_tensor(z3[:, :], sg3[:, :], bank(5, 2), MUL).then_inc(ln3_own, 1)
                dve.wait_ge(ln3_own, n + 1)
                V.scalar_tensor_tensor(z3[:, :], yt[b][:, :], ALPHA, z3[:, :], MUL, ADD).then_inc(z3_ready, 1)
                dve.wait_ge(z3_ready, t + 1)
                for c in range(2):
                    V.bn_stats(st3[:, c, :], z3[:, c * 512:(c + 1) * 512]).then_inc(ln3_own, 1)
                dve.wait_ge(ln3_own, n + 3)
                V.memset(turn3[:, :], 0.0)
                V.bn_aggr(mv3[:, :], st3[:, :, :].rearrange("q c s -> q (c s)")).then_inc(var3_ready, 1)
                dve.wait_ge(sd3_ready, t + 1)
                dve.wait_ge(var3_ready, t + 1)
                V.reciprocal(sd3[:, 0:1], sd3[:, 0:1]).then_inc(ln3_own, 1)
                dve.wait_ge(ln3_own, n + 4)
                V.tensor_scalar(z3[:, :], z3[:, :], mv3[:, 0:1], sd3[:, 0:1], SUB, MUL).then_inc(ln3_own, 1)
                dve.wait_ge(ln3_own, n + 5)
                V.tensor_tensor(z3[:, :], z3[:, :], g3[:, :], MUL).then_inc(ln3_own, 1)
                dve.wait_ge(ln3_own, n + 6)
                if at_least >= 2:
                    dve.wait_ge(o_stored[b], (t - b) * 8)
                V.tensor_tensor(ob[b][:, :], z3[:, :], b3[:, :], ADD).then_inc(o_ready, 1)

            def last_tile(t, b, at_least):
                n = t * 5
                xt = xh[:, bass.ds(t, 1), :].rearrange("q a n -> q (a n)")
                dve.wait_ge(yp_in[b], (t - b) * 8 + 16)
                V.scalar_tensor_tensor(xt, yp[b][:, 0, :], wts[:, 0, bass.ds(t, 1)], xt, MUL, ADD).then_inc(ln2_own, 1)
                dve.wait_ge(ln2_own, n + 1)
                V.scalar_tensor_tensor(yt[b][:, :], yp[b][:, 1, :], wts[:, 1, bass.ds(t, 1)], xt, MUL, ADD).then_inc(v2_ready, 1)
                dve.wait_ge(v2_ready, t + 1)
                for c in range(2):
                    V.bn_stats(st3[:, c, :], yt[b][:, c * 512:(c + 1) * 512]).then_inc(ln2_own, 1)
                dve.wait_ge(ln2_own, n + 3)
                V.memset(turn3[:, :], 0.0)
                V.bn_aggr(mv3[:, :], st3[:, :, :].rearrange("q c s -> q (c s)")).then_inc(var2_ready, 1)
                dve.wait_ge(sd2_ready, t + 1)
                dve.wait_ge(var2_ready, t + 1)
                V.reciprocal(sd3[:, 1:2], sd3[:, 1:2]).then_inc(ln2_own, 1)
                dve.wait_ge(ln2_own, n + 4)
                V.tensor_scalar(yt[b][:, :], yt[b][:, :], mv3[:, 0:1], sd3[:, 1:2], SUB, MUL).then_inc(ln2_own, 1)
                dve.wait_ge(ln2_own, n + 5)
                V.tensor_tensor(yt[b][:, :], yt[b][:, :], g2[:, :], MUL).then_inc(y2_own, 1)
                dve.wait_ge(y2_own, t + 1)
                V.tensor_tensor(yt[b][:, :], yt[b][:, :], b2[:, :], ADD).then_inc(y2_ready, 1)
                dve.wait_ge(yth_ready, t + 1)
                V.tensor_tensor(pTl[b][:, :, :], bank(2)[:, 0:DP].rearrange("q (k m) -> q k m", k=KP),
                                pTh[b][:, :, :].bitcast(f32), SUB)
                V.tensor_tensor(yTl[b][:, :, :], bank(0, 2).rearrange("q (k m) -> q k m", k=KC),
                                yTh[b][:, :, :].bitcast(f32), SUB).then_inc(ytl_ready, 1)
                if at_least >= 1:
                    finish_tile(t - 1, 1 - b, at_least - 1)

            pairs(dve, last_tile)
            finish_tile(TT - 1, 1, TT - 1)

        @block.tensor
        def _(pe):
            T = nc.tensor
            pe.wait_ge(ident_ready, 1)
            for t in range(TT):
                pe.wait_ge(x_in[t], 16)
                if t >= 2:
                    pe.wait_ge(xl_ready, t - 1)
                for k in range(KC):
                    ins = T.transpose(ps[:, 2 * (t % 2) + k // 4, (k % 4) * P:(k % 4 + 1) * P], xh[:, t, k * P:(k + 1) * P], ident[:, :])
                ins.then_inc(xt_done, 1)
            pe.wait_ge(rows_in, 80)
            for h in range(HEADS):
                ins = T.transpose(bank(7)[:, h * NPRM:(h + 1) * NPRM], rows[:, h * P:(h + 1) * P], ident[0:NPRM, 0:NPRM])
            ins.then_inc(prm_done, 1)
            pe.wait_ge(xl_ready, TT)
            pe.wait_ge(consts, 1)
            pe.wait_ge(prm_ready, 1)

            def z_chunk(j, i, first=False):
                pe.wait_ge(wcl_ready[j], i + 1)
                if not first:
                    if j < 2:
                        pe.wait_ge(u_ready, 2 * i)
                    else:
                        pe.wait_ge(up_ready, 2 * i)
                for th in range(2):
                    cols = slice(th * HALF, (th + 1) * HALF)
                    for k in range(KC):
                        ins = passes(bank(2 * j + th), wch[j][:, k, :], wcl[j][:, k, :], xTh[:, k, cols], xTl[:, k, cols], k == 0, k == KC - 1)
                    ins.then_inc(z_done[j], 1)

            def pool_mix(i):
                g = i
                pooled = (win2, win3)[(g + 1) % 2]
                pe.wait_ge(pooled_ready, g + 1)
                if g:
                    pe.wait_ge(csd_ready, 2 * g)
                for th in range(2):
                    T.matmul(bank(6 + th), wmix[:, g, :], pooled[:, th * HALF:(th + 1) * HALF], start=True, stop=True).then_inc(mix_done, 1)

            def head_stats(i):
                pe.wait_ge(mix_ready, 2 * (i + 1))
                for th in range(2):
                    pe.wait_ge(conv_ready, 2 * i + th + 1)
                    T.matmul(bank(6 + th), meanw[:, :], acc0[:, th * HALF:(th + 1) * HALF], start=True, stop=True).then_inc(mean_done, 1)
                for th in range(2):
                    pe.wait_ge(sq_ready, 2 * i + th + 1)
                    T.matmul(bank(6 + th), meanw[:, :], sqr[:, th * HALF:(th + 1) * HALF], start=True, stop=True).then_inc(var_done, 1)

            pe.wait_ge(small_in, 80)
            z_chunk(0, 0, first=True)
            z_chunk(1, 0, first=True)
            z_chunk(2, 0, first=True)
            for i in range(1, HEADS):
                z_chunk(0, i)
                z_chunk(1, i)
                pool_mix(i - 1)
                z_chunk(2, i)
                head_stats(i - 1)
            pool_mix(HEADS - 1)
            head_stats(HEADS - 1)

            pe.wait_ge(wol_ready, KC)
            pe.wait_ge(small_in, 80)

            def route(t, b):
                pe.wait_ge(h_ready, t + 1)
                for k in range(KC):
                    ins = T.transpose(ps[:, 4 + k // 4, (k % 4) * P:(k % 4 + 1) * P], hb[b][:, k * P:(k + 1) * P], ident[:, :])
                ins.then_inc(ht_done, 1)

            def route_mm(t, b, first):
                pe.wait_ge(ht_ready, t + 1)
                if not first:
                    pe.wait_ge(lg_ready, t)
                for k in range(KC):
                    ins = T.matmul(bank(6)[:, 0:NR], hTt[b][:, k, :], wr[:, k, :], start=(k == 0), stop=(k == KC - 1))
                ins.then_inc(rt_done, 1)

            def proj_tile(t, b, at_least):
                pe.wait_ge(ml_ready, t + 1)
                if at_least >= 2:
                    pe.wait_ge(v1_ready, t - 1)
                for c in range(2):
                    for k in range(KC):
                        ins = passes(bank(2 * b + c), mh[b][:, k, :], ml[b][:, k, :], woh[:, k, c * 512:(c + 1) * 512],
                                     wol[:, k, c * 512:(c + 1) * 512], k == 0, k == KC - 1)
                ins.then_inc(op_done, 1)
                if at_least >= 1:
                    route(t - 1, 1 - b)
                    route_mm(t - 1, 1 - b, at_least == 1)

            pairs(pe, proj_tile)
            route(TT - 1, 1)
            route_mm(TT - 1, 1, False)

            pe.wait_ge(oneh_ready, 1)
            M = gsel[:, :, :, :].rearrange("q t g e -> q (t g e)")
            T.matmul(bank(0)[:, 0:TT * NE], before[:, :], M, start=True, stop=True)
            T.matmul(bank(1)[:, 0:TT * NE], ones[:, :], M, start=True, stop=True).then_inc(rank_done, 1)
            pe.wait_ge(oh_ready, 2)
            for a in range(2 * TT):
                ins = T.matmul(bank(0)[:, 0:2 * MAXB], ohlo[:, a, :], ohab[:, a, :, :].rearrange("q c n -> q (c n)"),
                               start=(a == 0), stop=(a == 2 * TT - 1))
            ins.then_inc(tab_done, 1)
            pe.wait_ge(tab_ready, 1)

            def h_block(n):
                pe.wait_ge(gath, 16 * n)
                for c in range(KC // 2):
                    ins = T.transpose(bank(1)[:, c * P:(c + 1) * P], hblk[:, c * P:(c + 1) * P], ident[:, :])
                ins.then_inc(hbt_done, 1)

            def expert_block(n, s, r):
                pe.wait_ge(hbt_ready, n + 1)
                pe.wait_ge(gu_in[s], 32 * (r + 1))
                for k in range(KC):
                    for j in range(2):
                        ins = T.matmul(ps[j * BT:(j + 1) * BT, 0, :].rearrange("q (c n) -> q c n", c=2),
                                       hTb[:, k % (KC // 2), k // (KC // 2), :],
                                       gu_w[s][:, k, :, j * (FE // 2):(j + 1) * (FE // 2)],
                                       start=(k == 0), stop=(k == KC - 1))
                ins.then_inc(gu_done, 1)
                h_block(n + 2)
                pe.wait_ge(gact_ready, n + 1)
                for c in range(KF // 2):
                    ins = T.transpose(bank(2)[:, c * P:(c + 1) * P], gact[:, c * P:(c + 1) * P], ident[:, :])
                ins.then_inc(at_done, 1)
                pe.wait_ge(at_ready, n + 1)
                pe.wait_ge(wd_in[s], 16 * (r + 1))
                for k in range(KF):
                    for j in range(2):
                        ins = T.matmul(ps[j * BT:(j + 1) * BT, 3, :], aT[:, k % (KF // 2), k // (KF // 2), :],
                                       wd_w[s][:, k, j * (D // 2):(j + 1) * (D // 2)],
                                       start=(k == 0), stop=(k == KF - 1))
                ins.then_inc(down_done, 1)

            h_block(1)

            def expert(e, s, r):
                lo = pe.value_load(bnd[0:1, bass.ds(e, 1)], min_val=0, max_val=MAXB)
                hi = pe.value_load(bnd[0:1, bass.ds(e + 1, 1)], min_val=1, max_val=MAXB)
                with pe.Fori(lo, hi) as n:
                    expert_block(n, s, r)

            with pe.Fori(0, NE // SLOTS) as r:
                for s in range(SLOTS):
                    expert(SLOTS * r + s, s, r)
            for e in range(NE // SLOTS * SLOTS, NE):
                expert(e, e % SLOTS, NE // SLOTS)

            pe.wait_ge(wgl_ready, KC + KP)

            def turn(t, b, at_least):
                pe.wait_ge(pt_in[b], (t - b) * 8 + 16)
                pe.wait_ge(y2_ready, t + 1)
                if at_least >= 1:
                    pe.wait_ge(ytl_ready, t)
                for k in range(KP):
                    T.transpose(bank(2)[:, k * P:(k + 1) * P], pt[b][:, k * P:(k + 1) * P], ident[:, :])
                for k in range(KC):
                    ins = T.transpose(ps[:, k // 4, (k % 4) * P:(k % 4 + 1) * P], yt[b][:, k * P:(k + 1) * P], ident[:, :])
                ins.then_inc(yt_done, 1)

            def gate(t, b, at_least):
                pe.wait_ge(ytl_ready, t + 1)
                if at_least >= 1:
                    pe.wait_ge(z3_ready, t)
                for c in range(2):
                    cols = slice(c * 512, (c + 1) * 512)
                    for k in range(KC):
                        passes(bank(3 + c), yTh[b][:, k, :], yTl[b][:, k, :], wgh[:, k, cols], wgl[:, k, cols], k == 0, k == KC - 1)
                    for k in range(KP):
                        ins = passes(bank(5 + c), pTh[b][:, k, :], pTl[b][:, k, :], wph[:, k, cols], wpl[:, k, cols], k == 0, k == KP - 1)
                ins.then_inc(ple_done, 1)

            def last_tile(t, b, at_least):
                turn(t, b, at_least)
                if at_least >= 1:
                    gate(t - 1, 1 - b, at_least - 1)

            pairs(pe, last_tile)
            gate(TT - 1, 1, TT - 1)


_INS = ['x', 'p', 'w_in', 'w_pool_mix', 'pool_scale', 'w_dw', 'b_dw', 'conv_ln_g', 'conv_ln_b', 'w_out',
        'ln1_g', 'ln1_b', 'w_coarse', 'b_coarse', 'w_fine', 'b_fine', 'w_gate', 'w_up', 'w_down',
        'ln2_g', 'ln2_b', 'w_ple_proj', 'w_ple_gate', 'ln3_g', 'ln3_b']


def kernel(**inputs):
    import numpy as _np
    import concourse.bacc as _bacc
    from concourse import mybir as _mybir
    from concourse.bass_utils import run_bass_kernel_spmd as _run

    nc = _bacc.Bacc("TRN2", target_bir_lowering=False, num_devices=1)
    arrays, args = {}, []
    for name in _INS:
        a = _np.ascontiguousarray(inputs[name])
        arrays[f"in_{name}_dram"] = a
        args.append(nc.dram_tensor(f"in_{name}_dram", a.shape, _mybir.dt.from_np(a.dtype), kind="ExternalInput").ap())
    shape = inputs['x'].shape
    args.append(nc.dram_tensor("out_0_dram", shape, _mybir.dt.float32, kind="ExternalOutput").ap())
    build_block(nc, *args)
    r = _run(nc, [arrays], core_ids=[0])
    return r.results[0]["out_0_dram"]
```

```python
import concourse.bass as bass
from concourse import mybir
from contextlib import ExitStack

P = 128


def build_block(nc, x, p, w_in, w_pool_mix, pool_scale, w_dw, b_dw, conv_ln_g, conv_ln_b, w_out,
                ln1_g, ln1_b, w_coarse, b_coarse, w_fine, b_fine, w_gate, w_up, w_down,
                ln2_g, ln2_b, w_ple_proj, w_ple_gate, ln3_g, ln3_b, out, *debug):
    f32, f32r, i32 = mybir.dt.float32, mybir.dt.float32r, mybir.dt.int32
    ALU, ACT, AX = mybir.AluOpType, mybir.ActivationFunctionType, mybir.AxisListType
    ADD, SUB, MUL = ALU.add, ALU.subtract, ALU.mult

    _, S, D = x.shape
    TT = S // P
    KC = D // P
    HALF = S // 2
    DEPTH = p.shape[0]
    DP = p.shape[3]
    KP = DP // P
    NPG = w_pool_mix.shape[1]
    DPOOL = NPG * P
    DCONV = w_dw.shape[2]
    HEADS = DCONV // P
    TAPS = w_dw.shape[1]
    WINDOWS = [2 << g for g in range(NPG)]
    NG = w_coarse.shape[2]
    NE = w_fine.shape[2]
    EG = NE // NG
    NR = NG + NE
    FE = w_gate.shape[3]
    KF = FE // P
    KH = KC // 2
    BT = 64
    MAXB = 64
    IN_FLIGHT = 3
    SLOTS = 3
    ROUND = NG * SLOTS
    NG_TURN = ROUND // NG
    ALPHA = float((2 * DEPTH) ** 0.25)
    EPS = 1e-5
    BIG = 8192.0
    NPRM = TAPS + 4
    PAD = TAPS - 1
    WPAD = 16

    ctx = ExitStack()
    with ctx:
        RING = 16512
        GU = KC * 2 * FE * 4
        WD = KF * D * 4
        SLOT = GU + WD
        FIX = RING + SLOTS * SLOT

        def at(name, shape, dt, offset):
            return nc.alloc_sbuf_tensor_at(name, shape, dt, offset=offset)

        gu_w = [at(f"gu_w{s}", [P, KC, 2, FE], f32, RING + s * SLOT) for s in range(SLOTS)]
        wd_w = [at(f"wd_w{s}", [P, KF, D], f32, RING + s * SLOT + GU) for s in range(SLOTS)]

        top = [FIX]

        def fix(name, shape, dt=f32):
            size = 4
            for n in shape[1:]:
                size *= n
            a = at(name, shape, dt, top[0])
            top[0] += (size + 31) // 32 * 32
            return a

        xh = fix("xh", [P, TT, D])
        ident = fix("ident", [P, P])
        meanw = fix("meanw", [P, P])
        ones = fix("ones", [P, P])
        before = fix("before", [P, P])
        prm = fix("prm", [P, HEADS, NPRM])
        wr = fix("wr", [P, KC, NR])
        rbias = fix("rbias", [P, NR])
        io64 = fix("io64", [P, MAXB])
        iolo = fix("iolo", [P, P])
        tokA = fix("tokA", [P, 2, TT])
        tokB = fix("tokB", [P, 2, TT])
        halfv = fix("halfv", [P, 1])
        thr = fix("thr", [P, S // BT])
        rev4 = fix("rev4", [P, NG])
        rev8 = fix("rev8", [P, EG])
        rcnt = fix("rcnt", [P, WPAD])
        epsv = fix("epsv", [P, 1])
        onev = fix("onev", [P, NE])
        lg = fix("lg", [P, TT, NR])
        wts = fix("wts", [P, 2, TT])
        gtab = fix("gtab", [P, MAXB + 1], i32)
        stab = fix("stab", [P, MAXB], i32)
        bnd = fix("bnd", [P, NE + 1], i32)
        gidx = fix("gidx", [P, 1], i32)
        sidx = fix("sidx", [P, 1], i32)
        SCR = top[0]
        SCR_END = 229368

        xTh = at("xTh", [P, KC, S], f32r, RING)
        xTl = at("xTl", [P, KC, S], f32r, RING + SLOT)
        mixT = at("mixT", [P, KC, S], f32, RING + 2 * SLOT)
        P0, P1, P2 = (RING + s * SLOT + GU for s in range(SLOTS))
        wch = [at(f"wch{j}", [P, KC, P], f32r, P0 + j * 4096) for j in range(3)]
        wcl = [at(f"wcl{j}", [P, KC, P], f32r, (P0 + 3 * 4096, P1, P1 + 4096)[j]) for j in range(3)]
        win2 = at("win2", [P, S], f32, P1 + 8192)
        win3 = at("win3", [P, S], f32, P1 + 12288)
        wcs = [at(f"wcs{j}", [P, KC, P], f32, P2 + j * 4096) for j in range(3)]
        yv = at("yv", [P, S], f32, FIX + 4 * 4096)
        sqr = at("sqr", [P, TT, P], f32, FIX + 5 * 4096)
        diag = at("diag", [P, TT, P], f32, FIX + 6 * 4096)
        wmix = at("wmix", [P, NPG, P], f32, P2 + 12288)
        rows = at("rows", [NPRM, DCONV], f32, P2 + 12288 + 2048)
        scr = [SCR]

        def scratch(name, shape, dt=f32):
            size = 4
            for n in shape[1:]:
                size *= n
            a = at(name, shape, dt, scr[0])
            scr[0] += (size + 31) // 32 * 32
            if scr[0] > SCR_END:
                raise ValueError(name)
            return a

        uT = scratch("uT", [P, PAD + S])
        acc0 = scratch("acc0", [P, S])
        acc1 = scratch("acc1", [P, S])
        sig1 = scratch("sig1", [P, S])
        upT = scratch("upT", [P, WPAD + S])
        cur = [scratch(f"cur{b}", [P, NPRM]) for b in range(2)]
        csd = scratch("csd", [P, TT])
        crs = scratch("crs", [P, TT])

        woh = at("woh", [P, KC, D], f32r, RING)
        wol = at("wol", [P, KC, D], f32r, RING + SLOT)
        wos = [at(f"wos{b}", [P, D], f32, P2 + b * 4096) for b in range(2)]
        hb = [at(f"hb{b}", [P, D], f32, P2 + b * 4096) for b in range(2)]
        g1 = at("g1", [P, D], f32, P2 + 8192)
        b1 = at("b1", [P, D], f32, P2 + 12288)
        scr[0] = SCR
        mh = [scratch(f"mh{b}", [P, KC, P], f32r) for b in range(2)]
        ml = [scratch(f"ml{b}", [P, KC, P], f32r) for b in range(2)]
        hTt = scratch("hTt", [P, KC, P])
        vt1 = scratch("vt1", [P, D])
        turn1 = scratch("turn1", [P, 1])
        st1 = scratch("st1", [P, 2, 6])
        mv1 = scratch("mv1", [P, 2])
        sd1 = scratch("sd1", [P, 2])

        scr[0] = SCR
        hblk = scratch("hblk", [P, D // 2])
        hTb = scratch("hTb", [P, KC // 2, 2, BT])
        sg = scratch("sg", [P, FE // 2])
        gact = scratch("gact", [P, FE // 2])
        aT = scratch("aT", [P, KF // 2, 2, BT])
        yb = scratch("yb", [P, D // 2])
        RSCR = scr[0]
        onehot = scratch("onehot", [P, 2, TT, EG, NG])
        gsel = scratch("gsel", [P, TT, NG, EG])
        both = at("both", [P, TT, NE], f32, scr[0] - TT * NE * 4)
        base = scratch("base", [P, TT, NE])
        ohhi = scratch("ohhi", [P, 2 * TT, MAXB])
        ohlo = at("ohlo", [P, 2 * TT, P], f32, P2)
        ohab = at("ohab", [P, 2 * TT, 2, MAXB], f32, P2 + 8192)
        small = [RSCR + 2048 + 1024 + 1024 + 4096]

        def tiny(name, shape, dt=f32):
            size = 4
            for n in shape[1:]:
                size *= n
            a = at(name, shape, dt, small[0])
            small[0] += (size + 31) // 32 * 32
            return a

        cm = tiny("cm", [P, TT])
        cd = tiny("cd", [P, TT, NG])
        ce = tiny("ce", [P, TT, NG])
        cs = tiny("cs", [P, TT])
        ohg = tiny("ohg", [P, TT, NG])
        sel = tiny("sel", [P, TT, EG])
        sel2 = tiny("sel2", [P, TT, EG])
        oh12 = tiny("oh12", [P, 2, TT, EG])
        m2 = tiny("m2", [P, TT])
        ex = tiny("ex", [P, TT])
        tpre = tiny("tpre", [P, TT + 1, NE])
        nbf = tiny("nbf", [P, NE])
        incl = tiny("incl", [P, NE])
        cmp16 = tiny("cmp16", [P, NE, S // BT])
        posf = tiny("posf", [P, 2 * TT])
        posi = tiny("posi", [P, 2 * TT], i32)
        hif = tiny("hif", [P, 2 * TT])

        wgr = at("wgr", [P, KC, D], f32, RING + 2 * SLOT)
        wpr = at("wpr", [P, KP, D], f32, RING + 2 * SLOT + GU)
        wgl = at("wgl", [P, KC, D], f32r, RING + 2 * SLOT)
        wpl = at("wpl", [P, KP, D], f32r, RING + 2 * SLOT + GU)
        wph = at("wph", [P, KP, D], f32r, RING + 2 * SLOT + GU + KP * D * 4)
        wgh = at("wgh", [P, KC, D], f32r, RING)
        yp = [at(f"yp{b}", [P, 2, D], f32, RING + GU + b * 8192) for b in range(2)]
        yt = [at(f"yt{b}", [P, D], f32, RING + SLOT + b * 4096) for b in range(2)]
        yTh = [at(f"yTh{b}", [P, KC, P], f32r, RING + SLOT + 8192 + b * 4096) for b in range(2)]
        yTl = [at(f"yTl{b}", [P, KC, P], f32r, RING + SLOT + 16384 + b * 4096) for b in range(2)]
        sg3 = at("sg3", [P, D], f32, RING + SLOT + 24576)
        z3 = at("z3", [P, D], f32, RING + SLOT + 28672)
        ob = [at(f"ob{b}", [P, D], f32, RING + SLOT + 32768 + b * 4096) for b in range(2)]
        g2 = at("g2", [P, D], f32, RING + SLOT + 40960)
        b2 = at("b2", [P, D], f32, RING + SLOT + 45056)
        scr[0] = SCR
        g3 = scratch("g3", [P, D])
        b3 = scratch("b3", [P, D])
        pt = [scratch(f"pt{b}", [P, DP]) for b in range(2)]
        pTh = [scratch(f"pTh{b}", [P, KP, P], f32r) for b in range(2)]
        pTl = [scratch(f"pTl{b}", [P, KP, P], f32r) for b in range(2)]
        turn3 = scratch("turn3", [P, 1])
        st2 = scratch("st2", [P, 2, 6])
        mv2 = scratch("mv2", [P, 2])
        st3 = scratch("st3", [P, 2, 6])
        mv3 = scratch("mv3", [P, 2])
        sd3 = scratch("sd3", [P, 2])

        ps = ctx.enter_context(nc.psum_tensor("ps", [P, 8, 512], f32))

        def bank(b, n=1):
            return ps[:, b, :] if n == 1 else ps[:, b:b + n, :].rearrange("q b n -> q (b n)")

        h_dram = nc.dram_tensor("h_dram", [2 * S, D // 2], f32, kind="Internal").ap()
        y_dram = nc.dram_tensor("y_dram", [4 * S, D // 2], f32, kind="Internal").ap()

        def sem(name):
            return ctx.enter_context(nc.semaphore(name))

        x_in = [sem(f"x_in{c}") for c in range(TT // 2)]
        x_again = [sem(f"x_again{c}") for c in range(2)]
        rows_in = sem("rows_in")
        small_in = sem("small_in")
        wc_in = [sem(f"wc_in{j}") for j in range(3)]
        wch_ready = [sem(f"wch_ready{j}") for j in range(3)]
        wcl_ready = [sem(f"wcl_ready{j}") for j in range(3)]
        z_done = [sem(f"z_done{j}") for j in range(3)]
        consts = sem("consts")
        ident_ready = sem("ident_ready")
        pool_own = sem("pool_own")
        dve_own = sem("dve_own")
        act_own = sem("act_own")
        xt_done = sem("xt_done")
        xh_ready = sem("xh_ready")
        xl_ready = sem("xl_ready")
        rcnt_ready = sem("rcnt_ready")
        prm_done = sem("prm_done")
        prm_ready = sem("prm_ready")
        sig_ready = sem("sig_ready")
        u_ready = sem("u_ready")
        up_ready = sem("up_ready")
        pooled_ready = sem("pooled_ready")
        mix_done = sem("mix_done")
        mix_ready = sem("mix_ready")
        conv_step = sem("conv_step")
        conv_ready = sem("conv_ready")
        mean_done = sem("mean_done")
        dev_ready = sem("dev_ready")
        sq_ready = sem("sq_ready")
        var_done = sem("var_done")
        csd_ready = sem("csd_ready")
        yn_ready = sem("yn_ready")
        conv_out = sem("conv_out")
        wos_in = [sem(f"wos_in{b}") for b in range(2)]
        woh_ready = sem("woh_ready")
        wol_ready = sem("wol_ready")
        ln1_in = sem("ln1_in")
        mh_ready = sem("mh_ready")
        ml_ready = sem("ml_ready")
        op_done = sem("op_done")
        v1_ready = sem("v1_ready")
        var1_ready = sem("var1_ready")
        sd1_ready = sem("sd1_ready")
        h_ready = sem("h_ready")
        h_stored = [sem(f"h_stored{b}") for b in range(2)]
        h_kept = sem("h_kept")
        ht_done = sem("ht_done")
        ht_ready = sem("ht_ready")
        rt_done = sem("rt_done")
        lg_ready = sem("lg_ready")
        crs_ready = sem("crs_ready")
        diag_ready = sem("diag_ready")
        inv_done = sem("inv_done")
        ln1_own = sem("ln1_own")
        ln2_own = sem("ln2_own")
        ln3_own = sem("ln3_own")
        y2_own = sem("y2_own")
        cd_ready = sem("cd_ready")
        ce_ready = sem("ce_ready")
        m2_ready = sem("m2_ready")
        ex_ready = sem("ex_ready")
        oneh_ready = sem("oneh_ready")
        rank_done = sem("rank_done")
        oh_ready = sem("oh_ready")
        tab_done = sem("tab_done")
        tab_ready = sem("tab_ready")
        part_in = [[sem(f"part_in{s}_{m}") for m in range(6)] for s in range(SLOTS)]
        gath = sem("gath")
        gidx_ready = sem("gidx_ready")
        sidx_ready = sem("sidx_ready")
        hbt_done = sem("hbt_done")
        hbt_ready = sem("hbt_ready")
        gu_done = sem("gu_done")
        silu_ready = sem("silu_ready")
        gact_ready = sem("gact_ready")
        at_done = sem("at_done")
        at_ready = sem("at_ready")
        down_done = sem("down_done")
        y_ready = sem("y_ready")
        scat = sem("scat")
        ple_in = sem("ple_in")
        wgh_ready = sem("wgh_ready")
        wgl_ready = sem("wgl_ready")
        ln23_in = sem("ln23_in")
        yp_in = [sem(f"yp_in{b}") for b in range(2)]
        pt_in = [sem(f"pt_in{b}") for b in range(2)]
        v2_ready = sem("v2_ready")
        var2_ready = sem("var2_ready")
        sd2_ready = sem("sd2_ready")
        y2_ready = sem("y2_ready")
        y_kept = sem("y_kept")
        yt_done = sem("yt_done")
        yth_ready = sem("yth_ready")
        ytl_ready = sem("ytl_ready")
        gate_done = sem("gate_done")
        ple_done = sem("ple_done")
        n3_ready = sem("n3_ready")
        m3_ready = sem("m3_ready")
        sig3_ready = sem("sig3_ready")
        z3_ready = sem("z3_ready")
        var3_ready = sem("var3_ready")
        sd3_ready = sem("sd3_ready")
        o_ready = sem("o_ready")
        o_stored = [sem(f"o_stored{b}") for b in range(2)]

        block = ctx.enter_context(nc.Block())

        def passes(dst, ah, al, bh, bl, first, last):
            nc.tensor.matmul(dst, ah, bh, start=first, stop=False)
            nc.tensor.matmul(dst, ah, bl, start=False, stop=False)
            return nc.tensor.matmul(dst, al, bh, start=False, stop=last)

        def pairs(eng, body, lead=1):
            for t in range(2 * lead):
                body(t, t % 2, t)
            with eng.Fori(lead, TT // 2 - 1) as i:
                body(2 * i, 0, 2 * lead)
                body(2 * i + 1, 1, 2 * lead + 1)
            for t in range(TT - 2, TT):
                body(t, t % 2, t)

        def tile_cols(t):
            return bass.ds(t * P, P)

        def chunk_col(j, i):
            return (DPOOL, DPOOL + DCONV, 0)[j] + i * P

        def bc_row(v):
            return v.rearrange("a n -> (a n)").rearrange("(o n) -> o n", o=1).broadcast_to([P, v.shape[1]])

        @block.sync
        def _(sp):
            w_in_v = w_in[0].rearrange("(k q) n -> q k n", q=P)

            def chunk(j, i):
                sp.dma_start(wcs[j][:, :, :], w_in_v[:, :, bass.ds(chunk_col(j, i), P)]).then_inc(wc_in[j], 16)

            x_v = x[0].rearrange("(t q) d -> q t d", q=P)

            def load_x(c, done):
                sp.dma_start(xh[:, 2 * c:2 * c + 2, :], x_v[:, 2 * c:2 * c + 2, :]).then_inc(done, 16)

            load_x(0, x_in[0])
            load_x(1, x_in[1])
            chunk(0, 0)
            chunk(1, 0)
            load_x(2, x_in[2])
            load_x(3, x_in[3])
            chunk(2, 0)
            for i in range(1, HEADS):
                for j in range(3):
                    sp.wait_ge(wcl_ready[j], i)
                    chunk(j, i)
            sp.wait_ge(wcl_ready[2], HEADS)
            for k in range(KC):
                if k >= 2:
                    sp.wait_ge(wol_ready, k - 1)
                sp.dma_start(wos[k % 2][:, :], w_out[0, k * P:(k + 1) * P, :]).then_inc(wos_in[k % 2], 16)
            sp.wait_ge(mix_done, 2 * NPG)
            sp.dma_start(g1[:, :], bc_row(ln1_g)).then_inc(ln1_in, 16)
            sp.dma_start(b1[:, :], bc_row(ln1_b)).then_inc(ln1_in, 16)
            sp.dma_start(xh[:, 0:TT // 2, :], x_v[:, 0:TT // 2, :]).then_inc(x_again[0], 16)

            wg_v = w_gate[0].rearrange("(g e) (k q) f -> e g q k f", g=NG, q=P)
            wu_v = w_up[0].rearrange("(g e) (k q) f -> e g q k f", g=NG, q=P)
            wd_v = w_down[0].rearrange("(g e) (k q) d -> e g q k d", g=NG, q=P)

            def piece(v, s, m, turn=0):
                e, g = NG_TURN * turn + v // NG, v % NG
                if m < 4:
                    src = (wg_v, wu_v)[m % 2]
                    ks = slice(m // 2 * KH, (m // 2 + 1) * KH)
                    dst = gu_w[s][:, ks, m % 2, :]
                else:
                    src = wd_v
                    ks = slice((m - 4) * KF // 2, (m - 3) * KF // 2)
                    dst = wd_w[s][:, ks, :]
                sp.dma_start(dst, src[bass.ds(e, 1), g, :, ks, :].rearrange("a q k n -> (a q) k n"))\
                  .then_inc(part_in[s][m], 16)

            sp.wait_ge(conv_out, HEADS)
            sp.dma_start(xh[:, TT // 2:TT, :], x_v[:, TT // 2:TT, :]).then_inc(x_again[1], 16)
            for v in range(SLOTS - 1):
                for m in (4, 5):
                    piece(v, v, m)
            h_rows = h_dram.rearrange("(t q c) n -> t q (c n)", q=P, c=2)

            def store_h(t, b, at_least):
                if at_least == TT - 1:
                    sp.wait_ge(mh_ready, TT)
                    sp.wait_ge(ml_ready, TT)
                    for m in range(4):
                        piece(SLOTS - 1, SLOTS - 1, m)
                    sp.wait_ge(op_done, TT)
                    for m in range(4):
                        piece(0, 0, m)
                sp.wait_ge(h_ready, t + 1)
                sp.dma_start(h_rows[bass.ds(t, 1), :, :].rearrange("a q n -> (a q) n"), hb[b][:, :]).then_inc(h_stored[b], 16)

            pairs(sp, store_h)
            for m in range(4):
                piece(1, 1, m)
            sp.wait_ge(tab_ready, 1)
            sp.wait_ge(hbt_done, 1)
            for m in (4, 5):
                piece(SLOTS - 1, SLOTS - 1, m)

            def next_expert(v, turn):
                s, r = v % SLOTS, ROUND // SLOTS * turn + v // SLOTS
                sp_end = sp.value_load(bnd[0:1, bass.ds(ROUND * turn + v - (SLOTS - 1), 1)], min_val=1, max_val=MAXB)
                for m in range(6):
                    if m == 0:
                        sp.wait_ge(gu_done, sp_end)
                    if m == 4:
                        sp.wait_ge(down_done, sp_end)
                    if m >= IN_FLIGHT:
                        sp.wait_ge(part_in[s][m - IN_FLIGHT], 16 * (r + 1))
                    elif s:
                        sp.wait_ge(part_in[s - 1][m + 6 - IN_FLIGHT], 16 * (r + 1))
                    else:
                        sp.wait_ge(part_in[SLOTS - 1][m + 6 - IN_FLIGHT], 16 * r)
                    piece(v, s, m, turn)

            with sp.Fori(0, (NE - SLOTS) // ROUND) as turn:
                for v in range(SLOTS, SLOTS + ROUND):
                    next_expert(v, turn)
            for v in range(SLOTS + (NE - SLOTS) // ROUND * ROUND, NE):
                next_expert(v, 0)

            last2 = (NE - 1) // SLOTS * SLOTS - 1
            sp_end = sp.value_load(bnd[0:1, last2 + 1:last2 + 2], min_val=1, max_val=MAXB - 1)
            sp.wait_ge(down_done, sp_end)
            wpg_v = w_ple_gate[0].rearrange("(k q) n -> q k n", q=P)
            for c in range(KC // 2):
                if c:
                    sp.wait_ge(ple_in, 16 * c)
                sp.dma_start(wgr[:, 2 * c:2 * c + 2, :], wpg_v[:, 2 * c:2 * c + 2, :]).then_inc(ple_in, 16)
            sp.dma_start(wpr[:, :, :], w_ple_proj[0].rearrange("(k q) n -> q k n", q=P)).then_inc(ple_in, 16)
            sp_all = sp.value_load(bnd[0:1, NE:NE + 1], min_val=NE, max_val=MAXB - 1)
            sp.wait_ge(down_done, sp_all)
            for v, dst in ((ln2_g, g2), (ln2_b, b2)):
                sp.dma_start(dst[:, :], bc_row(v)).then_inc(ln23_in, 16)
            y_rows = y_dram.rearrange("(t q c) n -> t q (c n)", q=P, c=4)
            p_rows = p[0].rearrange("a (t q) n -> (a t) q n", q=P)
            out_rows = out.rearrange("a (t q) n -> (a t) q n", q=P)

            def load_tile(t, b):
                sp.dma_start(yp[b][:, :, :].rearrange("q c n -> q (c n)"),
                             y_rows[bass.ds(t, 1), :, :].rearrange("a q n -> (a q) n")).then_inc(yp_in[b], 16)
                sp.dma_start(pt[b][:, :], p_rows[bass.ds(t, 1), :, :].rearrange("a q n -> (a q) n")).then_inc(pt_in[b], 16)

            sp.wait_ge(scat, sp_all * 16)
            load_tile(0, 0)
            load_tile(1, 1)
            sp.wait_ge(gath, sp_all * 16 + 32)
            sp.wait_ge(wgl_ready, 1)
            for v, dst in ((ln3_g, g3), (ln3_b, b3)):
                sp.dma_start(dst[:, :], bc_row(v)).then_inc(ln23_in, 16)

            for t in range(2, 4):
                sp.wait_ge(v2_ready, t - 1)
                sp.wait_ge(yt_done, t - 1)
                load_tile(t, t % 2)
            for t in range(TT):
                if t + 4 < TT:
                    sp.wait_ge(v2_ready, t + 3)
                    sp.wait_ge(yt_done, t + 3)
                    load_tile(t + 4, t % 2)
                sp.wait_ge(o_ready, t + 1)
                sp.dma_start(out_rows[t, :, :], ob[t % 2][:, :]).then_inc(o_stored[t % 2], 16)
            sp.wait_ge(o_stored[0], 16 * TT // 2)
            sp.wait_ge(o_stored[1], 16 * TT // 2)

        @block.gpsimd
        def _(pool):
            n_own = [0]

            def own(ins):
                n_own[0] += 1
                ins.then_inc(pool_own, 1)
                pool.wait_ge(pool_own, n_own[0])

            own(nc.gpsimd.memset(ident[:, :], 0.0))
            nc.gpsimd.affine_select(out=ident[:, :], in_=ident[:, :], compare_op=ALU.not_equal, fill=1.0,
                                    base=0, pattern=[[-1, P]], channel_multiplier=1).then_inc(ident_ready, 1)
            for r, v in ((slice(0, TAPS), w_dw[0]), (slice(TAPS, TAPS + 1), b_dw), (slice(TAPS + 1, TAPS + 2), conv_ln_g),
                         (slice(TAPS + 2, TAPS + 3), conv_ln_b), (slice(TAPS + 3, TAPS + 4), pool_scale)):
                pool.dma_start(rows[r, :], v).then_inc(rows_in, 16)
            pool.dma_start(wmix[:, :, :], w_pool_mix[0].rearrange("g c d -> c g d")).then_inc(small_in, 16)
            pool.dma_start(wr[:, :, 0:NG], w_coarse[0].rearrange("(k q) n -> q k n", q=P)).then_inc(small_in, 16)
            pool.dma_start(wr[:, :, NG:NR], w_fine[0].rearrange("(k q) n -> q k n", q=P)).then_inc(small_in, 16)
            pool.dma_start(rbias[:, 0:NG], bc_row(b_coarse)).then_inc(small_in, 16)
            pool.dma_start(rbias[:, NG:NR], bc_row(b_fine)).then_inc(small_in, 16)

            own(nc.gpsimd.memset(ones[:, :], 1.0))
            own(nc.gpsimd.memset(meanw[:, :], 1.0 / P))
            own(nc.gpsimd.affine_select(out=before[:, :], in_=ones[:, :], compare_op=ALU.is_gt, fill=0.0,
                                        base=0, pattern=[[1, P]], channel_multiplier=-1))
            own(nc.gpsimd.memset(epsv[:, :], EPS))
            own(nc.gpsimd.memset(onev[:, :], 1.0))
            own(nc.gpsimd.memset(upT[:, 0:WPAD], 0.0))
            own(nc.gpsimd.memset(uT[:, 0:PAD], 0.0))

            def ramp(dst, pattern, base_, mult):
                nc.gpsimd.iota(dst, pattern, base=base_, channel_multiplier=mult,
                               allow_small_or_imprecise_dtypes=True)

            ramp(io64[:, :], [[1, MAXB]], 0, 0)
            ramp(iolo[:, :], [[0, 2], [1, BT]], 0, 0)
            ramp(tokA[:, :, :], [[0, 2], [2 * P, TT]], -int(BIG), 2)
            ramp(tokB[:, :, :], [[2, 2], [4 * P, TT]], -int(BIG), 4)
            ramp(thr[:, :], [[BT, S // BT]], 0, 0)
            ramp(rev4[:, :], [[-1, NG]], NG, 0)
            ramp(rev8[:, :], [[-1, EG]], EG, 0)
            ramp(rcnt[:, :], [[1, WPAD]], 1, 0)
            own(nc.gpsimd.memset(halfv[0:BT, :], BIG))
            own(nc.gpsimd.memset(halfv[BT:P, :], BIG + 1.0))
            own(nc.gpsimd.memset(thr[:, 0:1], -1.0))
            nc.gpsimd.memset(cur[0][:, 0:1], 0.0).then_inc(consts, 1)

            def low(j, i):
                pool.wait_ge(wch_ready[j], i + 1)
                nc.gpsimd.tensor_tensor(wcl[j][:, :, :], wcs[j][:, :, :], wch[j][:, :, :].bitcast(f32), SUB)\
                    .then_inc(wcl_ready[j], 1)

            def windows(g):
                pool.wait_ge(up_ready, 2 * (g + 1))
                src, pad = upT, WPAD
                w = 1
                dsts = [win2, win3]
                if g:
                    pool.wait_ge(mix_done, 2 * g)
                cur_sum, cur_pad = upT, WPAD
                n = 0
                while w < WINDOWS[g]:
                    dst = dsts[n % 2]
                    a = cur_sum[:, cur_pad + w:cur_pad + S]
                    b = cur_sum[:, cur_pad:cur_pad + S - w]
                    own(nc.gpsimd.tensor_tensor(dst[:, w:S], a, b, ADD))
                    own(nc.gpsimd.tensor_copy(dst[:, 0:w], cur_sum[:, cur_pad:cur_pad + w]))
                    cur_sum, cur_pad = dst, 0
                    w *= 2
                    n += 1
                pool.wait_ge(rcnt_ready, 1)
                W = WINDOWS[g]
                own(nc.gpsimd.tensor_tensor(cur_sum[:, 0:W], cur_sum[:, 0:W], rcnt[:, 0:W], MUL))
                own(nc.gpsimd.tensor_scalar(cur_sum[:, W:S], cur_sum[:, W:S], 1.0 / W, None, MUL))
                pooled = dsts[n % 2]
                nc.gpsimd.tensor_tensor(pooled[:, :], cur_sum[:, 0:S], upT[:, WPAD:WPAD + S], SUB).then_inc(pooled_ready, 1)

            for g in range(NPG):
                if g + 1 < HEADS:
                    for j in range(3):
                        low(j, g + 1)
                windows(g)

            for k in range(KC):
                pool.wait_ge(woh_ready, k + 1)
                nc.gpsimd.tensor_tensor(wol[:, k, :], wos[k % 2][:, :], woh[:, k, :].bitcast(f32), SUB).then_inc(wol_ready, 1)

            pool.wait_ge(tab_ready, 1)
            nc.gpsimd.memset(hblk[:, :], 0.0).then_inc(pool_own, 1)
            n_own[0] += 1
            pool.wait_ge(pool_own, n_own[0])

            bound = pool.alloc_register("bound")
            nil = pool.alloc_register("nil")
            pool.reg_mov(nil, 0)

            def gather(n):
                nc.gpsimd.tensor_copy(gidx[:, :], gtab[:, bass.ds(n, 1)]).then_inc(gidx_ready, 1)
                pool.wait_ge(gidx_ready, n + 1)
                pool.reg_alu(bound, nil, 2 * S - 1, ADD)
                nc.gpsimd.indirect_dma_start(
                    out=hblk[:, :], out_offset=None, in_=h_dram,
                    in_offset=bass.IndirectOffsetOnAxis(ap=gidx[:, 0:1], axis=0),
                    bounds_check=bound, oob_is_err=False).then_inc(gath, 16)

            def scatter(n, first=False):
                if not first:
                    pool.wait_ge(scat, n * 16)
                nc.gpsimd.tensor_copy(sidx[:, :], stab[:, bass.ds(n, 1)]).then_inc(sidx_ready, 1)
                pool.wait_ge(sidx_ready, n + 1)
                pool.wait_ge(y_ready, n + 1)
                pool.reg_alu(bound, nil, 4 * S - 1, ADD)
                nc.gpsimd.indirect_dma_start(
                    out=y_dram, out_offset=bass.IndirectOffsetOnAxis(ap=sidx[:, 0:1], axis=0),
                    in_=yb[:, :], in_offset=None,
                    bounds_check=bound, oob_is_err=False).then_inc(scat, 16)

            pool.wait_ge(h_stored[0], 16 * TT // 2)
            pool.wait_ge(h_stored[1], 16 * TT // 2)
            gather(0)
            n_blocks = pool.value_load(bnd[0:1, NE:NE + 1], min_val=NE, max_val=MAXB - 1)
            pool.wait_ge(hbt_done, 1)
            gather(1)
            pool.wait_ge(hbt_done, 2)
            gather(2)
            scatter(0, first=True)
            with pool.Fori(1, n_blocks) as n:
                pool.wait_ge(hbt_done, n + 2)
                gather(n + 2)
                scatter(n)
            pool.wait_ge(scat, n_blocks * 16)

            pool.wait_ge(ln23_in, 64)

            def scale_shift(t, b, _):
                pool.wait_ge(n3_ready, t + 1)
                nc.gpsimd.tensor_tensor(ob[b][:, :], ob[b][:, :], g3[:, :], MUL).then_inc(m3_ready, 1)
                pool.wait_ge(m3_ready, t + 1)
                nc.gpsimd.tensor_tensor(ob[b][:, :], ob[b][:, :], b3[:, :], ADD).then_inc(o_ready, 1)

            pairs(pool, scale_shift)

        @block.scalar
        def _(act):
            CP = ACT.Copy
            def high(j, i):
                act.wait_ge(wc_in[j], 16 * (i + 1))
                nc.scalar.activation(wch[j][:, :, :], wcs[j][:, :, :], CP).then_inc(wch_ready[j], 1)

            for t in range(TT):
                act.wait_ge(xt_done, t + 1)
                nc.scalar.activation(xTh[:, :, t * P:(t + 1) * P],
                                     bank(4 + 2 * (t % 2), 2).rearrange("q (k m) -> q k m", k=KC), CP).then_inc(xh_ready, 1)
                if t == 2:
                    high(0, 0)
                if t == 3:
                    high(1, 0)
            high(2, 0)

            def gate_sigmoid(i):
                for th in range(2):
                    act.wait_ge(z_done[1], 2 * i + th + 1)
                    if i:
                        act.wait_ge(u_ready, 2 * i)
                    nc.scalar.activation(sig1[:, th * HALF:(th + 1) * HALF], bank(2 + th), ACT.Sigmoid).then_inc(sig_ready, 1)

            def pool_input(i, th):
                act.wait_ge(z_done[2], 2 * i + th + 1)
                if i:
                    act.wait_ge(pooled_ready, i)
                nc.scalar.activation(upT[:, WPAD + th * HALF:WPAD + (th + 1) * HALF], bank(4 + th), CP).then_inc(up_ready, 1)

            def pool_output(i):
                for th in range(2):
                    act.wait_ge(mix_done, 2 * i + th + 1)
                    nc.scalar.activation(mixT[:, i, th * HALF:(th + 1) * HALF],
                                         bank(6 + th), CP, scale=prm[:, i, NPRM - 1:NPRM]).then_inc(mix_ready, 1)

            def head_square(i):
                act.wait_ge(dev_ready, i + 1)
                nc.scalar.activation(sqr[:, :, :].rearrange("q t m -> q (t m)"), yv[:, :], ACT.Square).then_inc(sq_ready, 1)

            def head_deviation(i):
                act.wait_ge(var_done, i + 1)
                nc.scalar.activation(csd[:, :], bank(6)[:, 0:TT], ACT.Sqrt, bias=epsv[:, :]).then_inc(csd_ready, 1)

            def head_swish(i):
                act.wait_ge(yn_ready, i + 1)
                nc.scalar.activation(mixT[:, i + NPG, :], yv[:, :], ACT.Silu,
                                     scale=cur[i % 2][:, TAPS + 1:TAPS + 2], bias=cur[i % 2][:, TAPS + 2:TAPS + 3]).then_inc(conv_out, 1)

            act.wait_ge(consts, 1)
            gate_sigmoid(0)
            high(0, 1)
            high(1, 1)
            pool_input(0, 0)
            pool_input(0, 1)
            high(2, 1)
            for i in range(1, HEADS):
                gate_sigmoid(i)
                if i < HEADS - 1:
                    high(0, i + 1)
                    high(1, i + 1)
                pool_output(i - 1)
                head_square(i - 1)
                pool_input(i, 0)
                head_deviation(i - 1)
                pool_input(i, 1)
                if i < HEADS - 1:
                    high(2, i + 1)
                head_swish(i - 1)
            def w_out_high(k):
                act.wait_ge(wos_in[k % 2], 16 * (k // 2 + 1))
                nc.scalar.activation(woh[:, k, :], wos[k % 2][:, :], CP).then_inc(woh_ready, 1)

            act.wait_ge(z_done[2], 2 * HEADS)
            w_out_high(0)
            w_out_high(1)
            pool_output(HEADS - 1)
            w_out_high(2)
            w_out_high(3)
            head_square(HEADS - 1)
            w_out_high(4)
            head_deviation(HEADS - 1)
            for k in range(5, KC):
                w_out_high(k)
            head_swish(HEADS - 1)

            def split_mix(t, b):
                nc.scalar.activation(mh[b][:, :, :], mixT[:, :, tile_cols(t)], CP).then_inc(mh_ready, 1)

            def evac_ht(t, b):
                act.wait_ge(ht_done, t + 1)
                nc.scalar.activation(hTt[:, :, :], bank(4, 2).rearrange("q (k m) -> q k m", k=KC), CP).then_inc(ht_ready, 1)

            act.wait_ge(conv_out, HEADS)
            act.wait_ge(mix_ready, 2 * NPG)
            split_mix(0, 0)

            def proj_tile(t, b, at_least):
                if at_least < TT - 1:
                    if at_least >= 1:
                        act.wait_ge(op_done, t)
                    split_mix(t + 1, 1 - b)
                if at_least >= 1:
                    evac_ht(t - 1, 1 - b)
                act.wait_ge(var1_ready, t + 1)
                nc.scalar.activation(sd1[:, 0:1], mv1[:, 1:2], ACT.Sqrt, bias=epsv[:, :]).then_inc(sd1_ready, 1)
                act.wait_ge(h_ready, t + 1)
                nc.scalar.activation(xh[:, bass.ds(t, 1), :].rearrange("q a n -> q (a n)"), hb[b][:, :], CP, scale=ALPHA).then_inc(h_kept, 1)

            pairs(act, proj_tile)
            evac_ht(TT - 1, 1)

            act.wait_ge(cd_ready, 1)
            nc.scalar.activation(ce[:, :, :], cd[:, :, :], ACT.Exp).then_inc(ce_ready, 1)
            act.wait_ge(m2_ready, 1)
            nc.scalar.activation(ex[:, :], m2[:, :], ACT.Exp).then_inc(ex_ready, 1)

            act.wait_ge(tab_ready, 1)
            act_blocks = act.value_load(bnd[0:1, NE:NE + 1], min_val=NE, max_val=MAXB - 1)

            def act_block(n, first=False):
                act.wait_ge(gu_done, n + 1)
                nc.scalar.activation(sg[:, :], bank(0)[:, 0:FE // 2], ACT.Silu).then_inc(silu_ready, 1)
                act.wait_ge(at_done, n + 1)
                nc.scalar.activation(aT[:, :, :, :].rearrange("q c h m -> q (c h m)"), bank(2)[:, 0:FE // 2], CP).then_inc(at_ready, 1)
                act.wait_ge(down_done, n + 1)
                if not first:
                    act.wait_ge(scat, n * 16)
                nc.scalar.activation(yb[:, :], bank(3), CP).then_inc(y_ready, 1)

            act_block(0, first=True)
            with act.Fori(1, act_blocks) as n:
                act_block(n)

            act.wait_ge(ple_in, 16 * (KC // 2 + 1))
            act.wait_ge(down_done, act_blocks)
            for k in range(KP):
                nc.scalar.activation(wph[:, k, :], wpr[:, k, :], CP).then_inc(wgh_ready, 1)
            for k in range(KC):
                nc.scalar.activation(wgh[:, k, :], wgr[:, k, :], CP).then_inc(wgh_ready, 1)

            def finish_tile(t, first=False):
                for c in range(2):
                    act.wait_ge(gate_done, 2 * t + c + 1)
                    if not first:
                        act.wait_ge(z3_ready, t)
                    nc.scalar.activation(sg3[:, c * 512:(c + 1) * 512], bank(3 + c), ACT.Sigmoid).then_inc(sig3_ready, 1)
                act.wait_ge(var3_ready, t + 1)
                nc.scalar.activation(sd3[:, 0:1], mv3[:, 1:2], ACT.Sqrt, bias=epsv[:, :]).then_inc(sd3_ready, 1)

            def deviation2(t):
                act.wait_ge(var2_ready, t + 1)
                nc.scalar.activation(sd3[:, 1:2], mv2[:, 1:2], ACT.Sqrt, bias=epsv[:, :]).then_inc(sd2_ready, 1)

            def last_tile(t, b, at_least):
                act.wait_ge(y2_ready, t + 1)
                nc.scalar.activation(xh[:, bass.ds(t, 1), :].rearrange("q a n -> q (a n)"), yt[b][:, :], CP, scale=ALPHA).then_inc(y_kept, 1)
                act.wait_ge(yt_done, t + 1)
                nc.scalar.activation(pTh[b][:, :, :], bank(2)[:, 0:DP].rearrange("q (k m) -> q k m", k=KP), CP)
                nc.scalar.activation(yTh[b][:, :, :], bank(0, 2).rearrange("q (k m) -> q k m", k=KC), CP).then_inc(yth_ready, 1)
                if at_least < TT - 1:
                    deviation2(t + 1)
                if at_least >= 1:
                    finish_tile(t - 1, first=(at_least == 1))

            deviation2(0)
            pairs(act, last_tile)
            finish_tile(TT - 1)

        @block.vector
        def _(dve):
            V = nc.vector
            n_own = [0]

            def own(ins):
                n_own[0] += 1
                ins.then_inc(dve_own, 1)
                dve.wait_ge(dve_own, n_own[0])

            def low(j):
                dve.wait_ge(wch_ready[j], 1)
                V.tensor_tensor(wcl[j][:, :, :], wcs[j][:, :, :], wch[j][:, :, :].bitcast(f32), SUB).then_inc(wcl_ready[j], 1)

            for t in range(TT):
                dve.wait_ge(xh_ready, t + 1)
                cols = slice(t * P, (t + 1) * P)
                V.tensor_tensor(xTl[:, :, cols], bank(4 + 2 * (t % 2), 2).rearrange("q (k m) -> q k m", k=KC),
                                xTh[:, :, cols].bitcast(f32), SUB).then_inc(xl_ready, 1)
                if t == TT // 2 - 1:
                    low(0)
                    low(1)
            low(2)
            dve.wait_ge(prm_done, 1)
            V.tensor_copy(prm[:, :, :].rearrange("q h n -> q (h n)"), bank(7)[:, 0:HEADS * NPRM]).then_inc(prm_ready, 1)
            dve.wait_ge(prm_ready, 1)
            dve.wait_ge(consts, 1)
            V.reciprocal(rcnt[:, :], rcnt[:, :]).then_inc(rcnt_ready, 1)
            NSTEP = TAPS + 1

            def deviation(i):
                dve.wait_ge(mean_done, 2 * (i + 1))
                V.tensor_tensor(yv[:, :], yv[:, :], bank(6, 2), SUB).then_inc(dev_ready, 1)

            def inverse(i):
                dve.wait_ge(csd_ready, i + 1)
                V.reciprocal(crs[:, :], csd[:, :]).then_inc(crs_ready, 1)
                dve.wait_ge(crs_ready, i + 1)
                V.tensor_tensor(diag[:, :, :], ident[:, :].unsqueeze(1).broadcast_to([P, TT, P]),
                                crs[:, :].unsqueeze(2).broadcast_to([P, TT, P]), MUL).then_inc(diag_ready, 1)

            def normalise(i):
                dve.wait_ge(inv_done, 2 * (i + 1))
                V.tensor_tensor(yv[:, :], yv[:, :], bank(6, 2), MUL).then_inc(yn_ready, 1)

            def conv_head(i):
                b = i % 2
                c = cur[b]
                if i >= 2:
                    dve.wait_ge(conv_out, i - 1)
                V.tensor_copy(c[:, :], prm[:, i, :]).then_inc(conv_step, 1)
                for th in range(2):
                    dve.wait_ge(sig_ready, 2 * i + th + 1)
                    dve.wait_ge(z_done[0], 2 * i + th + 1)
                    cols = slice(th * HALF, (th + 1) * HALF)
                    V.tensor_tensor(uT[:, PAD + th * HALF:PAD + (th + 1) * HALF], bank(th), sig1[:, cols], MUL).then_inc(u_ready, 1)
                dve.wait_ge(u_ready, 2 * (i + 1))
                dve.wait_ge(conv_step, i * NSTEP + 1)
                if i:
                    dve.wait_ge(conv_ready, i)
                V.tensor_scalar(acc0[:, :], uT[:, 0:S], c[:, 0:1], c[:, TAPS:TAPS + 1], MUL, ADD).then_inc(conv_step, 1)
                V.tensor_scalar(acc1[:, :], uT[:, 1:1 + S], c[:, 1:2], None, MUL).then_inc(conv_step, 1)
                for j in range(2, TAPS):
                    if i and j == NORM_AT[0]:
                        deviation(i - 1)
                    if i and j == NORM_AT[1]:
                        inverse(i - 1)
                    if i and j == NORM_AT[2]:
                        normalise(i - 1)
                    acc = (acc0, acc1)[j % 2]
                    dve.wait_ge(conv_step, i * NSTEP + j)
                    V.scalar_tensor_tensor(acc[:, :], uT[:, j:j + S], c[:, j:j + 1], acc[:, :], MUL, ADD).then_inc(conv_step, 1)
                dve.wait_ge(conv_step, (i + 1) * NSTEP)
                if i:
                    dve.wait_ge(conv_out, i)
                V.tensor_tensor(yv[:, :], acc0[:, :], acc1[:, :], ADD).then_inc(conv_ready, 1)

            NORM_AT = (6, 14, 22)
            for i in range(HEADS):
                conv_head(i)
            deviation(HEADS - 1)
            inverse(HEADS - 1)
            normalise(HEADS - 1)

            def split_mix(t, b):
                dve.wait_ge(mh_ready, t + 1)
                V.tensor_tensor(ml[b][:, :, :], mixT[:, :, tile_cols(t)], mh[b][:, :, :].bitcast(f32), SUB).then_inc(ml_ready, 1)

            def logits(t, b):
                dve.wait_ge(rt_done, t + 1)
                V.tensor_tensor(lg[:, bass.ds(t, 1), :].rearrange("q a n -> q (a n)"), bank(6 + b)[:, 0:NR], rbias[:, :], ADD).then_inc(lg_ready, 1)

            dve.wait_ge(ln1_in, 32)
            dve.wait_ge(small_in, 80)
            split_mix(0, 0)
            for c in range(2):
                dve.wait_ge(x_again[c], 16)
            LN1 = 5

            def proj_tile(t, b, at_least):
                xt = xh[:, bass.ds(t, 1), :].rearrange("q a n -> q (a n)")
                if at_least >= 1:
                    dve.wait_ge(h_ready, t)
                if at_least < TT - 1:
                    if at_least >= 1:
                        dve.wait_ge(op_done, t)
                    split_mix(t + 1, 1 - b)
                dve.wait_ge(op_done, t + 1)
                V.scalar_tensor_tensor(vt1[:, :], xt, ALPHA, bank(2 * b, 2), MUL, ADD).then_inc(v1_ready, 1)
                dve.wait_ge(v1_ready, t + 1)
                n = t * LN1
                for c in range(2):
                    V.bn_stats(st1[:, c, :], vt1[:, c * 512:(c + 1) * 512]).then_inc(ln1_own, 1)
                dve.wait_ge(ln1_own, n + 2)
                V.memset(turn1[:, :], 0.0)
                V.bn_aggr(mv1[:, :], st1[:, :, :].rearrange("q c s -> q (c s)")).then_inc(var1_ready, 1)
                dve.wait_ge(sd1_ready, t + 1)
                V.reciprocal(sd1[:, 1:2], sd1[:, 0:1]).then_inc(ln1_own, 1)
                dve.wait_ge(ln1_own, n + 3)
                dve.wait_ge(var1_ready, t + 1)
                V.tensor_scalar(vt1[:, :], vt1[:, :], mv1[:, 0:1], sd1[:, 1:2], SUB, MUL).then_inc(ln1_own, 1)
                dve.wait_ge(ln1_own, n + 4)
                V.tensor_tensor(vt1[:, :], vt1[:, :], g1[:, :], MUL).then_inc(ln1_own, 1)
                dve.wait_ge(ln1_own, n + 5)
                if at_least >= 2:
                    dve.wait_ge(h_stored[b], (t - b) * 8)
                    dve.wait_ge(h_kept, t - 1)
                    dve.wait_ge(ht_done, t - 1)
                V.tensor_tensor(hb[b][:, :], vt1[:, :], b1[:, :], ADD).then_inc(h_ready, 1)
                if at_least >= 2:
                    logits(t - 2, b)

            pairs(dve, proj_tile)
            logits(TT - 2, 0)
            logits(TT - 1, 1)

            dve.wait_ge(lg_ready, TT)
            coarse = lg[:, :, 0:NG]
            fine = lg[:, :, NG:NR].rearrange("q t (g e) -> q t g e", g=NG)

            def over(a, *shape):
                return a.broadcast_to([P, *shape])

            own(V.tensor_reduce(cm[:, :], coarse, op=ALU.max, axis=AX.X))
            V.tensor_tensor(cd[:, :, :], coarse, over(cm[:, :].unsqueeze(2), TT, NG), SUB).then_inc(cd_ready, 1)
            dve.wait_ge(cd_ready, 1)
            own(V.tensor_scalar(ohg[:, :, :], cd[:, :, :], 0.0, None, ALU.is_ge))
            own(V.tensor_tensor(ohg[:, :, :], ohg[:, :, :], over(rev4[:, :].unsqueeze(1), TT, NG), MUL))
            own(V.tensor_reduce(cm[:, :], ohg[:, :, :], op=ALU.max, axis=AX.X))
            own(V.tensor_tensor(ohg[:, :, :], over(rev4[:, :].unsqueeze(1), TT, NG), over(cm[:, :].unsqueeze(2), TT, NG), ALU.is_equal))
            own(V.tensor_tensor(gsel[:, :, :, :], fine, over(ohg[:, :, :].unsqueeze(3), TT, NG, EG), MUL))
            own(V.tensor_reduce(sel[:, :, :], gsel[:, :, :, :].rearrange("q t g e -> q t e g"), op=ADD, axis=AX.X))
            own(V.tensor_reduce(cm[:, :], sel[:, :, :], op=ALU.max, axis=AX.X))
            own(V.tensor_tensor(sel[:, :, :], sel[:, :, :], over(cm[:, :].unsqueeze(2), TT, EG), SUB))

            def first_max(src, limit, dst):
                own(V.tensor_tensor(dst, src, limit, ALU.is_ge))
                own(V.tensor_tensor(dst, dst, over(rev8[:, :].unsqueeze(1), TT, EG), MUL))
                own(V.tensor_reduce(cm[:, :], dst, op=ALU.max, axis=AX.X))
                own(V.tensor_tensor(dst, over(rev8[:, :].unsqueeze(1), TT, EG), over(cm[:, :].unsqueeze(2), TT, EG), ALU.is_equal))

            own(V.memset(m2[:, :], 0.0))
            first_max(sel[:, :, :], over(m2[:, :].unsqueeze(2), TT, EG), oh12[:, 0, :, :])
            own(V.scalar_tensor_tensor(sel2[:, :, :], oh12[:, 0, :, :], -1e30, sel[:, :, :], MUL, ADD))
            V.tensor_reduce(m2[:, :], sel2[:, :, :], op=ALU.max, axis=AX.X).then_inc(m2_ready, 1)
            dve.wait_ge(m2_ready, 1)
            first_max(sel2[:, :, :], over(m2[:, :].unsqueeze(2), TT, EG), oh12[:, 1, :, :])
            for k in range(2):
                own(V.tensor_tensor(onehot[:, k, :, :, :], over(ohg[:, :, :].unsqueeze(2), TT, EG, NG),
                                    over(oh12[:, k, :, :].unsqueeze(3), TT, EG, NG), MUL))
            V.tensor_tensor(both[:, :, :], onehot[:, 0, :, :, :].rearrange("q t e g -> q t (e g)"),
                            onehot[:, 1, :, :, :].rearrange("q t e g -> q t (e g)"), ADD).then_inc(oneh_ready, 1)
            dve.wait_ge(ce_ready, 1)
            own(V.tensor_reduce(cs[:, :], ce[:, :, :], op=ADD, axis=AX.X))
            dve.wait_ge(ex_ready, 1)
            own(V.scalar_tensor_tensor(cs[:, :], ex[:, :], 1.0, cs[:, :], ADD, MUL))
            own(V.reciprocal(wts[:, 0, :], cs[:, :]))
            own(V.tensor_tensor(wts[:, 1, :], wts[:, 0, :], ex[:, :], MUL))
            dve.wait_ge(rank_done, 1)
            tot = bank(1)[:, 0:TT * NE].rearrange("q (t e) -> q t e", t=TT)
            rank = bank(0)[:, 0:TT * NE].rearrange("q (t e) -> q t e", t=TT)
            own(V.memset(tpre[:, 0, :], 0.0))
            for t in range(TT):
                own(V.tensor_tensor(tpre[:, t + 1, :], tpre[:, t, :], tot[:, t, :], ADD))
            own(V.tensor_tensor(cmp16[:, :, :], over(tpre[:, TT, :].unsqueeze(2), NE, S // BT),
                                over(thr[:, :].unsqueeze(1), NE, S // BT), ALU.is_gt))
            own(V.tensor_reduce(nbf[:, :], cmp16[:, :, :], op=ADD, axis=AX.X))
            own(V.tensor_tensor_scan(incl[:, :], onev[:, :], nbf[:, :], 0.0, MUL, ADD))
            own(V.memset(bnd[:, 0:1], 0))
            own(V.tensor_copy(bnd[:, 1:NE + 1], incl[:, :]))
            own(V.tensor_tensor(nbf[:, :], incl[:, :], nbf[:, :], SUB))
            own(V.scalar_tensor_tensor(base[:, :, :], over(nbf[:, :].unsqueeze(1), TT, NE), float(BT), tpre[:, 0:TT, :], MUL, ADD))
            own(V.tensor_tensor(base[:, :, :], base[:, :, :], rank, ADD))
            for k in range(2):
                own(V.tensor_tensor(onehot[:, k, :, :, :].rearrange("q t e g -> q t (e g)"),
                                    onehot[:, k, :, :, :].rearrange("q t e g -> q t (e g)"), base[:, :, :], MUL))
                own(V.tensor_reduce(posf[:, k * TT:(k + 1) * TT], onehot[:, k, :, :, :].rearrange("q t e g -> q t (e g)"),
                                    op=ADD, axis=AX.X))
            own(V.tensor_copy(posi[:, :], posf[:, :]))
            own(V.tensor_scalar(posi[:, :], posi[:, :], 6, None, ALU.arith_shift_right))
            own(V.tensor_copy(hif[:, :], posi[:, :]))
            own(V.scalar_tensor_tensor(posf[:, :], hif[:, :], -float(BT), posf[:, :], MUL, ADD))
            for b in range(2):
                dve.wait_ge(h_stored[b], 16 * TT // 2)
            dve.wait_ge(h_kept, TT)
            own(V.tensor_tensor(ohlo[:, :, :], over(iolo[:, :].unsqueeze(1), 2 * TT, P), over(posf[:, :].unsqueeze(2), 2 * TT, P), ALU.is_equal))
            own(V.tensor_tensor(ohhi[:, :, :], over(io64[:, :].unsqueeze(1), 2 * TT, MAXB), over(hif[:, :].unsqueeze(2), 2 * TT, MAXB), ALU.is_equal))
            for c, tok in ((0, tokA), (1, tokB)):
                V.tensor_tensor(ohab[:, :, c, :], ohhi[:, :, :],
                                over(tok[:, :, :].rearrange("q k t -> q (k t)").unsqueeze(2), 2 * TT, MAXB), MUL).then_inc(oh_ready, 1)
            dve.wait_ge(tab_done, 1)
            own(V.memset(gtab[:, MAXB:MAXB + 1], int(BIG)))
            own(V.tensor_scalar(gtab[:, 0:MAXB], bank(0)[:, 0:MAXB], halfv[:, :], None, ADD))
            V.tensor_scalar(stab[:, :], bank(0)[:, MAXB:2 * MAXB], halfv[:, :], None, ADD).then_inc(tab_ready, 1)
            dve.wait_ge(tab_ready, 1)

            dve_blocks = dve.value_load(bnd[0:1, NE:NE + 1], min_val=NE, max_val=MAXB - 1)

            def h_block(n):
                dve.wait_ge(hbt_done, n)
                V.tensor_copy(hTb[:, :, :, :].rearrange("q c h m -> q (c h m)"), bank(1)).then_inc(hbt_ready, 1)

            h_block(1)
            with dve.Fori(0, dve_blocks) as n:
                dve.wait_ge(silu_ready, n + 1)
                V.tensor_tensor(gact[:, :], sg[:, :], bank(0)[:, FE // 2:FE], MUL).then_inc(gact_ready, 1)
                h_block(n + 2)

            for k in range(KP + KC):
                dve.wait_ge(wgh_ready, k + 1)
                if k < KP:
                    whole, hi, lo = wpr[:, k, :], wph[:, k, :], wpl[:, k, :]
                else:
                    whole, hi, lo = wgr[:, k - KP, :], wgh[:, k - KP, :], wgl[:, k - KP, :]
                V.tensor_tensor(lo, whole, hi.bitcast(f32), SUB).then_inc(wgl_ready, 1)
            dve.wait_ge(ln23_in, 64)

            def finish_tile(t, b, at_least):
                n = t * 4
                dve.wait_ge(sig3_ready, 2 * (t + 1))
                dve.wait_ge(ple_done, t + 1)
                if at_least >= 1:
                    dve.wait_ge(n3_ready, t)
                V.tensor_tensor(z3[:, :], sg3[:, :], bank(5, 2), MUL).then_inc(ln3_own, 1)
                dve.wait_ge(ln3_own, n + 1)
                dve.wait_ge(y_kept, t + 1)
                V.tensor_tensor(z3[:, :], xh[:, bass.ds(t, 1), :].rearrange("q a n -> q (a n)"), z3[:, :], ADD).then_inc(z3_ready, 1)
                dve.wait_ge(z3_ready, t + 1)
                for c in range(2):
                    V.bn_stats(st3[:, c, :], z3[:, c * 512:(c + 1) * 512]).then_inc(ln3_own, 1)
                dve.wait_ge(ln3_own, n + 3)
                V.memset(turn3[:, :], 0.0)
                V.bn_aggr(mv3[:, :], st3[:, :, :].rearrange("q c s -> q (c s)")).then_inc(var3_ready, 1)
                dve.wait_ge(sd3_ready, t + 1)
                dve.wait_ge(var3_ready, t + 1)
                V.reciprocal(sd3[:, 0:1], sd3[:, 0:1]).then_inc(ln3_own, 1)
                dve.wait_ge(ln3_own, n + 4)
                if at_least >= 2:
                    dve.wait_ge(o_stored[b], (t - b) * 8)
                V.tensor_scalar(ob[b][:, :], z3[:, :], mv3[:, 0:1], sd3[:, 0:1], SUB, MUL).then_inc(n3_ready, 1)

            def norm_tile(t, b, at_least):
                n = t * 5
                xt = xh[:, bass.ds(t, 1), :].rearrange("q a n -> q (a n)")
                dve.wait_ge(yp_in[b], (t - b) * 8 + 16)
                if at_least >= 2:
                    dve.wait_ge(y_kept, t - 1)
                    dve.wait_ge(yt_done, t - 1)
                V.scalar_tensor_tensor(xt, yp[b][:, 0, :], wts[:, 0, bass.ds(t, 1)], xt, MUL, ADD).then_inc(ln2_own, 1)
                dve.wait_ge(ln2_own, n + 1)
                V.scalar_tensor_tensor(yt[b][:, :], yp[b][:, 1, :], wts[:, 1, bass.ds(t, 1)], xt, MUL, ADD).then_inc(v2_ready, 1)
                dve.wait_ge(v2_ready, t + 1)
                for c in range(2):
                    V.bn_stats(st2[:, c, :], yt[b][:, c * 512:(c + 1) * 512]).then_inc(ln2_own, 1)
                dve.wait_ge(ln2_own, n + 3)
                V.memset(turn3[:, :], 0.0)
                V.bn_aggr(mv2[:, :], st2[:, :, :].rearrange("q c s -> q (c s)")).then_inc(var2_ready, 1)
                dve.wait_ge(sd2_ready, t + 1)
                dve.wait_ge(var2_ready, t + 1)
                V.reciprocal(sd3[:, 1:2], sd3[:, 1:2]).then_inc(ln2_own, 1)
                dve.wait_ge(ln2_own, n + 4)
                V.tensor_scalar(yt[b][:, :], yt[b][:, :], mv2[:, 0:1], sd3[:, 1:2], SUB, MUL).then_inc(ln2_own, 1)
                dve.wait_ge(ln2_own, n + 5)
                V.tensor_tensor(yt[b][:, :], yt[b][:, :], g2[:, :], MUL).then_inc(y2_own, 1)
                dve.wait_ge(y2_own, t + 1)
                V.tensor_tensor(yt[b][:, :], yt[b][:, :], b2[:, :], ADD).then_inc(y2_ready, 1)

            norm_tile(0, 0, 0)

            def last_tile(t, b, at_least):
                dve.wait_ge(yth_ready, t + 1)
                V.tensor_tensor(pTl[b][:, :, :], bank(2)[:, 0:DP].rearrange("q (k m) -> q k m", k=KP),
                                pTh[b][:, :, :].bitcast(f32), SUB)
                V.tensor_tensor(yTl[b][:, :, :], bank(0, 2).rearrange("q (k m) -> q k m", k=KC),
                                yTh[b][:, :, :].bitcast(f32), SUB).then_inc(ytl_ready, 1)
                if at_least < TT - 1:
                    norm_tile(t + 1, 1 - b, at_least + 1)
                if at_least >= 1:
                    finish_tile(t - 1, 1 - b, at_least - 1)

            pairs(dve, last_tile, lead=2)
            finish_tile(TT - 1, 1, TT - 1)

        @block.tensor
        def _(pe):
            T = nc.tensor
            pe.wait_ge(ident_ready, 1)
            def x_tile(t):
                if t % 2 == 0:
                    pe.wait_ge(x_in[t // 2], 16)
                if t >= 2:
                    pe.wait_ge(xl_ready, t - 1)
                for k in range(KC):
                    ins = T.transpose(ps[:, 4 + 2 * (t % 2) + k // 4, (k % 4) * P:(k % 4 + 1) * P], xh[:, t, k * P:(k + 1) * P], ident[:, :])
                ins.then_inc(xt_done, 1)

            def z_chunk(j, i, first=False, halves=(0, 1)):
                pe.wait_ge(wcl_ready[j], i + 1)
                if not first:
                    if j < 2:
                        pe.wait_ge(u_ready, 2 * i)
                    else:
                        pe.wait_ge(up_ready, 2 * i)
                for th in halves:
                    cols = slice(th * HALF, (th + 1) * HALF)
                    for k in range(KC):
                        ins = passes(bank(2 * j + th), wch[j][:, k, :], wcl[j][:, k, :], xTh[:, k, cols], xTl[:, k, cols], k == 0, k == KC - 1)
                    ins.then_inc(z_done[j], 1)

            def pool_mix(g):
                pooled = (win2, win3)[(g + 1) % 2]
                pe.wait_ge(pooled_ready, g + 1)
                if g:
                    pe.wait_ge(yn_ready, g)
                for th in range(2):
                    T.matmul(bank(6 + th), wmix[:, g, :], pooled[:, th * HALF:(th + 1) * HALF], start=True, stop=True).then_inc(mix_done, 1)

            def head_mean(i):
                pe.wait_ge(mix_ready, 2 * (i + 1))
                pe.wait_ge(conv_ready, i + 1)
                for th in range(2):
                    T.matmul(bank(6 + th), meanw[:, :], yv[:, th * HALF:(th + 1) * HALF], start=True, stop=True).then_inc(mean_done, 1)

            def head_variance(i):
                pe.wait_ge(sq_ready, i + 1)
                for t in range(TT):
                    ins = T.matmul(bank(6)[:, t:t + 1], sqr[:, t, :], meanw[:, 0:1], start=True, stop=True)
                ins.then_inc(var_done, 1)

            def head_inverse(i):
                pe.wait_ge(diag_ready, i + 1)
                for th in range(2):
                    T.matmul(bank(6 + th), ones[:, :], diag[:, th * TT // 2:(th + 1) * TT // 2, :].rearrange("q t m -> q (t m)"),
                             start=True, stop=True).then_inc(inv_done, 1)

            for t in range(TT // 2):
                x_tile(t)
            pe.wait_ge(xl_ready, TT // 2)
            z_chunk(0, 0, first=True, halves=(0,))
            z_chunk(1, 0, first=True, halves=(0,))
            for t in range(TT // 2, TT):
                x_tile(t)
            pe.wait_ge(xl_ready, TT)
            z_chunk(0, 0, first=True, halves=(1,))
            z_chunk(1, 0, first=True, halves=(1,))
            pe.wait_ge(rows_in, 80)
            for h in range(HEADS):
                ins = T.transpose(bank(7)[:, h * NPRM:(h + 1) * NPRM], rows[:, h * P:(h + 1) * P], ident[0:NPRM, 0:NPRM])
            ins.then_inc(prm_done, 1)
            z_chunk(2, 0, first=True)
            pe.wait_ge(small_in, 80)
            pe.wait_ge(consts, 1)
            pe.wait_ge(prm_ready, 1)
            for i in range(1, HEADS):
                z_chunk(0, i)
                z_chunk(1, i)
                pool_mix(i - 1)
                head_mean(i - 1)
                z_chunk(2, i, halves=(0,))
                head_variance(i - 1)
                z_chunk(2, i, halves=(1,))
                head_inverse(i - 1)
            pool_mix(HEADS - 1)
            head_mean(HEADS - 1)
            head_variance(HEADS - 1)
            head_inverse(HEADS - 1)

            pe.wait_ge(wol_ready, KC)
            pe.wait_ge(small_in, 80)

            def route(t, b):
                pe.wait_ge(h_ready, t + 1)
                for k in range(KC):
                    ins = T.transpose(ps[:, 4 + k // 4, (k % 4) * P:(k % 4 + 1) * P], hb[b][:, k * P:(k + 1) * P], ident[:, :])
                ins.then_inc(ht_done, 1)

            def route_mm(t, b):
                pe.wait_ge(ht_ready, t + 1)
                for k in range(KC):
                    ins = T.matmul(bank(6 + b)[:, 0:NR], hTt[:, k, :], wr[:, k, :], start=(k == 0), stop=(k == KC - 1))
                ins.then_inc(rt_done, 1)

            def proj_tile(t, b, at_least):
                pe.wait_ge(ml_ready, t + 1)
                if at_least >= 2:
                    pe.wait_ge(v1_ready, t - 1)
                for c in range(2):
                    if c and at_least >= 2:
                        route_mm(t - 2, b)
                    for k in range(KC):
                        ins = passes(bank(2 * b + c), mh[b][:, k, :], ml[b][:, k, :], woh[:, k, c * 512:(c + 1) * 512],
                                     wol[:, k, c * 512:(c + 1) * 512], k == 0, k == KC - 1)
                ins.then_inc(op_done, 1)
                if at_least >= 1:
                    route(t - 1, 1 - b)

            pairs(pe, proj_tile)
            pe.wait_ge(lg_ready, TT - 3)
            route_mm(TT - 2, 0)
            route(TT - 1, 1)
            pe.wait_ge(lg_ready, TT - 2)
            route_mm(TT - 1, 1)

            pe.wait_ge(oneh_ready, 1)
            M = both[:, :, :].rearrange("q t e -> q (t e)")
            T.matmul(bank(0)[:, 0:TT * NE], before[:, :], M, start=True, stop=True)
            T.matmul(bank(1)[:, 0:TT * NE], ones[:, :], M, start=True, stop=True).then_inc(rank_done, 1)
            pe.wait_ge(oh_ready, 2)
            for a in range(2 * TT):
                ins = T.matmul(bank(0)[:, 0:2 * MAXB], ohlo[:, a, :], ohab[:, a, :, :].rearrange("q c n -> q (c n)"),
                               start=(a == 0), stop=(a == 2 * TT - 1))
            ins.then_inc(tab_done, 1)
            pe.wait_ge(tab_ready, 1)

            def h_block(n):
                pe.wait_ge(gath, 16 * n)
                for c in range(KC // 2):
                    ins = T.transpose(bank(1)[:, c * P:(c + 1) * P], hblk[:, c * P:(c + 1) * P], ident[:, :])
                ins.then_inc(hbt_done, 1)

            def expert_block(n, s, r):
                pe.wait_ge(hbt_ready, n + 1)
                for k in range(KC):
                    if k % KH == 0:
                        for m in range(2):
                            pe.wait_ge(part_in[s][m + 2 * (k // KH)], 16 * (r + 1))
                    for j in range(2):
                        ins = T.matmul(ps[j * BT:(j + 1) * BT, 0, :].rearrange("q (c n) -> q c n", c=2),
                                       hTb[:, k % KH, k // KH, :], gu_w[s][:, k, :, j * (FE // 2):(j + 1) * (FE // 2)],
                                       start=(k == 0), stop=(k == KC - 1))
                ins.then_inc(gu_done, 1)
                h_block(n + 2)
                pe.wait_ge(gact_ready, n + 1)
                for c in range(KF // 2):
                    ins = T.transpose(bank(2)[:, c * P:(c + 1) * P], gact[:, c * P:(c + 1) * P], ident[:, :])
                ins.then_inc(at_done, 1)
                pe.wait_ge(at_ready, n + 1)
                for k in range(KF):
                    if k % (KF // 2) == 0:
                        pe.wait_ge(part_in[s][4 + k // (KF // 2)], 16 * (r + 1))
                    for j in range(2):
                        ins = T.matmul(ps[j * BT:(j + 1) * BT, 3, :], aT[:, k % (KF // 2), k // (KF // 2), :],
                                       wd_w[s][:, k, j * (D // 2):(j + 1) * (D // 2)],
                                       start=(k == 0), stop=(k == KF - 1))
                ins.then_inc(down_done, 1)

            h_block(1)

            def expert(e, s, r):
                lo = pe.value_load(bnd[0:1, bass.ds(e, 1)], min_val=0, max_val=MAXB)
                hi = pe.value_load(bnd[0:1, bass.ds(e + 1, 1)], min_val=1, max_val=MAXB)
                with pe.Fori(lo, hi) as n:
                    expert_block(n, s, r)

            with pe.Fori(0, NE // SLOTS) as r:
                for s in range(SLOTS):
                    expert(SLOTS * r + s, s, r)
            for e in range(NE // SLOTS * SLOTS, NE):
                expert(e, e % SLOTS, NE // SLOTS)

            pe.wait_ge(wgl_ready, KC + KP)

            def turn(t, b, at_least):
                pe.wait_ge(pt_in[b], (t - b) * 8 + 16)
                pe.wait_ge(y2_ready, t + 1)
                if at_least >= 1:
                    pe.wait_ge(ytl_ready, t)
                for k in range(KP):
                    T.transpose(bank(2)[:, k * P:(k + 1) * P], pt[b][:, k * P:(k + 1) * P], ident[:, :])
                for k in range(KC):
                    ins = T.transpose(ps[:, k // 4, (k % 4) * P:(k % 4 + 1) * P], yt[b][:, k * P:(k + 1) * P], ident[:, :])
                ins.then_inc(yt_done, 1)

            def gate(t, b, at_least):
                pe.wait_ge(ytl_ready, t + 1)
                for c in range(2):
                    cols = slice(c * 512, (c + 1) * 512)
                    if at_least >= 1:
                        pe.wait_ge(sig3_ready, 2 * t - 1 + c)
                    for k in range(KC):
                        ins = passes(bank(3 + c), yTh[b][:, k, :], yTl[b][:, k, :], wgh[:, k, cols], wgl[:, k, cols], k == 0, k == KC - 1)
                    ins.then_inc(gate_done, 1)
                if at_least >= 1:
                    pe.wait_ge(z3_ready, t)
                for c in range(2):
                    cols = slice(c * 512, (c + 1) * 512)
                    for k in range(KP):
                        ins = passes(bank(5 + c), pTh[b][:, k, :], pTl[b][:, k, :], wph[:, k, cols], wpl[:, k, cols], k == 0, k == KP - 1)
                ins.then_inc(ple_done, 1)

            def last_tile(t, b, at_least):
                turn(t, b, at_least)
                if at_least >= 1:
                    gate(t - 1, 1 - b, at_least - 1)

            pairs(pe, last_tile)
            gate(TT - 1, 1, TT - 1)


_INS = ['x', 'p', 'w_in', 'w_pool_mix', 'pool_scale', 'w_dw', 'b_dw', 'conv_ln_g', 'conv_ln_b', 'w_out',
        'ln1_g', 'ln1_b', 'w_coarse', 'b_coarse', 'w_fine', 'b_fine', 'w_gate', 'w_up', 'w_down',
        'ln2_g', 'ln2_b', 'w_ple_proj', 'w_ple_gate', 'ln3_g', 'ln3_b']


def kernel(**inputs):
    import numpy as _np
    import concourse.bacc as _bacc
    from concourse import mybir as _mybir
    from concourse.bass_utils import run_bass_kernel_spmd as _run

    nc = _bacc.Bacc("TRN2", target_bir_lowering=False, num_devices=1)
    arrays, args = {}, []
    for name in _INS:
        a = _np.ascontiguousarray(inputs[name])
        arrays[f"in_{name}_dram"] = a
        args.append(nc.dram_tensor(f"in_{name}_dram", a.shape, _mybir.dt.from_np(a.dtype), kind="ExternalInput").ap())
    shape = inputs['x'].shape
    args.append(nc.dram_tensor("out_0_dram", shape, _mybir.dt.float32, kind="ExternalOutput").ap())
    build_block(nc, *args)
    r = _run(nc, [arrays], core_ids=[0])
    return r.results[0]["out_0_dram"]
```

```python
import concourse.bass as bass
from concourse import mybir
from contextlib import ExitStack
from math import lcm

P = 128


def build_block(nc, x, p, w_in, w_pool_mix, pool_scale, w_dw, b_dw, conv_ln_g, conv_ln_b, w_out,
                ln1_g, ln1_b, w_coarse, b_coarse, w_fine, b_fine, w_gate, w_up, w_down,
                ln2_g, ln2_b, w_ple_proj, w_ple_gate, ln3_g, ln3_b, out):
    f32, f32r, i32 = mybir.dt.float32, mybir.dt.float32r, mybir.dt.int32
    ALU, ACT, AX = mybir.AluOpType, mybir.ActivationFunctionType, mybir.AxisListType
    ADD, SUB, MUL = ALU.add, ALU.subtract, ALU.mult

    _, S, D = x.shape
    TT = S // P
    KC = D // P
    HALF = S // 2
    DEPTH = p.shape[0]
    DP = p.shape[3]
    KP = DP // P
    NPG = w_pool_mix.shape[1]
    DPOOL = NPG * P
    DCONV = w_dw.shape[2]
    HEADS = DCONV // P
    TAPS = w_dw.shape[1]
    WINDOWS = [2 << g for g in range(NPG)]
    NG = w_coarse.shape[2]
    NE = w_fine.shape[2]
    EG = NE // NG
    NR = NG + NE
    FE = w_gate.shape[3]
    KF = FE // P
    KH = KC // 2
    BT = 64
    MAXB = 2 * S // BT + NE
    IN_FLIGHT = 3
    RING_SLOTS = 3
    SLOTS = RING_SLOTS + 1
    ROUND = lcm(NG, SLOTS)
    NG_TURN = ROUND // NG
    ALPHA = float((2 * DEPTH) ** 0.25)
    EPS = 1e-5
    BIG = 8192.0
    NPRM = TAPS + 4
    PAD = TAPS - 1
    OTHER_TAPS = 7
    DVE_TAPS = TAPS - OTHER_TAPS
    WPAD = 16

    ctx = ExitStack()
    with ctx:
        def wd_row(s, k):
            if s < RING_SLOTS:
                return wd_w[s][:, k, :]
            return wd_a[:, k, :] if k < KF - 1 else wd_b[:, :]

        def got(s, m, n):
            return (32 if (s, m) == (RING_SLOTS, 5) else 16) * n

        RING = 16512
        GU = KC * 2 * FE * 4
        WD = KF * D * 4
        SLOT = GU + WD
        FIX = RING + RING_SLOTS * SLOT

        def at(name, shape, dt, offset):
            return nc.alloc_sbuf_tensor_at(name, shape, dt, offset=offset)

        gu_w = [at(f"gu_w{s}", [P, KC, 2, FE], f32, RING + s * SLOT) for s in range(RING_SLOTS)]
        wd_w = [at(f"wd_w{s}", [P, KF, D], f32, RING + s * SLOT + GU) for s in range(RING_SLOTS)]

        gu_w.append(at(f"gu_w{RING_SLOTS}", [P, KC, 2, FE], f32, FIX))

        top = [FIX]

        def fix(name, shape, dt=f32):
            size = 4
            for n in shape[1:]:
                size *= n
            a = at(name, shape, dt, top[0])
            top[0] += (size + 31) // 32 * 32
            return a

        xh = fix("xh", [P, TT, D])
        ident = fix("ident", [P, P])
        CONSTS = top[0]
        meanw = fix("meanw", [P, P])
        prm = fix("prm", [P, HEADS, NPRM])
        within = at("within", [P, NE, TT], f32, CONSTS)
        if top[0] - CONSTS < NE * TT * 4:
            raise ValueError("no room for within")
        ones = fix("ones", [P, P])
        behind = fix("behind", [P, P])
        wr = fix("wr", [P, KC, NR])
        rbias = fix("rbias", [P, NR])
        io64 = fix("io64", [P, MAXB])
        iolo = fix("iolo", [P, P])
        if top[0] - CONSTS < D * 4:
            raise ValueError("no room for a row of down")
        tokA = fix("tokA", [P, 2, TT])
        tokB = fix("tokB", [P, 2, TT])
        halfv = fix("halfv", [P, 1])
        thr = fix("thr", [P, S // BT])
        rev4 = fix("rev4", [P, NG])
        rev8 = fix("rev8", [P, EG])
        rcnt = fix("rcnt", [P, WPAD])
        epsv = fix("epsv", [P, 1])
        onev = fix("onev", [P, NE])
        lg = fix("lg", [P, TT, NR])
        wts = fix("wts", [P, 2, TT])
        gtab = fix("gtab", [P, MAXB + 1], i32)
        stab = fix("stab", [P, MAXB], i32)
        bnd = fix("bnd", [P, NE + 1], i32)
        gidx = fix("gidx", [P, 1], i32)
        sidx = fix("sidx", [P, 1], i32)
        sidx_last = fix("sidx_last", [P, 1], i32)
        SCR = top[0]
        SCR_END = 229368

        xTh = at("xTh", [P, KC, S], f32r, RING)
        xTl = at("xTl", [P, KC, S], f32r, RING + SLOT)
        mixT = at("mixT", [P, KC, S], f32, RING + 2 * SLOT)
        P0, P1, P2 = (RING + s * SLOT + GU for s in range(RING_SLOTS))
        wch = [at(f"wch{j}", [P, KC, P], f32r, P0 + j * 4096) for j in range(3)]
        wcl = [at(f"wcl{j}", [P, KC, P], f32r, (P0 + 3 * 4096, P1, P1 + 4096)[j]) for j in range(3)]
        win2 = at("win2", [P, S], f32, P1 + 8192)
        win3 = at("win3", [P, S], f32, P1 + 12288)
        wcs = [at(f"wcs{j}", [P, KC, P], f32, P2 + j * 4096) for j in range(3)]
        prod = [at(f"prod{b}", [P, S], f32, FIX + b * 4096) for b in range(3)]
        acc2 = at("acc2", [P, S], f32, FIX + 3 * 4096)
        yv = at("yv", [P, S], f32, FIX + 4 * 4096)
        sqr = at("sqr", [P, TT, P], f32, FIX + 5 * 4096)
        diag = at("diag", [P, TT, P], f32, FIX + 6 * 4096)
        wmix = at("wmix", [P, NPG, P], f32, P2 + 12288)
        rows = at("rows", [NPRM, DCONV], f32, P2 + 12288 + 2048)
        scr = [SCR]

        def scratch(name, shape, dt=f32):
            size = 4
            for n in shape[1:]:
                size *= n
            a = at(name, shape, dt, scr[0])
            scr[0] += (size + 31) // 32 * 32
            if scr[0] > SCR_END:
                raise ValueError(name)
            return a

        uT = scratch("uT", [P, PAD + S])
        acc0 = scratch("acc0", [P, S])
        acc1 = scratch("acc1", [P, S])
        sig1 = scratch("sig1", [P, S])
        upT = scratch("upT", [P, WPAD + S])
        cur = [scratch(f"cur{b}", [P, NPRM]) for b in range(2)]
        csd = scratch("csd", [P, TT])
        crs = scratch("crs", [P, TT])

        woh = at("woh", [P, KC, D], f32r, RING)
        wol = at("wol", [P, KC, D], f32r, RING + SLOT)
        wor = at("wor", [P, KC, D], f32, RING + SLOT)
        hb = [at(f"hb{b}", [P, D], f32, P2 + b * 4096) for b in range(2)]
        g1 = at("g1", [P, D], f32, P2 + 8192)
        b1 = at("b1", [P, D], f32, P2 + 12288)
        scr[0] = SCR
        mh = [scratch(f"mh{b}", [P, KC, P], f32r) for b in range(2)]
        ml = [scratch(f"ml{b}", [P, KC, P], f32r) for b in range(2)]
        hTt = scratch("hTt", [P, KC, P])
        vt1 = scratch("vt1", [P, D])
        turn1 = scratch("turn1", [P, 1])
        st1 = scratch("st1", [P, 2, 6])
        mv1 = scratch("mv1", [P, 2])
        sd1 = scratch("sd1", [P, 2])

        scr[0] = SCR
        hblk = scratch("hblk", [P, D // 2])
        hTb = scratch("hTb", [P, KC // 2, 2, BT])
        sg = scratch("sg", [P, FE // 2])
        gact = scratch("gact", [P, FE // 2])
        aT = scratch("aT", [P, KF // 2, 2, BT])
        yb = scratch("yb", [P, D // 2])
        yb_last = scratch("yb_last", [P, D // 2])
        RSCR = scr[0]
        if RSCR + (KF - 1) * D * 4 > SCR_END:
            raise ValueError("no room for down")
        wd_a = at("wd_a", [P, KF - 1, D], f32, RSCR)
        wd_b = at("wd_b", [P, D], f32, CONSTS)
        onehot = scratch("onehot", [P, 2, TT, EG, NG])
        gsel = scratch("gsel", [P, TT, NG, EG])
        both = at("both", [P, TT, NE], f32, scr[0] - TT * NE * 4)
        base = scratch("base", [P, TT, NE])
        ohhi = scratch("ohhi", [P, 2 * TT, MAXB])
        ohlo = at("ohlo", [P, 2 * TT, P], f32, P2)
        ohab = at("ohab", [P, 2 * TT, 2, MAXB], f32, P2 + 8192)
        small = [RSCR + 2048 + 1024 + 1024 + 4096]

        def tiny(name, shape, dt=f32):
            size = 4
            for n in shape[1:]:
                size *= n
            a = at(name, shape, dt, small[0])
            small[0] += (size + 31) // 32 * 32
            return a

        cm = tiny("cm", [P, TT])
        cd = tiny("cd", [P, TT, NG])
        ce = tiny("ce", [P, TT, NG])
        cs = tiny("cs", [P, TT])
        ohg = tiny("ohg", [P, TT, NG])
        sel = tiny("sel", [P, TT, EG])
        sel2 = tiny("sel2", [P, TT, EG])
        oh12 = tiny("oh12", [P, 2, TT, EG])
        m2 = tiny("m2", [P, TT])
        ex = tiny("ex", [P, TT])
        upto = tiny("upto", [P, NE, TT])
        nbf = tiny("nbf", [P, NE])
        incl = tiny("incl", [P, NE])
        cmp16 = tiny("cmp16", [P, NE, S // BT])
        posf = tiny("posf", [P, 2 * TT])
        posi = tiny("posi", [P, 2 * TT], i32)
        hif = tiny("hif", [P, 2 * TT])

        wgr = at("wgr", [P, KC, D], f32, RING)
        wpr = at("wpr", [P, KP, D], f32, RING + GU)
        wgl = at("wgl", [P, KC, D], f32r, RING)
        wpl = at("wpl", [P, KP, D], f32r, RING + GU)
        wph = at("wph", [P, KP, D], f32r, RING + GU + KP * D * 4)
        wgh = at("wgh", [P, KC, D], f32r, RING + SLOT)
        yp = [at(f"yp{b}", [P, 2, D], f32, RING + SLOT + GU + b * 8192) for b in range(2)]
        yt = [at(f"yt{b}", [P, D], f32, RING + 2 * SLOT + b * 4096) for b in range(2)]
        yTh = [at(f"yTh{b}", [P, KC, P], f32r, RING + 2 * SLOT + 8192 + b * 4096) for b in range(2)]
        yTl = [at(f"yTl{b}", [P, KC, P], f32r, RING + 2 * SLOT + 16384 + b * 4096) for b in range(2)]
        sg3 = at("sg3", [P, D], f32, RING + 2 * SLOT + 24576)
        z3 = at("z3", [P, D], f32, RING + 2 * SLOT + 28672)
        ob = [at(f"ob{b}", [P, D], f32, RING + 2 * SLOT + 32768 + b * 4096) for b in range(2)]
        g2 = at("g2", [P, D], f32, RING + 2 * SLOT + 40960)
        b2 = at("b2", [P, D], f32, RING + 2 * SLOT + 45056)
        scr[0] = SCR
        g3 = scratch("g3", [P, D])
        b3 = scratch("b3", [P, D])
        pt = [scratch(f"pt{b}", [P, DP]) for b in range(2)]
        pTh = [scratch(f"pTh{b}", [P, KP, P], f32r) for b in range(2)]
        pTl = [scratch(f"pTl{b}", [P, KP, P], f32r) for b in range(2)]
        turn3 = scratch("turn3", [P, 1])
        st2 = scratch("st2", [P, 2, 6])
        mv2 = scratch("mv2", [P, 2])
        st3 = scratch("st3", [P, 2, 6])
        mv3 = scratch("mv3", [P, 2])
        sd3 = scratch("sd3", [P, 2])

        ps = ctx.enter_context(nc.psum_tensor("ps", [P, 8, 512], f32))

        def bank(b, n=1):
            return ps[:, b, :] if n == 1 else ps[:, b:b + n, :].rearrange("q b n -> q (b n)")

        h_dram = nc.dram_tensor("h_dram", [2 * S, D // 2], f32, kind="Internal").ap()
        y_dram = nc.dram_tensor("y_dram", [4 * S, D // 2], f32, kind="Internal").ap()

        def sem(name):
            return ctx.enter_context(nc.semaphore(name))

        x_in = [sem(f"x_in{c}") for c in range(TT // 2)]
        x_again = [sem(f"x_again{c}") for c in range(2)]
        rows_in = sem("rows_in")
        small_in = sem("small_in")
        wc_in = [sem(f"wc_in{j}") for j in range(3)]
        wch_ready = [sem(f"wch_ready{j}") for j in range(3)]
        wcl_ready = [sem(f"wcl_ready{j}") for j in range(3)]
        z_done = [sem(f"z_done{j}") for j in range(3)]
        consts = sem("consts")
        ident_ready = sem("ident_ready")
        pool_own = sem("pool_own")
        dve_own = sem("dve_own")
        xt_done = sem("xt_done")
        xh_ready = sem("xh_ready")
        xl_ready = sem("xl_ready")
        rcnt_ready = sem("rcnt_ready")
        prm_done = sem("prm_done")
        prm_ready = sem("prm_ready")
        sig_ready = sem("sig_ready")
        u_ready = sem("u_ready")
        up_ready = sem("up_ready")
        pooled_ready = sem("pooled_ready")
        mix_done = sem("mix_done")
        mix_ready = sem("mix_ready")
        conv_step = sem("conv_step")
        conv_ready = sem("conv_ready")
        prod_ready = sem("prod_ready")
        prod_used = sem("prod_used")
        mean_done = sem("mean_done")
        dev_ready = sem("dev_ready")
        sq_ready = sem("sq_ready")
        var_done = sem("var_done")
        csd_ready = sem("csd_ready")
        yn_ready = sem("yn_ready")
        conv_out = sem("conv_out")
        wo_in = [sem(f"wo_in{c}") for c in range(KC // 2)]
        woh_ready = sem("woh_ready")
        wol_ready = sem("wol_ready")
        ln1_in = sem("ln1_in")
        mh_ready = sem("mh_ready")
        ml_ready = sem("ml_ready")
        op_done = sem("op_done")
        v1_ready = sem("v1_ready")
        var1_ready = sem("var1_ready")
        sd1_ready = sem("sd1_ready")
        h_ready = sem("h_ready")
        h_stored = [sem(f"h_stored{b}") for b in range(2)]
        h_again = [sem(f"h_again{c}") for c in range(2)]
        w1_ready = sem("w1_ready")
        ht_done = sem("ht_done")
        ht_ready = sem("ht_ready")
        rt_done = sem("rt_done")
        lg_ready = sem("lg_ready")
        crs_ready = sem("crs_ready")
        diag_ready = sem("diag_ready")
        inv_done = sem("inv_done")
        ln1_own = sem("ln1_own")
        ln2_own = sem("ln2_own")
        ln3_own = sem("ln3_own")
        y2_own = sem("y2_own")
        cd_ready = sem("cd_ready")
        ce_ready = sem("ce_ready")
        m2_ready = sem("m2_ready")
        ex_ready = sem("ex_ready")
        oneh_ready = sem("oneh_ready")
        rank_done = sem("rank_done")
        oh_ready = sem("oh_ready")
        tab_done = sem("tab_done")
        tab_ready = sem("tab_ready")
        part_in = [[sem(f"part_in{s}_{m}") for m in range(6)] for s in range(SLOTS)]
        gath = sem("gath")
        gidx_ready = sem("gidx_ready")
        sidx_ready = sem("sidx_ready")
        hbt_done = sem("hbt_done")
        hbt_ready = sem("hbt_ready")
        gu_done = sem("gu_done")
        silu_ready = sem("silu_ready")
        gact_ready = sem("gact_ready")
        at_done = sem("at_done")
        at_ready = sem("at_ready")
        down_done = sem("down_done")
        y_ready = sem("y_ready")
        scat = sem("scat")
        ple_in = sem("ple_in")
        wgh_ready = sem("wgh_ready")
        wgl_ready = sem("wgl_ready")
        wgl_pool_ready = sem("wgl_pool_ready")
        ln2_in = sem("ln2_in")
        ln3_in = sem("ln3_in")
        yp_in = [sem(f"yp_in{b}") for b in range(2)]
        pt_in = [sem(f"pt_in{b}") for b in range(2)]
        v2_ready = sem("v2_ready")
        var2_ready = sem("var2_ready")
        sd2_ready = sem("sd2_ready")
        y2_ready = sem("y2_ready")
        y_kept = sem("y_kept")
        yt_done = sem("yt_done")
        yth_ready = sem("yth_ready")
        ytl_ready = sem("ytl_ready")
        gate_done = sem("gate_done")
        ple_done = sem("ple_done")
        n3_ready = sem("n3_ready")
        m3_ready = sem("m3_ready")
        sig3_ready = sem("sig3_ready")
        z3_ready = sem("z3_ready")
        var3_ready = sem("var3_ready")
        sd3_ready = sem("sd3_ready")
        o_ready = sem("o_ready")
        o_stored = [sem(f"o_stored{b}") for b in range(2)]

        block = ctx.enter_context(nc.Block())

        def passes(dst, ah, al, bh, bl, first, last):
            nc.tensor.matmul(dst, ah, bh, start=first, stop=False)
            nc.tensor.matmul(dst, ah, bl, start=False, stop=False)
            return nc.tensor.matmul(dst, al, bh, start=False, stop=last)

        def pairs(eng, body, lead=1):
            for t in range(2 * lead):
                body(t, t % 2, t)
            with eng.Fori(lead, TT // 2 - 1) as i:
                body(2 * i, 0, 2 * lead)
                body(2 * i + 1, 1, 2 * lead + 1)
            for t in range(TT - 2, TT):
                body(t, t % 2, t)

        def tile_cols(t):
            return bass.ds(t * P, P)

        def ple_parts(k):
            if k < KP:
                return wpr[:, k, :], wph[:, k, :], wpl[:, k, :]
            return wgr[:, k - KP, :], wgh[:, k - KP, :], wgl[:, k - KP, :]

        def chunk_col(j, i):
            return (DPOOL, DPOOL + DCONV, 0)[j] + i * P

        def bc_row(v):
            return v.rearrange("a n -> (a n)").rearrange("(o n) -> o n", o=1).broadcast_to([P, v.shape[1]])

        @block.sync
        def _(sp):
            w_in_v = w_in[0].rearrange("(k q) n -> q k n", q=P)

            def chunk(j, i):
                sp.dma_start(wcs[j][:, :, :], w_in_v[:, :, bass.ds(chunk_col(j, i), P)]).then_inc(wc_in[j], 16)

            x_v = x[0].rearrange("(t q) d -> q t d", q=P)

            def load_x(c, done):
                sp.dma_start(xh[:, 2 * c:2 * c + 2, :], x_v[:, 2 * c:2 * c + 2, :]).then_inc(done, 16)

            load_x(0, x_in[0])
            load_x(1, x_in[1])
            chunk(0, 0)
            chunk(1, 0)
            load_x(2, x_in[2])
            load_x(3, x_in[3])
            chunk(2, 0)
            for i in range(1, HEADS):
                for j in range(3):
                    sp.wait_ge(wcl_ready[j], i)
                    chunk(j, i)
            sp.wait_ge(z_done[2], 2 * HEADS)
            w_out_v = w_out[0].rearrange("(k q) n -> q k n", q=P)
            for c in range(KC // 2):
                sp.dma_start(wor[:, 2 * c:2 * c + 2, :], w_out_v[:, 2 * c:2 * c + 2, :]).then_inc(wo_in[c], 16)
            sp.wait_ge(mix_done, 2 * NPG)
            sp.dma_start(g1[:, :], bc_row(ln1_g)).then_inc(ln1_in, 16)
            sp.dma_start(b1[:, :], bc_row(ln1_b)).then_inc(ln1_in, 16)
            sp.wait_ge(conv_ready, HEADS)
            sp.dma_start(xh[:, 0:TT // 2, :], x_v[:, 0:TT // 2, :]).then_inc(x_again[0], 16)

            wg_v = w_gate[0].rearrange("(g e) (k q) f -> e g q k f", g=NG, q=P)
            wu_v = w_up[0].rearrange("(g e) (k q) f -> e g q k f", g=NG, q=P)
            wd_v = w_down[0].rearrange("(g e) (k q) d -> e g q k d", g=NG, q=P)

            def piece(v, s, m, turn=0):
                e, g = NG_TURN * turn + v // NG, v % NG
                def load(dst, src, ks):
                    sp.dma_start(dst, src[bass.ds(e, 1), g, :, ks, :].rearrange("a q k n -> (a q) k n")).then_inc(part_in[s][m], 16)

                if m < 4:
                    ks = slice(m // 2 * KH, (m // 2 + 1) * KH)
                    load(gu_w[s][:, ks, m % 2, :], (wg_v, wu_v)[m % 2], ks)
                elif s < RING_SLOTS:
                    ks = slice((m - 4) * KF // 2, (m - 3) * KF // 2)
                    load(wd_w[s][:, ks, :], wd_v, ks)
                elif m == 4:
                    load(wd_a[:, 0:KF // 2, :], wd_v, slice(0, KF // 2))
                else:
                    load(wd_a[:, KF // 2:KF - 1, :], wd_v, slice(KF // 2, KF - 1))
                    load(wd_b[:, :].unsqueeze(1), wd_v, slice(KF - 1, KF))

            sp.wait_ge(conv_out, HEADS)
            sp.dma_start(xh[:, TT // 2:TT, :], x_v[:, TT // 2:TT, :]).then_inc(x_again[1], 16)
            for v in range(RING_SLOTS - 1):
                for m in (4, 5):
                    piece(v, v, m)
            h_rows = h_dram.rearrange("(t q c) n -> t q (c n)", q=P, c=2)

            def store_h(t, b, at_least):
                if at_least == TT - 2:
                    sp.wait_ge(v1_ready, TT // 2)
                    for m in range(2):
                        piece(RING_SLOTS, RING_SLOTS, m)
                if at_least == TT - 1:
                    sp.wait_ge(mh_ready, TT)
                    sp.wait_ge(ml_ready, TT)
                    for m in range(4):
                        piece(RING_SLOTS - 1, RING_SLOTS - 1, m)
                    sp.wait_ge(op_done, TT)
                    for m in range(4):
                        piece(0, 0, m)
                sp.wait_ge(h_ready, t + 1)
                sp.dma_start(h_rows[bass.ds(t, 1), :, :].rearrange("a q n -> (a q) n"), hb[b][:, :]).then_inc(h_stored[b], 16)

            pairs(sp, store_h)
            for m in range(4):
                piece(1, 1, m)
            sp.wait_ge(v1_ready, TT)
            for m in range(2, 4):
                piece(RING_SLOTS, RING_SLOTS, m)
            sp.wait_ge(tab_ready, 1)
            sp.wait_ge(hbt_done, 1)
            for s in (RING_SLOTS - 1, RING_SLOTS):
                for m in (4, 5):
                    if s == RING_SLOTS:
                        sp.wait_ge(part_in[s - 1][m], 16)
                    piece(s, s, m)

            def next_expert(v, turn):
                s, r = v % SLOTS, ROUND // SLOTS * turn + v // SLOTS
                sp_end = sp.value_load(bnd[0:1, bass.ds(ROUND * turn + v - (SLOTS - 1), 1)], min_val=1, max_val=MAXB)
                for m in range(6):
                    if m == 0:
                        sp.wait_ge(gu_done, sp_end)
                    if m == 4:
                        sp.wait_ge(down_done, sp_end)
                    if m >= IN_FLIGHT:
                        sp.wait_ge(part_in[s][m - IN_FLIGHT], got(s, m - IN_FLIGHT, r + 1))
                    elif s:
                        sp.wait_ge(part_in[s - 1][m + 6 - IN_FLIGHT], got(s - 1, m + 6 - IN_FLIGHT, r + 1))
                    else:
                        sp.wait_ge(part_in[SLOTS - 1][m + 6 - IN_FLIGHT], got(SLOTS - 1, m + 6 - IN_FLIGHT, r))
                    piece(v, s, m, turn)

            with sp.Fori(0, (NE - SLOTS) // ROUND) as turn:
                for v in range(SLOTS, SLOTS + ROUND):
                    next_expert(v, turn)
            for v in range(SLOTS + (NE - SLOTS) // ROUND * ROUND, NE):
                next_expert(v, 0)

            last0 = (NE - 1) // SLOTS * SLOTS
            sp_end = sp.value_load(bnd[0:1, last0 + 1:last0 + 2], min_val=1, max_val=MAXB - 1)
            sp.wait_ge(down_done, sp_end)
            wpg_v = w_ple_gate[0].rearrange("(k q) n -> q k n", q=P)
            for c in range(KC // 2):
                if c:
                    sp.wait_ge(ple_in, 16 * c)
                sp.dma_start(wgr[:, 2 * c:2 * c + 2, :], wpg_v[:, 2 * c:2 * c + 2, :]).then_inc(ple_in, 16)
            sp.dma_start(wpr[:, :, :], w_ple_proj[0].rearrange("(k q) n -> q k n", q=P)).then_inc(ple_in, 16)
            sp_all = sp.value_load(bnd[0:1, NE:NE + 1], min_val=NE, max_val=MAXB - 1)
            sp.wait_ge(down_done, sp_all)
            for v, dst in ((ln2_g, g2), (ln2_b, b2)):
                sp.dma_start(dst[:, :], bc_row(v)).then_inc(ln2_in, 16)
            h_tiles = h_dram.rearrange("(t q c) n -> q t (c n)", q=P, c=2)
            sp.dma_start(xh[:, 0:2, :], h_tiles[:, 0:2, :]).then_inc(h_again[0], 16)
            y_rows = y_dram.rearrange("(t q c) n -> t q (c n)", q=P, c=4)
            p_rows = p[0].rearrange("a (t q) n -> (a t) q n", q=P)
            out_rows = out.rearrange("a (t q) n -> (a t) q n", q=P)

            def load_tile(t, b):
                sp.dma_start(yp[b][:, :, :].rearrange("q c n -> q (c n)"),
                             y_rows[bass.ds(t, 1), :, :].rearrange("a q n -> (a q) n")).then_inc(yp_in[b], 16)
                sp.dma_start(pt[b][:, :], p_rows[bass.ds(t, 1), :, :].rearrange("a q n -> (a q) n")).then_inc(pt_in[b], 16)

            sp.wait_ge(scat, sp_all * 16)
            load_tile(0, 0)
            load_tile(1, 1)
            sp.dma_start(xh[:, 2:TT, :], h_tiles[:, 2:TT, :]).then_inc(h_again[1], 16)
            sp.wait_ge(gath, sp_all * 16 + 32)
            sp.wait_ge(wgl_ready, 1)
            for v, dst in ((ln3_g, g3), (ln3_b, b3)):
                sp.dma_start(dst[:, :], bc_row(v)).then_inc(ln3_in, 16)

            for t in range(2, 4):
                sp.wait_ge(v2_ready, t - 1)
                sp.wait_ge(yt_done, t - 1)
                load_tile(t, t % 2)
            for t in range(TT):
                if t + 4 < TT:
                    sp.wait_ge(v2_ready, t + 3)
                    sp.wait_ge(yt_done, t + 3)
                    load_tile(t + 4, t % 2)
                sp.wait_ge(o_ready, t + 1)
                sp.dma_start(out_rows[t, :, :], ob[t % 2][:, :]).then_inc(o_stored[t % 2], 16)
            sp.wait_ge(o_stored[0], 16 * TT // 2)
            sp.wait_ge(o_stored[1], 16 * TT // 2)

        @block.gpsimd
        def _(pool):
            n_own = [0]

            def own(ins):
                n_own[0] += 1
                ins.then_inc(pool_own, 1)
                pool.wait_ge(pool_own, n_own[0])

            own(nc.gpsimd.memset(ident[:, :], 0.0))
            nc.gpsimd.affine_select(out=ident[:, :], in_=ident[:, :], compare_op=ALU.not_equal, fill=1.0,
                                    base=0, pattern=[[-1, P]], channel_multiplier=1).then_inc(ident_ready, 1)
            for r, v in ((slice(0, TAPS), w_dw[0]), (slice(TAPS, TAPS + 1), b_dw), (slice(TAPS + 1, TAPS + 2), conv_ln_g),
                         (slice(TAPS + 2, TAPS + 3), conv_ln_b), (slice(TAPS + 3, TAPS + 4), pool_scale)):
                pool.dma_start(rows[r, :], v).then_inc(rows_in, 16)
            pool.dma_start(wmix[:, :, :], w_pool_mix[0].rearrange("g c d -> c g d")).then_inc(small_in, 16)
            pool.dma_start(wr[:, :, 0:NG], w_coarse[0].rearrange("(k q) n -> q k n", q=P)).then_inc(small_in, 16)
            pool.dma_start(wr[:, :, NG:NR], w_fine[0].rearrange("(k q) n -> q k n", q=P)).then_inc(small_in, 16)
            pool.dma_start(rbias[:, 0:NG], bc_row(b_coarse)).then_inc(small_in, 16)
            pool.dma_start(rbias[:, NG:NR], bc_row(b_fine)).then_inc(small_in, 16)

            own(nc.gpsimd.memset(ones[:, :], 1.0))
            own(nc.gpsimd.memset(meanw[:, :], 1.0 / P))
            own(nc.gpsimd.memset(behind[:, :], 0.0))
            own(nc.gpsimd.affine_select(out=behind[:, :], in_=behind[:, :], compare_op=ALU.is_gt, fill=-1.0,
                                        base=0, pattern=[[1, P]], channel_multiplier=-1))
            own(nc.gpsimd.memset(epsv[:, :], EPS))
            own(nc.gpsimd.memset(onev[:, :], 1.0))
            own(nc.gpsimd.memset(upT[:, 0:WPAD], 0.0))
            own(nc.gpsimd.memset(uT[:, 0:PAD], 0.0))

            def ramp(dst, pattern, base_, mult):
                nc.gpsimd.iota(dst, pattern, base=base_, channel_multiplier=mult,
                               allow_small_or_imprecise_dtypes=True)

            ramp(io64[:, :], [[1, MAXB]], 0, 0)
            ramp(iolo[:, :], [[0, 2], [1, BT]], 0, 0)
            ramp(tokA[:, :, :], [[0, 2], [2 * P, TT]], -int(BIG), 2)
            ramp(tokB[:, :, :], [[2, 2], [4 * P, TT]], -int(BIG), 4)
            ramp(thr[:, :], [[BT, S // BT]], 0, 0)
            ramp(rev4[:, :], [[-1, NG]], NG, 0)
            ramp(rev8[:, :], [[-1, EG]], EG, 0)
            ramp(rcnt[:, :], [[1, WPAD]], 1, 0)
            own(nc.gpsimd.memset(halfv[0:BT, :], BIG))
            own(nc.gpsimd.memset(halfv[BT:P, :], BIG + 1.0))
            own(nc.gpsimd.memset(thr[:, 0:1], -1.0))
            nc.gpsimd.memset(cur[0][:, 0:1], 0.0).then_inc(consts, 1)

            def low(j, i):
                pool.wait_ge(wch_ready[j], i + 1)
                nc.gpsimd.tensor_tensor(wcl[j][:, :, :], wcs[j][:, :, :], wch[j][:, :, :].bitcast(f32), SUB)\
                    .then_inc(wcl_ready[j], 1)

            def windows(g):
                pool.wait_ge(up_ready, 2 * (g + 1))
                src, pad = upT, WPAD
                w = 1
                dsts = [win2, win3]
                if g:
                    pool.wait_ge(mix_done, 2 * g)
                cur_sum, cur_pad = upT, WPAD
                n = 0
                while w < WINDOWS[g]:
                    dst = dsts[n % 2]
                    a = cur_sum[:, cur_pad + w:cur_pad + S]
                    b = cur_sum[:, cur_pad:cur_pad + S - w]
                    own(nc.gpsimd.tensor_tensor(dst[:, w:S], a, b, ADD))
                    own(nc.gpsimd.tensor_copy(dst[:, 0:w], cur_sum[:, cur_pad:cur_pad + w]))
                    cur_sum, cur_pad = dst, 0
                    w *= 2
                    n += 1
                pool.wait_ge(rcnt_ready, 1)
                W = WINDOWS[g]
                own(nc.gpsimd.tensor_tensor(cur_sum[:, 0:W], cur_sum[:, 0:W], rcnt[:, 0:W], MUL))
                own(nc.gpsimd.tensor_scalar(cur_sum[:, W:S], cur_sum[:, W:S], 1.0 / W, None, MUL))
                pooled = dsts[n % 2]
                nc.gpsimd.tensor_tensor(pooled[:, :], cur_sum[:, 0:S], upT[:, WPAD:WPAD + S], SUB).then_inc(pooled_ready, 1)

            def other_taps(i, which):
                for a in which:
                    n = i * OTHER_TAPS + a
                    if a == 0:
                        continue
                    pool.wait_ge(prod_ready, n + 1)
                    if a == 1:
                        if i:
                            pool.wait_ge(conv_ready, i)
                        nc.gpsimd.tensor_tensor(acc2[:, :], prod[(n - 1) % 3][:, :], prod[n % 3][:, :], ADD).then_inc(prod_used, 2)
                    else:
                        pool.wait_ge(prod_used, n)
                        nc.gpsimd.tensor_tensor(acc2[:, :], acc2[:, :], prod[n % 3][:, :], ADD).then_inc(prod_used, 1)

            for g in range(NPG):
                if g:
                    other_taps(g, range(0, 3))
                if g + 1 < HEADS:
                    low(0, g + 1)
                    low(1, g + 1)
                other_taps(g, range(3 if g else 0, OTHER_TAPS))
                if g + 1 < HEADS:
                    low(2, g + 1)
                windows(g)

            pool.wait_ge(op_done, TT)
            nc.gpsimd.memset(hblk[:, :], 0.0).then_inc(pool_own, 1)
            n_own[0] += 1
            pool.wait_ge(pool_own, n_own[0])

            bound = pool.alloc_register("bound")
            nil = pool.alloc_register("nil")
            pool.reg_mov(nil, 0)

            def gather(n):
                nc.gpsimd.tensor_copy(gidx[:, :], gtab[:, bass.ds(n, 1)]).then_inc(gidx_ready, 1)
                pool.wait_ge(gidx_ready, n + 1)
                pool.reg_alu(bound, nil, 2 * S - 1, ADD)
                nc.gpsimd.indirect_dma_start(
                    out=hblk[:, :], out_offset=None, in_=h_dram,
                    in_offset=bass.IndirectOffsetOnAxis(ap=gidx[:, 0:1], axis=0),
                    bounds_check=bound, oob_is_err=False).then_inc(gath, 16)

            def scatter(n, first=False, last=False):
                idx, src = (sidx_last, yb_last) if last else (sidx, yb)
                if not (first or last):
                    pool.wait_ge(scat, n * 16)
                nc.gpsimd.tensor_copy(idx[:, :], stab[:, bass.ds(n, 1)]).then_inc(sidx_ready, 1)
                pool.wait_ge(sidx_ready, n_blocks if last else n + 1)
                pool.wait_ge(y_ready, n_blocks if last else n + 1)
                pool.reg_alu(bound, nil, 4 * S - 1, ADD)
                nc.gpsimd.indirect_dma_start(
                    out=y_dram, out_offset=bass.IndirectOffsetOnAxis(ap=idx[:, 0:1], axis=0),
                    in_=src[:, :], in_offset=None,
                    bounds_check=bound, oob_is_err=False).then_inc(scat, 16)

            pool.wait_ge(tab_ready, 1)
            pool.wait_ge(h_stored[0], 16 * TT // 2)
            pool.wait_ge(h_stored[1], 16 * TT // 2)
            gather(0)
            n_blocks = pool.value_load(bnd[0:1, NE:NE + 1], min_val=NE, max_val=MAXB - 1)
            for n in range(1, 4):
                pool.wait_ge(hbt_done, n)
                gather(n)
            scatter(0, first=True)
            with pool.Fori(2, n_blocks) as n:
                pool.wait_ge(hbt_done, n + 2)
                gather(n + 2)
                scatter(n - 1)
            scatter(n_blocks - 1, last=True)
            for k in range(1, KP + KC, 2):
                pool.wait_ge(wgh_ready, k + 1)
                whole, hi, lo = ple_parts(k)
                nc.gpsimd.tensor_tensor(lo, whole, hi.bitcast(f32), SUB).then_inc(wgl_pool_ready, 1)
            pool.wait_ge(scat, n_blocks * 16)
            pool.wait_ge(ln3_in, 32)

            def scale_shift(t, b, _):
                pool.wait_ge(n3_ready, t + 1)
                nc.gpsimd.tensor_tensor(ob[b][:, :], ob[b][:, :], g3[:, :], MUL).then_inc(m3_ready, 1)
                pool.wait_ge(m3_ready, t + 1)
                nc.gpsimd.tensor_tensor(ob[b][:, :], ob[b][:, :], b3[:, :], ADD).then_inc(o_ready, 1)

            pairs(pool, scale_shift)

        @block.scalar
        def _(act):
            CP = ACT.Copy
            def high(j, i):
                act.wait_ge(wc_in[j], 16 * (i + 1))
                nc.scalar.activation(wch[j][:, :, :], wcs[j][:, :, :], CP).then_inc(wch_ready[j], 1)

            for t in range(TT):
                act.wait_ge(xt_done, t + 1)
                nc.scalar.activation(xTh[:, :, t * P:(t + 1) * P],
                                     bank(4 + 2 * (t % 2), 2).rearrange("q (k m) -> q k m", k=KC), CP).then_inc(xh_ready, 1)
                if t == 2:
                    high(0, 0)
                if t == 3:
                    high(1, 0)
            high(2, 0)

            def gate_sigmoid(i):
                for th in range(2):
                    act.wait_ge(z_done[1], 2 * i + th + 1)
                    if i:
                        act.wait_ge(u_ready, 2 * i)
                    nc.scalar.activation(sig1[:, th * HALF:(th + 1) * HALF], bank(2 + th), ACT.Sigmoid).then_inc(sig_ready, 1)

            def pool_input(i, th):
                act.wait_ge(z_done[2], 2 * i + th + 1)
                if i:
                    act.wait_ge(pooled_ready, i)
                nc.scalar.activation(upT[:, WPAD + th * HALF:WPAD + (th + 1) * HALF], bank(4 + th), CP).then_inc(up_ready, 1)

            def pool_output(i, banks=6):
                for th in range(2):
                    act.wait_ge(mix_done, 2 * i + th + 1)
                    nc.scalar.activation(mixT[:, i, th * HALF:(th + 1) * HALF],
                                         bank(banks + th), CP, scale=prm[:, i, NPRM - 1:NPRM]).then_inc(mix_ready, 1)

            def head_square(i):
                act.wait_ge(dev_ready, i + 1)
                nc.scalar.activation(sqr[:, :, :].rearrange("q t m -> q (t m)"), yv[:, :], ACT.Square).then_inc(sq_ready, 1)

            def head_deviation(i):
                act.wait_ge(var_done, i + 1)
                nc.scalar.activation(csd[:, :], bank(6)[:, 0:TT], ACT.Sqrt, bias=epsv[:, :]).then_inc(csd_ready, 1)

            def head_swish(i):
                act.wait_ge(yn_ready, i + 1)
                nc.scalar.activation(mixT[:, i + NPG, :], yv[:, :], ACT.Silu,
                                     scale=cur[i % 2][:, TAPS + 1:TAPS + 2], bias=cur[i % 2][:, TAPS + 2:TAPS + 3]).then_inc(conv_out, 1)

            def products(i, which):
                act.wait_ge(u_ready, 2 * (i + 1))
                for a in which:
                    n = i * OTHER_TAPS + a
                    if n >= 3:
                        act.wait_ge(prod_used, n - 2)
                    j = DVE_TAPS + a
                    nc.scalar.activation(prod[n % 3][:, :], uT[:, j:j + S], CP, scale=prm[:, i, j:j + 1]).then_inc(prod_ready, 1)

            act.wait_ge(consts, 1)
            gate_sigmoid(0)
            high(0, 1)
            high(1, 1)
            products(0, range(0, 3))
            pool_input(0, 0)
            pool_input(0, 1)
            products(0, range(3, OTHER_TAPS))
            high(2, 1)
            for i in range(1, HEADS):
                gate_sigmoid(i)
                pool_output(i - 1)
                products(i, range(0, 3))
                if i < HEADS - 1:
                    high(0, i + 1)
                    high(1, i + 1)
                head_square(i - 1)
                products(i, range(3, 4))
                pool_input(i, 0)
                head_deviation(i - 1)
                products(i, range(4, 5))
                pool_input(i, 1)
                products(i, range(5, OTHER_TAPS))
                if i < HEADS - 1:
                    high(2, i + 1)
                head_swish(i - 1)
            def w_out_high(k):
                act.wait_ge(wo_in[k // 2], 16)
                nc.scalar.activation(woh[:, k, :], wor[:, k, :], CP).then_inc(woh_ready, 1)

            for k in range(KC):
                w_out_high(k)
            head_square(HEADS - 1)
            head_deviation(HEADS - 1)
            pool_output(HEADS - 1, banks=4)
            head_swish(HEADS - 1)

            def split_mix(t, b):
                nc.scalar.activation(mh[b][:, :, :], mixT[:, :, tile_cols(t)], CP).then_inc(mh_ready, 1)

            def evac_ht(t, b):
                act.wait_ge(ht_done, t + 1)
                nc.scalar.activation(hTt[:, :, :], bank(4, 2).rearrange("q (k m) -> q k m", k=KC), CP).then_inc(ht_ready, 1)

            act.wait_ge(conv_out, HEADS)
            act.wait_ge(mix_ready, 2 * NPG)
            split_mix(0, 0)

            def proj_tile(t, b, at_least):
                if at_least < TT - 1:
                    if at_least >= 1:
                        act.wait_ge(op_done, t)
                    split_mix(t + 1, 1 - b)
                if at_least >= 1:
                    evac_ht(t - 1, 1 - b)
                act.wait_ge(var1_ready, t + 1)
                nc.scalar.activation(sd1[:, 0:1], mv1[:, 1:2], ACT.Sqrt, bias=epsv[:, :]).then_inc(sd1_ready, 1)

            pairs(act, proj_tile)
            evac_ht(TT - 1, 1)

            act.wait_ge(cd_ready, 1)
            nc.scalar.activation(ce[:, :, :], cd[:, :, :], ACT.Exp).then_inc(ce_ready, 1)
            act.wait_ge(m2_ready, 1)
            nc.scalar.activation(ex[:, :], m2[:, :], ACT.Exp).then_inc(ex_ready, 1)

            act.wait_ge(tab_ready, 1)
            act_blocks = act.value_load(bnd[0:1, NE:NE + 1], min_val=NE, max_val=MAXB - 1)

            def act_silu(n):
                act.wait_ge(gu_done, n + 1)
                nc.scalar.activation(sg[:, :], bank(0)[:, 0:FE // 2], ACT.Silu).then_inc(silu_ready, 1)

            def act_at(n):
                act.wait_ge(at_done, n + 1)
                nc.scalar.activation(aT[:, :, :, :].rearrange("q c h m -> q (c h m)"), bank(2)[:, 0:FE // 2], CP).then_inc(at_ready, 1)

            def act_y(n, first=False):
                act.wait_ge(down_done, n)
                if not first:
                    act.wait_ge(scat, (n - 1) * 16)
                nc.scalar.activation(yb[:, :], bank(3), CP).then_inc(y_ready, 1)

            act_silu(0)
            act_at(0)
            act_silu(1)
            act_y(1, first=True)
            act_at(1)
            with act.Fori(2, act_blocks) as n:
                act_silu(n)
                act_y(n)
                act_at(n)
            act.wait_ge(down_done, act_blocks)
            nc.scalar.activation(yb_last[:, :], bank(3), CP).then_inc(y_ready, 1)

            act.wait_ge(ple_in, 16 * (KC // 2 + 1))
            act.wait_ge(down_done, act_blocks)
            for k in range(KP):
                nc.scalar.activation(wph[:, k, :], wpr[:, k, :], CP).then_inc(wgh_ready, 1)
            for k in range(KC):
                nc.scalar.activation(wgh[:, k, :], wgr[:, k, :], CP).then_inc(wgh_ready, 1)

            def gate_half(t, c, first=False):
                act.wait_ge(gate_done, 2 * t + c + 1)
                if not first:
                    act.wait_ge(z3_ready, t)
                nc.scalar.activation(sg3[:, c * 512:(c + 1) * 512], bank(3 + c), ACT.Sigmoid).then_inc(sig3_ready, 1)

            def deviation3(t):
                act.wait_ge(var3_ready, t + 1)
                nc.scalar.activation(sd3[:, 0:1], mv3[:, 1:2], ACT.Sqrt, bias=epsv[:, :]).then_inc(sd3_ready, 1)

            def deviation2(t):
                act.wait_ge(var2_ready, t + 1)
                nc.scalar.activation(sd3[:, 1:2], mv2[:, 1:2], ACT.Sqrt, bias=epsv[:, :]).then_inc(sd2_ready, 1)

            def first_output(t, b):
                act.wait_ge(yp_in[b], (t - b) * 8 + 16)
                nc.scalar.activation(yp[b][:, 0, :], yp[b][:, 0, :], CP, scale=wts[:, 0, bass.ds(t, 1)]).then_inc(w1_ready, 1)

            def last_tile(t, b, at_least):
                act.wait_ge(y2_ready, t + 1)
                nc.scalar.activation(xh[:, bass.ds(t, 1), :].rearrange("q a n -> q (a n)"), yt[b][:, :], CP, scale=ALPHA).then_inc(y_kept, 1)
                act.wait_ge(yt_done, t + 1)
                nc.scalar.activation(pTh[b][:, :, :], bank(2)[:, 0:DP].rearrange("q (k m) -> q k m", k=KP), CP)
                nc.scalar.activation(yTh[b][:, :, :], bank(0, 2).rearrange("q (k m) -> q k m", k=KC), CP).then_inc(yth_ready, 1)
                if at_least < TT - 2:
                    first_output(t + 2, b)
                if at_least >= 1:
                    gate_half(t - 1, 0, first=(at_least == 1))
                if at_least < TT - 2:
                    deviation2(t + 2)
                if at_least >= 1:
                    gate_half(t - 1, 1, first=(at_least == 1))
                    deviation3(t - 1)

            for t in range(2):
                first_output(t, t)
                deviation2(t)
            pairs(act, last_tile)
            for c in range(2):
                gate_half(TT - 1, c)
            deviation3(TT - 1)

        @block.vector
        def _(dve):
            V = nc.vector
            n_own = [0]

            def own(ins):
                n_own[0] += 1
                ins.then_inc(dve_own, 1)
                dve.wait_ge(dve_own, n_own[0])

            def low(j):
                dve.wait_ge(wch_ready[j], 1)
                V.tensor_tensor(wcl[j][:, :, :], wcs[j][:, :, :], wch[j][:, :, :].bitcast(f32), SUB).then_inc(wcl_ready[j], 1)

            for t in range(TT):
                dve.wait_ge(xh_ready, t + 1)
                cols = slice(t * P, (t + 1) * P)
                V.tensor_tensor(xTl[:, :, cols], bank(4 + 2 * (t % 2), 2).rearrange("q (k m) -> q k m", k=KC),
                                xTh[:, :, cols].bitcast(f32), SUB).then_inc(xl_ready, 1)
                if t == TT // 2 - 1:
                    low(0)
                    low(1)
            low(2)
            dve.wait_ge(prm_done, 1)
            V.tensor_copy(prm[:, :, :].rearrange("q h n -> q (h n)"), bank(7)[:, 0:HEADS * NPRM]).then_inc(prm_ready, 1)
            dve.wait_ge(prm_ready, 1)
            dve.wait_ge(consts, 1)
            V.reciprocal(rcnt[:, :], rcnt[:, :]).then_inc(rcnt_ready, 1)
            NSTEP = DVE_TAPS + 2

            def deviation(i):
                dve.wait_ge(mean_done, 2 * (i + 1))
                V.tensor_tensor(yv[:, :], yv[:, :], bank(6, 2), SUB).then_inc(dev_ready, 1)

            def inverse(i):
                dve.wait_ge(csd_ready, i + 1)
                V.reciprocal(crs[:, :], csd[:, :]).then_inc(crs_ready, 1)
                dve.wait_ge(crs_ready, i + 1)
                V.tensor_tensor(diag[:, :, :], ident[:, :].unsqueeze(1).broadcast_to([P, TT, P]),
                                crs[:, :].unsqueeze(2).broadcast_to([P, TT, P]), MUL).then_inc(diag_ready, 1)

            def normalise(i):
                dve.wait_ge(inv_done, 2 * (i + 1))
                V.tensor_tensor(yv[:, :], yv[:, :], bank(6, 2), MUL).then_inc(yn_ready, 1)

            def conv_head(i):
                b = i % 2
                c = cur[b]
                if i >= 2:
                    dve.wait_ge(conv_out, i - 1)
                V.tensor_copy(c[:, :], prm[:, i, :]).then_inc(conv_step, 1)
                if i:
                    dve.wait_ge(prod_ready, OTHER_TAPS * i)
                for th in range(2):
                    dve.wait_ge(sig_ready, 2 * i + th + 1)
                    dve.wait_ge(z_done[0], 2 * i + th + 1)
                    cols = slice(th * HALF, (th + 1) * HALF)
                    V.tensor_tensor(uT[:, PAD + th * HALF:PAD + (th + 1) * HALF], bank(th), sig1[:, cols], MUL).then_inc(u_ready, 1)
                dve.wait_ge(u_ready, 2 * (i + 1))
                dve.wait_ge(conv_step, i * NSTEP + 1)
                if i:
                    dve.wait_ge(conv_ready, i)
                V.tensor_scalar(acc0[:, :], uT[:, 0:S], c[:, 0:1], c[:, TAPS:TAPS + 1], MUL, ADD).then_inc(conv_step, 1)
                V.tensor_scalar(acc1[:, :], uT[:, 1:1 + S], c[:, 1:2], None, MUL).then_inc(conv_step, 1)
                for j in range(2, DVE_TAPS):
                    if i and j == NORM_AT[0]:
                        deviation(i - 1)
                    if i and j == NORM_AT[1]:
                        inverse(i - 1)
                    if i and j == NORM_AT[2]:
                        normalise(i - 1)
                    acc = (acc0, acc1)[j % 2]
                    dve.wait_ge(conv_step, i * NSTEP + j)
                    V.scalar_tensor_tensor(acc[:, :], uT[:, j:j + S], c[:, j:j + 1], acc[:, :], MUL, ADD).then_inc(conv_step, 1)
                dve.wait_ge(prod_used, (i + 1) * OTHER_TAPS)
                dve.wait_ge(conv_step, i * NSTEP + DVE_TAPS)
                acc = (acc0, acc1)[DVE_TAPS % 2]
                V.tensor_tensor(acc[:, :], acc[:, :], acc2[:, :], ADD).then_inc(conv_step, 1)
                dve.wait_ge(conv_step, (i + 1) * NSTEP)
                if i:
                    dve.wait_ge(conv_out, i)
                V.tensor_tensor(yv[:, :], acc0[:, :], acc1[:, :], ADD).then_inc(conv_ready, 1)

            NORM_AT = (5, 11, 18)
            for i in range(HEADS):
                conv_head(i)

            def w_out_low(k):
                dve.wait_ge(woh_ready, k + 1)
                V.tensor_tensor(wol[:, k, :], wor[:, k, :], woh[:, k, :].bitcast(f32), SUB).then_inc(wol_ready, 1)

            w_out_low(0)
            w_out_low(1)
            deviation(HEADS - 1)
            for k in range(2, 5):
                w_out_low(k)
            inverse(HEADS - 1)
            w_out_low(5)
            w_out_low(6)
            normalise(HEADS - 1)
            w_out_low(7)

            def split_mix(t, b):
                dve.wait_ge(mh_ready, t + 1)
                V.tensor_tensor(ml[b][:, :, :], mixT[:, :, tile_cols(t)], mh[b][:, :, :].bitcast(f32), SUB).then_inc(ml_ready, 1)

            def logits(t, b):
                dve.wait_ge(rt_done, t + 1)
                V.tensor_tensor(lg[:, bass.ds(t, 1), :].rearrange("q a n -> q (a n)"), bank(6 + b)[:, 0:NR], rbias[:, :], ADD).then_inc(lg_ready, 1)

            dve.wait_ge(ln1_in, 32)
            dve.wait_ge(small_in, 80)
            split_mix(0, 0)
            dve.wait_ge(var_done, HEADS)
            dve.wait_ge(mix_ready, 2 * NPG)
            dve.wait_ge(conv_out, HEADS)
            own(V.memset(within[:, :, :], 1.0))
            own(V.memset(within[:, :, 0:1], 0.0))
            for c in range(2):
                dve.wait_ge(x_again[c], 16)
            LN1 = 5

            def proj_tile(t, b, at_least):
                xt = xh[:, bass.ds(t, 1), :].rearrange("q a n -> q (a n)")
                if at_least >= 1:
                    dve.wait_ge(h_ready, t)
                if at_least < TT - 1:
                    if at_least >= 1:
                        dve.wait_ge(op_done, t)
                    split_mix(t + 1, 1 - b)
                dve.wait_ge(op_done, t + 1)
                V.scalar_tensor_tensor(vt1[:, :], xt, ALPHA, bank(2 * b, 2), MUL, ADD).then_inc(v1_ready, 1)
                dve.wait_ge(v1_ready, t + 1)
                n = t * LN1
                for c in range(2):
                    V.bn_stats(st1[:, c, :], vt1[:, c * 512:(c + 1) * 512]).then_inc(ln1_own, 1)
                dve.wait_ge(ln1_own, n + 2)
                V.memset(turn1[:, :], 0.0)
                V.bn_aggr(mv1[:, :], st1[:, :, :].rearrange("q c s -> q (c s)")).then_inc(var1_ready, 1)
                dve.wait_ge(sd1_ready, t + 1)
                V.reciprocal(sd1[:, 1:2], sd1[:, 0:1]).then_inc(ln1_own, 1)
                dve.wait_ge(ln1_own, n + 3)
                dve.wait_ge(var1_ready, t + 1)
                V.tensor_scalar(vt1[:, :], vt1[:, :], mv1[:, 0:1], sd1[:, 1:2], SUB, MUL).then_inc(ln1_own, 1)
                dve.wait_ge(ln1_own, n + 4)
                V.tensor_tensor(vt1[:, :], vt1[:, :], g1[:, :], MUL).then_inc(ln1_own, 1)
                dve.wait_ge(ln1_own, n + 5)
                if at_least >= 2:
                    dve.wait_ge(h_stored[b], (t - b) * 8)
                    dve.wait_ge(ht_done, t - 1)
                V.tensor_tensor(hb[b][:, :], vt1[:, :], b1[:, :], ADD).then_inc(h_ready, 1)
                if at_least >= 2:
                    logits(t - 2, b)

            pairs(dve, proj_tile)
            logits(TT - 2, 0)
            logits(TT - 1, 1)

            dve.wait_ge(lg_ready, TT)
            coarse = lg[:, :, 0:NG]
            fine = lg[:, :, NG:NR].rearrange("q t (g e) -> q t g e", g=NG)

            def over(a, *shape):
                return a.broadcast_to([P, *shape])

            own(V.tensor_reduce(cm[:, :], coarse, op=ALU.max, axis=AX.X))
            V.tensor_tensor(cd[:, :, :], coarse, over(cm[:, :].unsqueeze(2), TT, NG), SUB).then_inc(cd_ready, 1)
            dve.wait_ge(cd_ready, 1)
            own(V.scalar_tensor_tensor(ohg[:, :, :], cd[:, :, :], 0.0, over(rev4[:, :].unsqueeze(1), TT, NG), ALU.is_ge, MUL))
            own(V.tensor_reduce(cm[:, :], ohg[:, :, :], op=ALU.max, axis=AX.X))
            own(V.tensor_tensor(ohg[:, :, :], over(rev4[:, :].unsqueeze(1), TT, NG), over(cm[:, :].unsqueeze(2), TT, NG), ALU.is_equal))
            own(V.tensor_tensor(gsel[:, :, :, :], fine, over(ohg[:, :, :].unsqueeze(3), TT, NG, EG), MUL))
            own(V.tensor_reduce(sel[:, :, :], gsel[:, :, :, :].rearrange("q t g e -> q t e g"), op=ADD, axis=AX.X))
            own(V.tensor_reduce(cm[:, :], sel[:, :, :], op=ALU.max, axis=AX.X))
            own(V.tensor_tensor(sel[:, :, :], sel[:, :, :], over(cm[:, :].unsqueeze(2), TT, EG), SUB))

            def first_max(src, dst):
                own(V.scalar_tensor_tensor(dst, src, 0.0, over(rev8[:, :].unsqueeze(1), TT, EG), ALU.is_ge, MUL))
                own(V.tensor_reduce(cm[:, :], dst, op=ALU.max, axis=AX.X))
                own(V.tensor_tensor(dst, over(rev8[:, :].unsqueeze(1), TT, EG), over(cm[:, :].unsqueeze(2), TT, EG), ALU.is_equal))

            first_max(sel[:, :, :], oh12[:, 0, :, :])
            own(V.scalar_tensor_tensor(sel2[:, :, :], oh12[:, 0, :, :], -1e30, sel[:, :, :], MUL, ADD))
            V.tensor_reduce(m2[:, :], sel2[:, :, :], op=ALU.max, axis=AX.X).then_inc(m2_ready, 1)
            dve.wait_ge(m2_ready, 1)
            own(V.tensor_tensor(sel2[:, :, :], sel2[:, :, :], over(m2[:, :].unsqueeze(2), TT, EG), SUB))
            first_max(sel2[:, :, :], oh12[:, 1, :, :])
            for k in range(2):
                own(V.tensor_tensor(onehot[:, k, :, :, :], over(ohg[:, :, :].unsqueeze(2), TT, EG, NG),
                                    over(oh12[:, k, :, :].unsqueeze(3), TT, EG, NG), MUL))
            V.tensor_tensor(both[:, :, :], onehot[:, 0, :, :, :].rearrange("q t e g -> q t (e g)"),
                            onehot[:, 1, :, :, :].rearrange("q t e g -> q t (e g)"), ADD).then_inc(oneh_ready, 1)
            dve.wait_ge(ce_ready, 1)
            own(V.tensor_reduce(cs[:, :], ce[:, :, :], op=ADD, axis=AX.X))
            dve.wait_ge(ex_ready, 1)
            own(V.scalar_tensor_tensor(cs[:, :], ex[:, :], 1.0, cs[:, :], ADD, MUL))
            own(V.reciprocal(wts[:, 0, :], cs[:, :]))
            own(V.tensor_tensor(wts[:, 1, :], wts[:, 0, :], ex[:, :], MUL))
            dve.wait_ge(rank_done, 1)
            tot = bank(1)[:, 0:TT * NE]
            rank = bank(0)[:, 0:TT * NE].rearrange("q (t e) -> q t e", t=TT)
            own(V.tensor_tensor_scan(upto[:, :, :].rearrange("q e t -> q (e t)"), within[:, :, :].rearrange("q e t -> q (e t)"), tot, 0.0, MUL, ADD))
            own(V.tensor_tensor(cmp16[:, :, :], over(upto[:, :, TT - 1:TT], NE, S // BT),
                                over(thr[:, :].unsqueeze(1), NE, S // BT), ALU.is_gt))
            own(V.tensor_reduce(nbf[:, :], cmp16[:, :, :], op=ADD, axis=AX.X))
            own(V.tensor_tensor_scan(incl[:, :], onev[:, :], nbf[:, :], 0.0, MUL, ADD))
            own(V.tensor_tensor(nbf[:, :], incl[:, :], nbf[:, :], SUB))
            own(V.scalar_tensor_tensor(upto[:, :, :], over(nbf[:, :].unsqueeze(2), NE, TT), float(BT), upto[:, :, :], MUL, ADD))
            own(V.tensor_tensor(base[:, :, :], rank, upto[:, :, :].rearrange("q e t -> q t e"), ADD))
            flat = onehot[:, :, :, :, :].rearrange("q k t e g -> q k (t e g)")
            own(V.tensor_tensor(flat, flat, over(base[:, :, :].rearrange("q t e -> q (t e)").unsqueeze(1), 2, TT * NE), MUL))
            own(V.tensor_reduce(posf[:, :], onehot[:, :, :, :, :].rearrange("q k t e g -> q (k t) (e g)"), op=ADD, axis=AX.X))
            own(V.tensor_copy(posi[:, :], posf[:, :]))
            own(V.tensor_scalar(posi[:, :], posi[:, :], 6, None, ALU.arith_shift_right))
            own(V.tensor_copy(hif[:, :], posi[:, :]))
            own(V.scalar_tensor_tensor(posf[:, :], hif[:, :], -float(BT), posf[:, :], MUL, ADD))
            for b in range(2):
                dve.wait_ge(h_stored[b], 16 * TT // 2)
            for k in range(2):
                c = slice(k * TT, (k + 1) * TT)
                V.tensor_tensor(ohlo[:, c, :], over(iolo[:, :].unsqueeze(1), TT, P), over(posf[:, c].unsqueeze(2), TT, P), ALU.is_equal)
                own(V.tensor_tensor(ohhi[:, c, :], over(io64[:, :].unsqueeze(1), TT, MAXB), over(hif[:, c].unsqueeze(2), TT, MAXB), ALU.is_equal))
                V.tensor_tensor(ohab[:, c, 0, :], ohhi[:, c, :], over(tokA[:, k, :].unsqueeze(2), TT, MAXB), MUL)
                V.tensor_tensor(ohab[:, c, 1, :], ohhi[:, c, :], over(tokB[:, k, :].unsqueeze(2), TT, MAXB), MUL).then_inc(oh_ready, 1)
            own(V.tensor_copy(bnd[:, 1:NE + 1], incl[:, :]))
            own(V.memset(bnd[:, 0:1], 0))
            own(V.memset(gtab[:, MAXB:MAXB + 1], int(BIG)))
            dve.wait_ge(tab_done, 1)
            own(V.tensor_scalar(gtab[:, 0:MAXB], bank(0)[:, 0:MAXB], halfv[:, :], None, ADD))
            V.tensor_scalar(stab[:, :], bank(0)[:, MAXB:2 * MAXB], halfv[:, :], None, ADD).then_inc(tab_ready, 1)
            dve.wait_ge(tab_ready, 1)

            dve_blocks = dve.value_load(bnd[0:1, NE:NE + 1], min_val=NE, max_val=MAXB - 1)

            def h_block(n):
                dve.wait_ge(hbt_done, n)
                V.tensor_copy(hTb[:, :, :, :].rearrange("q c h m -> q (c h m)"), bank(1)).then_inc(hbt_ready, 1)

            h_block(1)
            with dve.Fori(0, dve_blocks) as n:
                dve.wait_ge(silu_ready, n + 1)
                V.tensor_tensor(gact[:, :], sg[:, :], bank(0)[:, FE // 2:FE], MUL).then_inc(gact_ready, 1)
                h_block(n + 2)

            for k in range(0, KP + KC, 2):
                dve.wait_ge(wgh_ready, k + 1)
                whole, hi, lo = ple_parts(k)
                V.tensor_tensor(lo, whole, hi.bitcast(f32), SUB).then_inc(wgl_ready, 1)
            dve.wait_ge(ln2_in, 32)

            def finish_tile(t, b, at_least):
                n = t * 4
                dve.wait_ge(sig3_ready, 2 * (t + 1))
                dve.wait_ge(ple_done, t + 1)
                if at_least >= 1:
                    dve.wait_ge(n3_ready, t)
                V.tensor_tensor(z3[:, :], sg3[:, :], bank(5, 2), MUL).then_inc(ln3_own, 1)
                dve.wait_ge(ln3_own, n + 1)
                dve.wait_ge(y_kept, t + 1)
                V.tensor_tensor(z3[:, :], xh[:, bass.ds(t, 1), :].rearrange("q a n -> q (a n)"), z3[:, :], ADD).then_inc(z3_ready, 1)
                dve.wait_ge(z3_ready, t + 1)
                for c in range(2):
                    V.bn_stats(st3[:, c, :], z3[:, c * 512:(c + 1) * 512]).then_inc(ln3_own, 1)
                dve.wait_ge(ln3_own, n + 3)
                V.memset(turn3[:, :], 0.0)
                V.bn_aggr(mv3[:, :], st3[:, :, :].rearrange("q c s -> q (c s)")).then_inc(var3_ready, 1)
                dve.wait_ge(sd3_ready, t + 1)
                dve.wait_ge(var3_ready, t + 1)
                V.reciprocal(sd3[:, 0:1], sd3[:, 0:1]).then_inc(ln3_own, 1)
                dve.wait_ge(ln3_own, n + 4)
                if at_least >= 2:
                    dve.wait_ge(o_stored[b], (t - b) * 8)
                V.tensor_scalar(ob[b][:, :], z3[:, :], mv3[:, 0:1], sd3[:, 0:1], SUB, MUL).then_inc(n3_ready, 1)

            def norm_tile(t, b, at_least):
                n = t * 5
                xt = xh[:, bass.ds(t, 1), :].rearrange("q a n -> q (a n)")
                dve.wait_ge(yp_in[b], (t - b) * 8 + 16)
                if at_least >= 2:
                    dve.wait_ge(y_kept, t - 1)
                    dve.wait_ge(yt_done, t - 1)
                dve.wait_ge(w1_ready, t + 1)
                dve.wait_ge(h_again[0] if at_least < 2 else h_again[1], 16)
                V.scalar_tensor_tensor(xt, xt, ALPHA, yp[b][:, 0, :], MUL, ADD).then_inc(ln2_own, 1)
                dve.wait_ge(ln2_own, n + 1)
                V.scalar_tensor_tensor(yt[b][:, :], yp[b][:, 1, :], wts[:, 1, bass.ds(t, 1)], xt, MUL, ADD).then_inc(v2_ready, 1)
                dve.wait_ge(v2_ready, t + 1)
                for c in range(2):
                    V.bn_stats(st2[:, c, :], yt[b][:, c * 512:(c + 1) * 512]).then_inc(ln2_own, 1)
                dve.wait_ge(ln2_own, n + 3)
                V.memset(turn3[:, :], 0.0)
                V.bn_aggr(mv2[:, :], st2[:, :, :].rearrange("q c s -> q (c s)")).then_inc(var2_ready, 1)
                dve.wait_ge(sd2_ready, t + 1)
                dve.wait_ge(var2_ready, t + 1)
                V.reciprocal(sd3[:, 1:2], sd3[:, 1:2]).then_inc(ln2_own, 1)
                dve.wait_ge(ln2_own, n + 4)
                V.tensor_scalar(yt[b][:, :], yt[b][:, :], mv2[:, 0:1], sd3[:, 1:2], SUB, MUL).then_inc(ln2_own, 1)
                dve.wait_ge(ln2_own, n + 5)
                V.tensor_tensor(yt[b][:, :], yt[b][:, :], g2[:, :], MUL).then_inc(y2_own, 1)
                dve.wait_ge(y2_own, t + 1)
                V.tensor_tensor(yt[b][:, :], yt[b][:, :], b2[:, :], ADD).then_inc(y2_ready, 1)

            norm_tile(0, 0, 0)
            norm_tile(1, 1, 1)

            def last_tile(t, b, at_least):
                dve.wait_ge(yth_ready, t + 1)
                V.tensor_tensor(pTl[b][:, :, :], bank(2)[:, 0:DP].rearrange("q (k m) -> q k m", k=KP),
                                pTh[b][:, :, :].bitcast(f32), SUB)
                V.tensor_tensor(yTl[b][:, :, :], bank(0, 2).rearrange("q (k m) -> q k m", k=KC),
                                yTh[b][:, :, :].bitcast(f32), SUB).then_inc(ytl_ready, 1)
                if at_least < TT - 2:
                    norm_tile(t + 2, b, at_least + 2)
                if at_least >= 1:
                    finish_tile(t - 1, 1 - b, at_least - 1)

            pairs(dve, last_tile, lead=2)
            finish_tile(TT - 1, 1, TT - 1)

        @block.tensor
        def _(pe):
            T = nc.tensor
            pe.wait_ge(ident_ready, 1)

            def keep_warm(n, b):
                for _ in range(n):
                    T.matmul(bank(b), ident[:, :], ident[:, :].unsqueeze(1).broadcast_to([P, 4, P]), start=True, stop=True)

            def x_tile(t):
                if t % 2 == 0:
                    pe.wait_ge(x_in[t // 2], 16)
                if t >= 2:
                    pe.wait_ge(xl_ready, t - 1)
                for k in range(KC):
                    ins = T.transpose(ps[:, 4 + 2 * (t % 2) + k // 4, (k % 4) * P:(k % 4 + 1) * P], xh[:, t, k * P:(k + 1) * P], ident[:, :])
                ins.then_inc(xt_done, 1)

            def z_chunk(j, i, first=False, halves=(0, 1)):
                pe.wait_ge(wcl_ready[j], i + 1)
                if not first:
                    if j < 2:
                        pe.wait_ge(u_ready, 2 * i)
                    else:
                        pe.wait_ge(up_ready, 2 * i)
                for th in halves:
                    cols = slice(th * HALF, (th + 1) * HALF)
                    for k in range(KC):
                        ins = passes(bank(2 * j + th), wch[j][:, k, :], wcl[j][:, k, :], xTh[:, k, cols], xTl[:, k, cols], k == 0, k == KC - 1)
                    ins.then_inc(z_done[j], 1)

            def pool_mix(g, banks=6):
                pooled = (win2, win3)[(g + 1) % 2]
                pe.wait_ge(pooled_ready, g + 1)
                if banks == 4:
                    pe.wait_ge(up_ready, 2 * NPG)
                elif g:
                    pe.wait_ge(yn_ready, g)
                for th in range(2):
                    T.matmul(bank(banks + th), wmix[:, g, :], pooled[:, th * HALF:(th + 1) * HALF], start=True, stop=True).then_inc(mix_done, 1)

            def head_mean(i):
                if i < HEADS - 1:
                    pe.wait_ge(mix_ready, 2 * (i + 1))
                else:
                    pe.wait_ge(yn_ready, i)
                pe.wait_ge(conv_ready, i + 1)
                for th in range(2):
                    T.matmul(bank(6 + th), meanw[:, :], yv[:, th * HALF:(th + 1) * HALF], start=True, stop=True).then_inc(mean_done, 1)

            def head_variance(i):
                pe.wait_ge(sq_ready, i + 1)
                for t in range(TT):
                    ins = T.matmul(bank(6)[:, t:t + 1], sqr[:, t, :], meanw[:, 0:1], start=True, stop=True)
                ins.then_inc(var_done, 1)

            def head_inverse(i):
                pe.wait_ge(diag_ready, i + 1)
                for th in range(2):
                    T.matmul(bank(6 + th), ones[:, :], diag[:, th * TT // 2:(th + 1) * TT // 2, :].rearrange("q t m -> q (t m)"),
                             start=True, stop=True).then_inc(inv_done, 1)

            keep_warm(2, 3)
            for t in range(TT // 2):
                x_tile(t)
            keep_warm(2, 3)
            pe.wait_ge(xl_ready, TT // 2)
            z_chunk(0, 0, first=True, halves=(0,))
            z_chunk(1, 0, first=True, halves=(0,))
            for t in range(TT // 2, TT):
                x_tile(t)
            pe.wait_ge(xl_ready, TT)
            z_chunk(0, 0, first=True, halves=(1,))
            z_chunk(1, 0, first=True, halves=(1,))
            pe.wait_ge(rows_in, 80)
            for h in range(HEADS):
                ins = T.transpose(bank(7)[:, h * NPRM:(h + 1) * NPRM], rows[:, h * P:(h + 1) * P], ident[0:NPRM, 0:NPRM])
            ins.then_inc(prm_done, 1)
            z_chunk(2, 0, first=True)
            pe.wait_ge(small_in, 80)
            pe.wait_ge(consts, 1)
            pe.wait_ge(prm_ready, 1)
            for i in range(1, HEADS):
                z_chunk(0, i)
                z_chunk(1, i)
                pool_mix(i - 1)
                head_mean(i - 1)
                z_chunk(2, i, halves=(0,))
                head_variance(i - 1)
                z_chunk(2, i, halves=(1,))
                head_inverse(i - 1)
            pe.wait_ge(u_ready, 2 * HEADS)
            keep_warm(17, 2)
            head_mean(HEADS - 1)
            keep_warm(2, 2)
            head_variance(HEADS - 1)
            pool_mix(HEADS - 1, banks=4)
            head_inverse(HEADS - 1)
            keep_warm(5, 2)

            pe.wait_ge(small_in, 80)

            def route(t, b):
                pe.wait_ge(h_ready, t + 1)
                for k in range(KC):
                    ins = T.transpose(ps[:, 4 + k // 4, (k % 4) * P:(k % 4 + 1) * P], hb[b][:, k * P:(k + 1) * P], ident[:, :])
                ins.then_inc(ht_done, 1)

            def route_mm(t, b):
                pe.wait_ge(ht_ready, t + 1)
                for k in range(KC):
                    ins = T.matmul(bank(6 + b)[:, 0:NR], hTt[:, k, :], wr[:, k, :], start=(k == 0), stop=(k == KC - 1))
                ins.then_inc(rt_done, 1)

            def proj_tile(t, b, at_least):
                pe.wait_ge(ml_ready, t + 1)
                if at_least >= 2:
                    pe.wait_ge(v1_ready, t - 1)
                for c in range(2):
                    if c and at_least >= 2:
                        route_mm(t - 2, b)
                    for k in range(KC):
                        if at_least == 0 and c == 0:
                            pe.wait_ge(wol_ready, k + 1)
                        ins = passes(bank(2 * b + c), mh[b][:, k, :], ml[b][:, k, :], woh[:, k, c * 512:(c + 1) * 512],
                                     wol[:, k, c * 512:(c + 1) * 512], k == 0, k == KC - 1)
                ins.then_inc(op_done, 1)
                if at_least >= 1:
                    route(t - 1, 1 - b)

            pairs(pe, proj_tile)
            pe.wait_ge(lg_ready, TT - 3)
            route_mm(TT - 2, 0)
            route(TT - 1, 1)
            pe.wait_ge(lg_ready, TT - 2)
            route_mm(TT - 1, 1)

            keep_warm(6, 5)
            pe.wait_ge(oneh_ready, 1)
            M = both[:, :, :].rearrange("q t e -> q (t e)")
            T.matmul(bank(0)[:, 0:TT * NE], behind[:, :], M, start=True, stop=True)
            T.matmul(bank(1)[:, 0:TT * NE], ones[:, :], both[:, :, :].rearrange("q t e -> q e t"), start=True, stop=True).then_inc(rank_done, 1)
            keep_warm(9, 5)
            for a in range(2 * TT):
                if a % TT == 0:
                    pe.wait_ge(oh_ready, a // TT + 1)
                ins = T.matmul(bank(0)[:, 0:2 * MAXB], ohlo[:, a, :], ohab[:, a, :, :].rearrange("q c n -> q (c n)"),
                               start=(a == 0), stop=(a == 2 * TT - 1))
            ins.then_inc(tab_done, 1)
            keep_warm(4, 5)
            pe.wait_ge(tab_ready, 1)

            def h_block(n):
                pe.wait_ge(gath, 16 * n)
                for c in range(KC // 2):
                    ins = T.transpose(bank(1)[:, c * P:(c + 1) * P], hblk[:, c * P:(c + 1) * P], ident[:, :])
                ins.then_inc(hbt_done, 1)

            def gate_up(n, s, r):
                pe.wait_ge(hbt_ready, n + 1)
                for k in range(KC):
                    if k % KH == 0:
                        for m in range(2):
                            pe.wait_ge(part_in[s][m + 2 * (k // KH)], 16 * (r + 1))
                    for j in range(2):
                        ins = T.matmul(ps[j * BT:(j + 1) * BT, 0, :].rearrange("q (c n) -> q c n", c=2),
                                       hTb[:, k % KH, k // KH, :], gu_w[s][:, k, :, j * (FE // 2):(j + 1) * (FE // 2)],
                                       start=(k == 0), stop=(k == KC - 1))
                ins.then_inc(gu_done, 1)
                h_block(n + 2)

            def turn_product(n):
                pe.wait_ge(gact_ready, n + 1)
                for c in range(KF // 2):
                    ins = T.transpose(bank(2)[:, c * P:(c + 1) * P], gact[:, c * P:(c + 1) * P], ident[:, :])
                ins.then_inc(at_done, 1)

            def down(n, s, r):
                pe.wait_ge(at_ready, n)
                for k in range(KF):
                    if k % (KF // 2) == 0:
                        pe.wait_ge(part_in[s][4 + k // (KF // 2)], got(s, 4 + k // (KF // 2), r + 1))
                    for j in range(2):
                        ins = T.matmul(ps[j * BT:(j + 1) * BT, 3, :], aT[:, k % (KF // 2), k // (KF // 2), :],
                                       wd_row(s, k)[:, j * (D // 2):(j + 1) * (D // 2)],
                                       start=(k == 0), stop=(k == KF - 1))
                ins.then_inc(down_done, 1)

            def expert(v, s, r, s_before=None, r_before=None):
                lo = 0 if s_before is None else pe.value_load(bnd[0:1, bass.ds(v, 1)], min_val=0, max_val=MAXB)
                hi = pe.value_load(bnd[0:1, bass.ds(v + 1, 1)], min_val=1, max_val=MAXB)
                if s_before is None:
                    h_block(1)
                gate_up(lo, s, r)
                if s_before is not None:
                    down(lo, s_before, r_before)
                turn_product(lo)
                more = lo + 1
                with pe.If(hi > more):
                    with pe.Fori(more, hi) as n:
                        gate_up(n, s, r)
                        down(n, s, r)
                        turn_product(n)
                return hi

            expert(0, 0, 0)
            with pe.Fori(0, (NE - 1) // SLOTS) as r:
                for s in range(1, SLOTS):
                    expert(SLOTS * r + s, s, r, s - 1, r)
                expert(SLOTS * r + SLOTS, 0, r + 1, SLOTS - 1, r)
            for v in range((NE - 1) // SLOTS * SLOTS + 1, NE):
                pe_blocks = expert(v, v % SLOTS, v // SLOTS, (v - 1) % SLOTS, (v - 1) // SLOTS)
            down(pe_blocks, (NE - 1) % SLOTS, (NE - 1) // SLOTS)

            keep_warm(24, 5)
            pe.wait_ge(wgl_ready, (KC + KP) // 2)
            pe.wait_ge(wgl_pool_ready, (KC + KP) // 2)

            def turn(t, b, at_least):
                pe.wait_ge(pt_in[b], (t - b) * 8 + 16)
                pe.wait_ge(y2_ready, t + 1)
                if at_least >= 1:
                    pe.wait_ge(ytl_ready, t)
                for k in range(KP):
                    T.transpose(bank(2)[:, k * P:(k + 1) * P], pt[b][:, k * P:(k + 1) * P], ident[:, :])
                for k in range(KC):
                    ins = T.transpose(ps[:, k // 4, (k % 4) * P:(k % 4 + 1) * P], yt[b][:, k * P:(k + 1) * P], ident[:, :])
                ins.then_inc(yt_done, 1)

            def gate(t, b, at_least):
                pe.wait_ge(ytl_ready, t + 1)
                for c in range(2):
                    cols = slice(c * 512, (c + 1) * 512)
                    if at_least >= 1:
                        pe.wait_ge(sig3_ready, 2 * t - 1 + c)
                    for k in range(KC):
                        ins = passes(bank(3 + c), yTh[b][:, k, :], yTl[b][:, k, :], wgh[:, k, cols], wgl[:, k, cols], k == 0, k == KC - 1)
                    ins.then_inc(gate_done, 1)
                if at_least >= 1:
                    pe.wait_ge(z3_ready, t)
                for c in range(2):
                    cols = slice(c * 512, (c + 1) * 512)
                    for k in range(KP):
                        ins = passes(bank(5 + c), pTh[b][:, k, :], pTl[b][:, k, :], wph[:, k, cols], wpl[:, k, cols], k == 0, k == KP - 1)
                ins.then_inc(ple_done, 1)

            def last_tile(t, b, at_least):
                turn(t, b, at_least)
                if at_least >= 1:
                    gate(t - 1, 1 - b, at_least - 1)

            pairs(pe, last_tile)
            gate(TT - 1, 1, TT - 1)


_INS = ['x', 'p', 'w_in', 'w_pool_mix', 'pool_scale', 'w_dw', 'b_dw', 'conv_ln_g', 'conv_ln_b', 'w_out',
        'ln1_g', 'ln1_b', 'w_coarse', 'b_coarse', 'w_fine', 'b_fine', 'w_gate', 'w_up', 'w_down',
        'ln2_g', 'ln2_b', 'w_ple_proj', 'w_ple_gate', 'ln3_g', 'ln3_b']


def kernel(**inputs):
    import numpy as _np
    import concourse.bacc as _bacc
    from concourse import mybir as _mybir
    from concourse.bass_utils import run_bass_kernel_spmd as _run

    nc = _bacc.Bacc("TRN2", target_bir_lowering=False, num_devices=1)
    arrays, args = {}, []
    for name in _INS:
        a = _np.ascontiguousarray(inputs[name])
        arrays[f"in_{name}_dram"] = a
        args.append(nc.dram_tensor(f"in_{name}_dram", a.shape, _mybir.dt.from_np(a.dtype), kind="ExternalInput").ap())
    shape = inputs['x'].shape
    args.append(nc.dram_tensor("out_0_dram", shape, _mybir.dt.float32, kind="ExternalOutput").ap())
    build_block(nc, *args)
    r = _run(nc, [arrays], core_ids=[0])
    return r.results[0]["out_0_dram"]
```
